# Optimizing a Trainium2 kernel written in Bass

```python
import jax
import jax.numpy as jnp
from jax import lax
import numpy as np

D_MODEL = 1024
BATCH = 1
SEQ = 1024
DEPTH = 2

HEAD_DIM = 64
N_GROUPS = 4
MIX_W = N_GROUPS * HEAD_DIM
N_BRANCH = 4
CONV_W = 3
Q_LORA = 256
KV_LORA = 128
QK_NOPE = 64
QK_ROPE = 32
QK_HEAD = QK_NOPE + QK_ROPE
V_HEAD = 64
Q_BLOCK = 128
SG_CHUNK = 128
RET_CHUNK = 128
D_FF = 2816
N_EXPERTS = 8
TOP_K = 2
D_FF_EXPERT = 3584
N_DENSE = (DEPTH + 1) // 2
N_MOE = DEPTH // 2
ROPE_THETA = 10000.0
EPS = 1e-6
IN_SIZES = (MIX_W, MIX_W, MIX_W, Q_LORA, KV_LORA, QK_ROPE, MIX_W, MIX_W, MIX_W, MIX_W, MIX_W, MIX_W, N_BRANCH * D_MODEL)
D_IN = 9 * MIX_W + Q_LORA + KV_LORA + QK_ROPE + N_BRANCH * D_MODEL

kernel_name = 'hybrid_gated_mixers_moe_trunk'

def rms_norm(x, g):
    xf = x.astype(jnp.float32)
    y = xf * lax.rsqrt(jnp.mean(xf * xf, axis=-1, keepdims=True) + EPS)
    return (y * g.astype(jnp.float32)).astype(x.dtype)

def head_layer_norm(x, g):
    xf = x.astype(jnp.float32)
    xc = xf - jnp.mean(xf, axis=-1, keepdims=True)
    var = jnp.mean(xc * xc, axis=-1, keepdims=True)
    return (xc * lax.rsqrt(var + EPS) * g.astype(jnp.float32)).astype(x.dtype)

def rotary(x, positions):
    half = x.shape[-1] // 2
    inv_freq = ROPE_THETA ** (-jnp.arange(half, dtype=jnp.float32) / half)
    ang = positions.astype(jnp.float32)[:, :, None] * inv_freq
    cos = jnp.cos(ang)[:, :, None, :]
    sin = jnp.sin(ang)[:, :, None, :]
    xf = x.astype(jnp.float32)
    x1, x2 = xf[..., :half], xf[..., half:]
    return jnp.concatenate([x1 * cos - x2 * sin, x2 * cos + x1 * sin], axis=-1).astype(x.dtype)

def modulate(h, shift, scale):
    return h * (1.0 + scale) + shift

def short_conv_mixer(b_gate, c_gate, z, conv_w):
    u = c_gate * z
    y = lax.conv_general_dilated(u, conv_w[:, None, :].astype(u.dtype), window_strides=(1,),
                                 padding=[(CONV_W - 1, 0)], dimension_numbers=('NWC', 'WIO', 'NWC'),
                                 feature_group_count=MIX_W)
    return b_gate * y

def blocked_causal_attention(q, k, v):
    B, S, H, Dq = q.shape
    nb = S // Q_BLOCK
    qb = q.reshape(B, nb, Q_BLOCK, H, Dq).transpose(1, 0, 2, 3, 4)
    k_idx = jnp.arange(S)
    scale = Dq ** -0.5

    def one_block(args):
        q_blk, i = args
        s = jnp.einsum('bqhd,bkhd->bhqk', q_blk, k).astype(jnp.float32) * scale
        q_idx = i * Q_BLOCK + jnp.arange(Q_BLOCK)
        s = jnp.where(k_idx[None, :] <= q_idx[:, None], s, -jnp.inf)
        p = jax.nn.softmax(s, axis=-1).astype(v.dtype)
        return jnp.einsum('bhqk,bkhd->bqhd', p, v)

    out = lax.map(one_block, (qb, jnp.arange(nb)))
    return out.transpose(1, 0, 2, 3, 4).reshape(B, S, H, v.shape[-1])

def mla_mixer(c_q, c_kv, k_rope, positions, cq_g, w_uq, ckv_g, w_ukv, qn_g, kn_g):
    B, S, _ = c_q.shape
    q = (rms_norm(c_q, cq_g) @ w_uq).reshape(B, S, N_GROUPS, QK_HEAD)
    kv = (rms_norm(c_kv, ckv_g) @ w_ukv).reshape(B, S, N_GROUPS, QK_NOPE + V_HEAD)
    k_nope, v = kv[..., :QK_NOPE], kv[..., QK_NOPE:]
    k_pe = jnp.broadcast_to(k_rope[:, :, None, :], (B, S, N_GROUPS, QK_ROPE))
    k = jnp.concatenate([k_nope, k_pe], axis=-1)
    q = rms_norm(q, qn_g)
    k = rms_norm(k, kn_g)
    q = jnp.concatenate([q[..., :QK_NOPE], rotary(q[..., QK_NOPE:], positions)], axis=-1)
    k = jnp.concatenate([k[..., :QK_NOPE], rotary(k[..., QK_NOPE:], positions)], axis=-1)
    return blocked_causal_attention(q, k, v).reshape(B, S, N_GROUPS * V_HEAD)

def spatial_gating_mixer(u, v, gv_g, w_s, b_s):
    B, S, _ = u.shape
    nc = S // SG_CHUNK
    u = jax.nn.gelu(u).reshape(B, nc, SG_CHUNK, N_GROUPS, HEAD_DIM)
    v = rms_norm(jax.nn.gelu(v).reshape(B, S, N_GROUPS, HEAD_DIM), gv_g)
    v = v.reshape(B, nc, SG_CHUNK, N_GROUPS, HEAD_DIM)
    ws = jnp.tril(w_s)
    mixed = jnp.einsum('gts,bnsgc->bntgc', ws, v) + b_s.T[:, :, None]
    return (u * mixed).reshape(B, S, MIX_W)

def retention_mixer(q, k, v, g, positions, ret_g):
    B, S, _ = q.shape
    H, dk, C = N_GROUPS, HEAD_DIM, RET_CHUNK
    nc = S // C
    f32 = jnp.float32
    q = rotary(q.reshape(B, S, H, dk), positions).astype(f32)
    k = rotary(k.reshape(B, S, H, dk), positions).astype(f32) * dk ** -0.5
    v = v.reshape(B, S, H, dk).astype(f32)
    log_gamma = jnp.log1p(-(2.0 ** (-5.0 - jnp.arange(H, dtype=f32))))
    qc = q.reshape(B, nc, C, H, dk)
    kc = k.reshape(B, nc, C, H, dk)
    vc = v.reshape(B, nc, C, H, dk)
    pos = jnp.arange(C, dtype=f32)
    rel = pos[:, None] - pos[None, :]
    decay = jnp.where(rel >= 0, jnp.exp(log_gamma[:, None, None] * jnp.maximum(rel, 0.0)), 0.0)
    scores = jnp.einsum('bnihd,bnjhd->bnhij', qc, kc) * decay
    o_inner = jnp.einsum('bnhij,bnjhd->bnihd', scores, vc)
    k_decay = jnp.exp(log_gamma[None, :] * (C - 1.0 - pos)[:, None])
    kv_chunk = jnp.einsum('bnjhd,bnjhe->bnhde', kc * k_decay[:, :, None], vc)
    chunk_decay = jnp.exp(log_gamma * C)[None, :, None, None]

    def step(state, kv_n):
        return state * chunk_decay + kv_n, state

    init = jnp.zeros((B, H, dk, dk), f32)
    _, prev = lax.scan(step, init, kv_chunk.transpose(1, 0, 2, 3, 4))
    prev = prev.transpose(1, 0, 2, 3, 4)
    q_decay = jnp.exp(log_gamma[None, :] * (pos + 1.0)[:, None])
    o_cross = jnp.einsum('bnihd,bnhde->bnihe', qc * q_decay[:, :, None], prev)
    o = head_layer_norm((o_inner + o_cross).reshape(B, S, H, dk), ret_g).reshape(B, S, MIX_W)
    return (jax.nn.silu(g.astype(f32)) * o).astype(g.dtype)

def mixer_sublayer(h, positions, w_in, conv_w, cq_g, w_uq, ckv_g, w_ukv, qn_g, kn_g,
                   gv_g, w_s, b_s, ret_g, w_branch, w_o):
    B, S, _ = h.shape
    points = np.cumsum(IN_SIZES)[:-1].tolist()
    (a_b, a_c, a_x, m_cq, m_ckv, m_kr, s_u, s_v, r_q, r_k, r_v, r_g, gate_logits) = jnp.split(h @ w_in, points, axis=-1)
    ys = (
        short_conv_mixer(a_b, a_c, a_x, conv_w),
        mla_mixer(m_cq, m_ckv, m_kr, positions, cq_g, w_uq, ckv_g, w_ukv, qn_g, kn_g),
        spatial_gating_mixer(s_u, s_v, gv_g, w_s, b_s),
        retention_mixer(r_q, r_k, r_v, r_g, positions, ret_g),
    )
    merged = jnp.zeros((B, S, D_MODEL), h.dtype)
    for n in range(N_BRANCH):
        gate = jax.nn.sigmoid(gate_logits[..., n * D_MODEL:(n + 1) * D_MODEL])
        merged = merged + gate * (ys[n] @ w_branch[n])
    return merged @ w_o

def swiglu(h, w1, w3, w2):
    return (jax.nn.silu(h @ w1) * (h @ w3)) @ w2

def moe_swiglu(h, router_w, router_b, w1, w3, w2):
    B, S, D = h.shape
    t = h.reshape(B * S, D)
    n_tok = t.shape[0]
    probs = jax.nn.softmax((t @ router_w + router_b).astype(jnp.float32), axis=-1)
    top_p, top_i = lax.top_k(probs, TOP_K)
    top_p = top_p / jnp.sum(top_p, axis=-1, keepdims=True)
    flat_e = top_i.reshape(-1)
    order = jnp.argsort(flat_e)
    tok = order // TOP_K
    sizes = jnp.bincount(flat_e, length=N_EXPERTS).astype(jnp.int32)
    xs = t[tok]
    hid = jax.nn.silu(lax.ragged_dot(xs, w1, sizes)) * lax.ragged_dot(xs, w3, sizes)
    y = lax.ragged_dot(hid, w2, sizes) * top_p.reshape(-1)[order][:, None].astype(h.dtype)
    out = jnp.zeros((n_tok, D), h.dtype).at[tok].add(y)
    return out.reshape(B, S, D)

def setup_inputs(seed: int = 0) -> dict:
    key = jax.random.key(seed)
    ks = jax.random.split(key, 32)
    f32 = jnp.float32
    L = DEPTH

    def nrm(k, shape, scale):
        return jax.random.normal(k, shape, f32) * scale

    def gain(k, shape):
        return 1.0 + 0.02 * jax.random.normal(k, shape, f32)

    start = jax.random.randint(ks[2], (BATCH, 1), 0, 4096, dtype=jnp.int32)
    return {
        'x': nrm(ks[0], (BATCH, SEQ, D_MODEL), 1.0),
        'c': nrm(ks[1], (BATCH, D_MODEL), 1.0),
        'positions': start + jnp.arange(SEQ, dtype=jnp.int32)[None, :],
        'norm1_g': gain(ks[3], (L, D_MODEL)),
        'norm2_g': gain(ks[4], (L, D_MODEL)),
        'ada_w': nrm(ks[5], (L, D_MODEL, 6 * D_MODEL), D_MODEL ** -0.5),
        'ada_b': nrm(ks[6], (L, 6 * D_MODEL), 0.02),
        'w_in': nrm(ks[7], (L, D_MODEL, D_IN), D_MODEL ** -0.5),
        'conv_w': nrm(ks[8], (L, CONV_W, MIX_W), CONV_W ** -0.5),
        'cq_g': gain(ks[9], (L, Q_LORA)),
        'w_uq': nrm(ks[10], (L, Q_LORA, N_GROUPS * QK_HEAD), Q_LORA ** -0.5),
        'ckv_g': gain(ks[11], (L, KV_LORA)),
        'w_ukv': nrm(ks[12], (L, KV_LORA, N_GROUPS * (QK_NOPE + V_HEAD)), KV_LORA ** -0.5),
        'qn_g': gain(ks[13], (L, QK_HEAD)),
        'kn_g': gain(ks[14], (L, QK_HEAD)),
        'gv_g': gain(ks[15], (L, N_GROUPS, HEAD_DIM)),
        'w_s': nrm(ks[16], (L, N_GROUPS, SG_CHUNK, SG_CHUNK), SG_CHUNK ** -0.5),
        'b_s': gain(ks[17], (L, N_GROUPS, SG_CHUNK)),
        'ret_g': gain(ks[18], (L, N_GROUPS, HEAD_DIM)),
        'w_branch': nrm(ks[19], (L, N_BRANCH, MIX_W, D_MODEL), MIX_W ** -0.5),
        'w_o': nrm(ks[20], (L, D_MODEL, D_MODEL), D_MODEL ** -0.5),
        'ffn_w1': nrm(ks[21], (N_DENSE, D_MODEL, D_FF), D_MODEL ** -0.5),
        'ffn_w3': nrm(ks[22], (N_DENSE, D_MODEL, D_FF), D_MODEL ** -0.5),
        'ffn_w2': nrm(ks[23], (N_DENSE, D_FF, D_MODEL), D_FF ** -0.5),
        'router_w': nrm(ks[24], (N_MOE, D_MODEL, N_EXPERTS), D_MODEL ** -0.5),
        'router_b': nrm(ks[25], (N_MOE, N_EXPERTS), 0.01),
        'moe_w1': nrm(ks[26], (N_MOE, N_EXPERTS, D_MODEL, D_FF_EXPERT), D_MODEL ** -0.5),
        'moe_w3': nrm(ks[27], (N_MOE, N_EXPERTS, D_MODEL, D_FF_EXPERT), D_MODEL ** -0.5),
        'moe_w2': nrm(ks[28], (N_MOE, N_EXPERTS, D_FF_EXPERT, D_MODEL), D_FF_EXPERT ** -0.5),
    }

def reference(x, c, positions, norm1_g, norm2_g, ada_w, ada_b, w_in, conv_w, cq_g, w_uq, ckv_g, w_ukv,
              qn_g, kn_g, gv_g, w_s, b_s, ret_g, w_branch, w_o, ffn_w1, ffn_w3, ffn_w2,
              router_w, router_b, moe_w1, moe_w3, moe_w2):
    cond = jax.nn.silu(c)
    for l in range(DEPTH):
        ada = (cond @ ada_w[l] + ada_b[l])[:, None, :]
        sh1, sc1, g1, sh2, sc2, g2 = jnp.split(ada, 6, axis=-1)
        h = modulate(rms_norm(x, norm1_g[l]), sh1, sc1)
        x = x + g1 * mixer_sublayer(h, positions, w_in[l], conv_w[l], cq_g[l], w_uq[l], ckv_g[l], w_ukv[l],
                                    qn_g[l], kn_g[l], gv_g[l], w_s[l], b_s[l], ret_g[l], w_branch[l], w_o[l])
        h = modulate(rms_norm(x, norm2_g[l]), sh2, sc2)
        if l % 2 == 0:
            f = swiglu(h, ffn_w1[l // 2], ffn_w3[l // 2], ffn_w2[l // 2])
        else:
            f = moe_swiglu(h, router_w[l // 2], router_b[l // 2], moe_w1[l // 2], moe_w3[l // 2], moe_w2[l // 2])
        x = x + g2 * f
    return x


_drawn_inputs = setup_inputs


def setup_inputs(seed=0):
    import zlib

    import numpy as np

    out = dict(_drawn_inputs(seed))
    spreads = {}
    factors = {'cq_g': 8.0,
     'ckv_g': 5.972,
     'qn_g': 8.0,
     'kn_g': 8.0,
     'gv_g': 5.293,
     'b_s': 3.254,
     'ret_g': 4.373,
     'router_b': 12.711}
    for name, (base, spread) in spreads.items():
        noise = np.random.default_rng([zlib.crc32(name.encode()), seed]).standard_normal(out[name].shape)
        drawn = base * np.exp(spread * noise) if base else spread * noise
        out[name] = jnp.asarray(drawn.astype(out[name].dtype))
    for name, factor in factors.items():
        out[name] = (out[name] * factor).astype(out[name].dtype)
    return out
```

```python
from collections import namedtuple
from contextlib import ExitStack, contextmanager

import numpy as np
import concourse.bass as bass
from concourse import mybir

F32 = mybir.dt.float32
F32R = mybir.dt.float32r
I32 = mybir.dt.int32
U32 = mybir.dt.uint32
ACT = mybir.ActivationFunctionType
ALU = mybir.AluOpType
AX = mybir.AxisListType
ds = bass.ds

P = 128
D = 1024
S = 1024
DEPTH = 2
KT = D // P
HALF = 512
NHALF = S // HALF
ST = S // P
HD = 64
NG = 4
MIX = NG * HD
NBR = 4
QL = 256
QKN = 64
QKR = 32
QK = QKN + QKR
FF = 2816
FT = FF // P
NE = 8
FE = 3584
EPS = 1e-6
BIG = 1e30
TWO_PI = 2.0 * np.pi

C_B, C_C, C_X, C_CQ, C_CKV, C_KR = 0, 256, 512, 768, 1024, 1152
C_SU, C_SV, C_RQ, C_RK, C_RV, C_RG, C_GATE = 1184, 1440, 1696, 1952, 2208, 2464, 2720

(K_ID, K_ONE, K_BLK, K_PRET, K_PMLA, K_NEG, K_TRI, K_LOW) = [P * i for i in range(8)]
K_DEC = 8 * P
K_KDEC = K_DEC + NG * P
K_QDEC = K_KDEC + MIX
K_CD = K_QDEC + 2 * P
K_FRET = K_CD + 2
K_FMLA = K_FRET + 1
K_ITEM = K_FMLA + 1
K_EXP = K_ITEM + 1
K_N = K_EXP + NE


def constants():
    f = np.float32
    c = np.zeros((P, K_N), f)
    i = np.arange(P)
    c[:, K_ID:K_ID + P] = np.eye(P)
    c[:, K_ONE:K_ONE + P] = 1.0
    c[:, K_BLK:K_BLK + P] = i[:, None] // HD == i[None, :] // HD

    def swap(first, half, col):
        for j in range(half):
            c[first + half + j, col + first + j] = -1.0
            c[first + j, col + first + half + j] = 1.0

    swap(0, HD // 2, K_PRET)
    swap(HD, HD // 2, K_PRET)
    swap(QKN, QKR // 2, K_PMLA)
    c[:, K_NEG:K_NEG + P] = np.where(i[None, :] > i[:, None], -BIG, 0.0)
    c[:, K_TRI:K_TRI + P] = i[:, None] <= i[None, :]
    c[:, K_LOW:K_LOW + P] = i[:, None] < i[None, :]
    lg = np.log1p(-(2.0 ** (-5.0 - np.arange(NG)))).astype(f).astype(np.float64)
    for h in range(NG):
        rel = i[None, :] - i[:, None]
        slot = 2 * (h % 2) + h // 2
        c[:, K_DEC + P * slot:K_DEC + P * slot + P] = np.where(rel >= 0, np.exp(lg[h] * np.maximum(rel, 0)), 0) * HD ** -0.5
        c[:, K_KDEC + HD * h:K_KDEC + HD * h + HD] = (np.exp(lg[h] * (P - 1 - i)) * HD ** -0.5)[:, None]
        rows = slice(HD * (h % 2), HD * (h % 2) + HD)
        c[rows, K_QDEC + P * (h // 2):K_QDEC + P * (h // 2) + P] = np.exp(lg[h] * (i + 1.0))[None, :]
        c[rows, K_CD + h // 2] = np.exp(lg[h] * P)

    def freq(half):
        return (f(10000.0) ** (-np.arange(half, dtype=f) / f(half))).astype(f)

    c[:, K_FRET] = np.tile(freq(HD // 2), P // (HD // 2))
    c[:, K_FMLA] = np.tile(freq(QKR // 2), P // (QKR // 2))
    c[:, K_ITEM] = i
    c[:, K_EXP:K_EXP + NE] = np.arange(NE)
    return c


SEM0 = 104
SW_DMA = ("scattered", "ga0", "ga1", "gb0", "gb1")
SEM_SW = 160


@contextmanager
def phase(nc, *names):
    with ExitStack() as stack:
        sems = {n: stack.enter_context(nc.semaphore(n, num=SEM_SW + SW_DMA.index(n) if n in SW_DMA else SEM0 + i))
                for i, n in enumerate(names)}
        with nc.Block() as block:
            yield block, namedtuple("Semaphores", names)(**sems)
        nc.all_engine_barrier(sems_to_clear=range(SEM0, SEM0 + len(names)))


def looped(eng, n, body):
    if n > 1:
        with eng.Fori(0, n - 1) as i:
            body(i, False)
    body(n - 1, True)


def two_pi_parts():
    rest, parts = TWO_PI, []
    for bits in (8, 8, 8):
        e = int(np.floor(np.log2(rest)))
        q = 2.0 ** (e - bits + 1)
        v = float(np.floor(rest / q) * q)
        parts.append(v)
        rest -= v
    return parts + [float(np.float32(rest))]


class Memory:

    def __init__(self, nc, stack):
        self.nc = nc
        self.base = (nc.sbuf_base + 63) // 64 * 64
        self.end = nc.sbuf_usable_end
        self.at = {}
        ps = stack.enter_context(nc.psum_tensor("banks", [P, 8, HALF], F32))
        self.ps = ps
        KB = 1024
        o = 0
        self.const = self.place("const", [P, K_N], F32, o)
        o += 9 * KB
        self.small = self.place("small", [P, S_END], F32, o)
        o += KB + KB // 2
        R = o
        self.R = R
        self.h_hi = self.place("h_hi", [P, KT, S], F32R, R)
        self.h_lo = self.place("h_lo", [P, KT, S], F32R, R + 32 * KB)
        self.h_f = self.place("h_f", [P, KT, S], F32, R)
        self.w_raw = [self.place(f"w_raw{b}", [P, KT, P], F32, R + (64 + 4 * b) * KB) for b in range(2)]
        self.w_hi = [self.place(f"w_hi{b}", [P, KT, P], F32R, R + (72 + 4 * b) * KB) for b in range(2)]
        self.w_lo = [self.place(f"w_lo{b}", [P, KT, P], F32R, R + (80 + 4 * b) * KB) for b in range(2)]
        self.W0 = R + 64 * KB
        self.table = self.place("rope_tables", [P, 4, S], F32, R + 88 * KB)
        self.ys = self.place("ys", [P, 2 * NBR, S], F32, R + 104 * KB)
        self.x = self.place("x_res", [P, KT, S], F32, R + 104 * KB)
        LP = R + 136 * KB
        self.w_uq = self.place("w_uq_sb", [P, QL // P, NG * QK], F32, LP)
        self.w_ukv = self.place("w_ukv_sb", [P, NG * (QKN + HD)], F32, LP + 3 * KB)
        self.bs = self.place("bs_sb", [P, 2, P], F32, LP + 5 * KB)
        self.ws_t = self.place("ws_t", [P, NG, P], F32, LP + 6 * KB)
        self.Z0 = R + 146 * KB
        self.z = self.place("z", [P, 12, 2, HALF], F32, self.Z0)
        self.top = R + 194 * KB

    def place(self, name, shape, dt, offset):
        return self.nc.alloc_sbuf_tensor_at(name, shape, dt, offset=self.base + offset)


S_ADA = 0
S_A = S_ADA + DEPTH * 6 * KT
S_COND = S_A + DEPTH * 2 * KT
S_VEC = S_COND + KT
(V_BIAS, V_NORM, V_CW, V_CQ, V_CKV, V_QN, V_KN, V_GV, V_RET, V_N) = (0, 48, 64, 70, 72, 73, 74, 75, 77, 79)
S_END = S_VEC + DEPTH * V_N


def pack_vectors(inp):
    def cols(v):
        return v.reshape(-1, P).T

    def padded(v):
        return np.concatenate([v, np.zeros(P - len(v), v.dtype)])[:, None]

    parts = [cols(inp["c"])]
    for l in range(DEPTH):
        parts += [cols(inp["ada_b"][l]), cols(inp["norm1_g"][l]), cols(inp["norm2_g"][l]), cols(inp["conv_w"][l]),
                  cols(inp["cq_g"][l]), cols(inp["ckv_g"][l]), padded(inp["qn_g"][l]), padded(inp["kn_g"][l]),
                  cols(inp["gv_g"][l]), cols(inp["ret_g"][l])]
    return np.ascontiguousarray(np.concatenate(parts, axis=1))



def credit_pool(pool, s):
    pool.sem_inc(s.lo_ready, 2)


def credit_pe(pe, s):
    pe.sem_inc(s.mm_done, 2)


def w_load(sp, s, m, j, b, src, kt=KT):
    sp.wait_ge(s.lo_ready, j + 1)
    sp.dma_start(m.w_raw[b][:, 0:kt, :], src).then_inc((s.raw0, s.raw1)[b], 16)


def w_round(act, s, m, j, r, b, kt=KT):
    act.wait_ge((s.raw0, s.raw1)[b], 16 * r + 16)
    act.wait_ge(s.mm_done, j + 1)
    act.activation(m.w_hi[b][:, 0:kt, :], m.w_raw[b][:, 0:kt, :], ACT.Copy).then_inc(s.hi_ready, 1)


def w_rest(pool, s, m, j, b, kt=KT):
    pool.wait_ge(s.hi_ready, j + 1)
    pool.tensor_tensor(m.w_lo[b][:, 0:kt, :], m.w_raw[b][:, 0:kt, :], m.w_hi[b][:, 0:kt, :].bitcast(F32),
                       ALU.subtract).then_inc(s.lo_ready, 1)


def mm3(pe, out, wh, wl, rh, rl, first, last):
    pe.matmul(out, wh, rh, start=first, stop=False)
    pe.matmul(out, wh, rl, start=False, stop=False)
    return pe.matmul(out, wl, rh, start=False, stop=last)


def h_block(pe, m, b, bank):
    for half in range(NHALF):
        tok = slice(half * HALF, (half + 1) * HALF)
        for k in range(KT):
            last = mm3(pe, m.ps[:, bank + half, :], m.w_hi[b][:, k, :], m.w_lo[b][:, k, :],
                       m.h_hi[:, k, tok], m.h_lo[:, k, tok], k == 0, k == KT - 1)
    return last


def w_view(w2d, col, n=P):
    return w2d.rearrange("(k p) n -> p k n", p=P)[:, :, ds(col, n)]


def setup_phases(nc, m, a):
    cst = m.const
    xrow = m.place("x_rows", [P, ST, D], F32, m.R)
    xt = m.place("x_turned", [P, 2, 2, HALF], F32, m.R + 32 * 1024)
    with phase(nc, "c_in", "x_in", "turned", "copied", "stored0", "stored1") as (block, s):
        @block.sync
        def _(sp):
            sp.dma_start(cst[:, :], a.const).then_inc(s.c_in, 16)
            sp.dma_start(m.small[:, S_COND:S_END], a.vectors).then_inc(s.c_in, 16)
            sp.dma_start(xrow[:, :, :], a.x.rearrange("o (t p) d -> p (o t) d", p=P)).then_inc(s.x_in, 16)
            for k in range(KT):
                sp.wait_ge(s.copied, k + 1)
                sp.dma_start(a.xs[P * k:P * (k + 1), :], xt[:, k % 2]).then_inc((s.stored0, s.stored1)[k % 2], 16)
            sp.wait_ge(s.stored0, 16 * KT // 2)
            sp.wait_ge(s.stored1, 16 * KT // 2)

        @block.tensor
        def _(pe):
            pe.wait_ge(s.c_in, 32)
            pe.wait_ge(s.x_in, 16)
            for k in range(KT):
                if k >= 2:
                    pe.wait_ge(s.copied, k - 1)
                for t in range(ST):
                    last = pe.transpose(m.ps[:, 2 * (k % 2) + t // 4, P * (t % 4):P * (t % 4 + 1)],
                                        xrow[:, t, P * k:P * (k + 1)], cst[:, K_ID:K_ID + P])
                last.then_inc(s.turned, 1)

        @block.vector
        def _(dve):
            for k in range(KT):
                dve.wait_ge(s.turned, k + 1)
                if k >= 2:
                    dve.wait_ge((s.stored0, s.stored1)[k % 2], 16 * (k // 2))
                dve.tensor_copy(xt[:, k % 2], m.ps[:, 2 * (k % 2):2 * (k % 2) + 2, :]).then_inc(s.copied, 1)

    pos_i = m.place("pos_i", [P, S], I32, m.R)
    pos_f, ang, cnt, red, wrap = (m.place(n, [P, S], F32, m.R + 1024 * 4 * (i + 1))
                                  for i, n in enumerate(("pos_f", "ang", "cnt", "red", "wrap")))
    parts = two_pi_parts()
    edge = 3.1415925
    with phase(nc, "p_in", "step", "reduced", "used", "silu") as (block, s):
        @block.sync
        def _(sp):
            sp.dma_start(pos_i[:, :], a.positions.rearrange("o s -> (o s)").partition_broadcast(P)).then_inc(s.p_in, 16)

        @block.vector
        def _(dve):
            n = 0

            def chain(ins):
                nonlocal n
                n += 1
                ins.then_inc(s.step, 1)
                dve.wait_ge(s.step, n)

            dve.wait_ge(s.p_in, 16)
            chain(dve.tensor_copy(pos_f[:, :], pos_i[:, :]))
            for t, col in enumerate((K_FRET, K_FMLA)):
                if t:
                    dve.wait_ge(s.used, 2)
                chain(dve.tensor_scalar(ang[:, :], pos_f[:, :], cst[:, col:col + 1], None, ALU.mult))
                chain(dve.tensor_scalar(cnt[:, :], ang[:, :], float(np.float32(1.0 / TWO_PI)), None, ALU.mult))
                chain(dve.tensor_scalar(cnt[:, :], cnt[:, :], 12582912.0, None, ALU.add))
                chain(dve.tensor_scalar(cnt[:, :], cnt[:, :], -12582912.0, None, ALU.add))
                for part in parts:
                    chain(dve.scalar_tensor_tensor(out=ang[:, :], in0=cnt[:, :], scalar=-part, in1=ang[:, :],
                                                   op0=ALU.mult, op1=ALU.add))
                dve.tensor_scalar(red[:, :], ang[:, :], edge, -edge, ALU.min, ALU.max).then_inc(s.reduced, 1)
                chain(dve.tensor_scalar(ang[:, :], ang[:, :], float(np.pi / 2), None, ALU.add))
                chain(dve.tensor_scalar(wrap[:, :], ang[:, :], edge, -float(TWO_PI), ALU.is_gt, ALU.mult))
                chain(dve.tensor_tensor(ang[:, :], ang[:, :], wrap[:, :], ALU.add))
                dve.tensor_scalar(wrap[:, :], ang[:, :], edge, -edge, ALU.min, ALU.max).then_inc(s.reduced, 1)

        @block.scalar
        def _(act):
            act.activation(m.small[:, S_COND:S_COND + KT], m.small[:, S_COND:S_COND + KT], ACT.Silu).then_inc(s.silu, 1)
            for t in range(2):
                act.wait_ge(s.reduced, 2 * t + 1)
                act.activation(m.table[:, 2 * t + 1, :], red[:, :], ACT.Sin).then_inc(s.used, 1)
                act.wait_ge(s.reduced, 2 * t + 2)
                act.activation(m.table[:, 2 * t, :], wrap[:, :], ACT.Sin).then_inc(s.used, 1)
    with phase(nc, "saved") as (block, s):
        @block.sync
        def _(sp):
            sp.dma_start(a.tables, m.table[:, :, :]).then_inc(s.saved, 16)
            sp.wait_ge(s.saved, 16)


def ada_phase(nc, m, a):
    GRP = 6
    NB = 6 * D // (P * GRP)
    wb = [m.place(f"ada_w{b}", [P, KT, P * GRP], F32, m.R + 24 * 1024 * b) for b in range(3)]
    with phase(nc, "w0", "w1", "w2", "done", "summed", "step") as (block, s):
        w_in = (s.w0, s.w1, s.w2)

        @block.sync
        def _(sp):
            for j in range(DEPTH * NB):
                if j >= 3:
                    sp.wait_ge(s.done, j - 2)
                sp.dma_start(wb[j % 3][:, :, :], w_view(a.ada_w[j // NB], (j % NB) * P * GRP, P * GRP)).then_inc(w_in[j % 3], 16)

        @block.tensor
        def _(pe):
            for j in range(DEPTH * NB):
                pe.wait_ge(w_in[j % 3], 16 * (j // 3) + 16)
                for i in range(GRP):
                    for k in range(KT):
                        last = pe.matmul(m.ps[:, 0, j * GRP + i:j * GRP + i + 1], wb[j % 3][:, k, P * i:P * i + P],
                                         m.small[:, S_COND + k:S_COND + k + 1], start=(k == 0), stop=(k == KT - 1))
                last.then_inc(s.done, 1)

        @block.vector
        def _(dve):
            dve.wait_ge(s.done, DEPTH * NB)
            for l in range(DEPTH):
                v = S_VEC + V_N * l + V_BIAS
                dve.tensor_tensor(m.small[:, S_ADA + 48 * l:S_ADA + 48 * l + 48], m.ps[:, 0, 48 * l:48 * l + 48],
                                  m.small[:, v:v + 48], ALU.add).then_inc(s.summed, 1)
            dve.wait_ge(s.summed, DEPTH)
            for l in range(DEPTH):
                for q in range(2):
                    sc = S_ADA + 48 * l + 8 * (3 * q + 1)
                    i = 8 * (2 * l + q)
                    g = S_VEC + V_N * l + V_NORM + 8 * q
                    dve.scalar_tensor_tensor(out=m.small[:, S_A + i:S_A + i + 8], in0=m.small[:, sc:sc + 8], scalar=1.0,
                                             in1=m.small[:, g:g + 8], op0=ALU.add, op1=ALU.mult).then_inc(s.step, 1)


def param_phase(nc, m, a, l):
    ws = m.place(f"ws_nat{l}", [P, NG, P], F32, m.W0)
    cst = m.const
    with phase(nc, "p_in", "ws_in", "turned", "masked") as (block, s):
        @block.sync
        def _(sp):
            sp.dma_start(ws[:, :, :], a.w_s[l].rearrange("g t s -> t g s")).then_inc(s.ws_in, 16)
            sp.dma_start(m.w_uq[:, :, :], a.w_uq[l].rearrange("(k p) n -> p k n", p=P)).then_inc(s.p_in, 16)
            sp.dma_start(m.w_ukv[:, :], a.w_ukv[l]).then_inc(s.p_in, 16)
            if l:
                sp.dma_start(m.table[:, :, :], a.tables).then_inc(s.p_in, 16)
            for h in range(NG):
                sp.dma_start(m.bs[HD * (h % 2):HD * (h % 2) + HD, h // 2, :], a.b_s[l, h].partition_broadcast(HD)).then_inc(s.p_in, 16)
            sp.wait_ge(s.p_in, 16 * (6 + (l > 0)))

        @block.tensor
        def _(pe):
            pe.wait_ge(s.ws_in, 16)
            for g in range(NG):
                last = pe.transpose(m.ps[:, 0, P * g:P * g + P], ws[:, g, :], cst[:, K_ID:K_ID + P])
            last.then_inc(s.turned, 1)

        @block.vector
        def _(dve):
            dve.wait_ge(s.turned, 1)
            for g in range(NG):
                dve.tensor_tensor(m.ws_t[:, g, :], m.ps[:, 0, P * g:P * g + P], cst[:, K_TRI:K_TRI + P], ALU.mult).then_inc(s.masked, 1)


def norm_phase(nc, m, a, l, which, load, split):
    cst = m.const
    sq = [m.place(f"n_sq{l}{which}{b}", [P, S], F32, m.Z0 + 4096 * b) for b in range(2)]
    rstd = m.place(f"n_rstd{l}{which}", [P, 2, HALF], F32, m.Z0 + 8192)
    tmp = [m.place(f"n_tmp{l}{which}{b}", [P, S], F32, m.Z0 + 12288 + 4096 * b) for b in range(2)]
    hf = [m.place(f"n_hf{l}{which}{b}", [P, S], F32, m.Z0 + 20480 + 4096 * b) for b in range(2)]
    A = S_A + 8 * (2 * l + which)
    B = S_ADA + 48 * l + 24 * which
    with phase(nc, "x_in", "squared", "summed", "var", "inv", "rstd", "scaled", "shifted", "hi", "lo") as (block, s):
        if load:
            @block.sync
            def _(sp):
                for k in range(KT):
                    if k:
                        sp.wait_ge(s.x_in, 16 * k)
                    sp.dma_start(m.x[:, k, :], a.xs[P * k:P * k + P, :]).then_inc(s.x_in, 16)

        @block.scalar
        def _(act):
            for k in range(KT):
                if load:
                    act.wait_ge(s.x_in, 16 * k + 16)
                if k >= 2:
                    act.wait_ge(s.summed, k - 1)
                act.activation(sq[k % 2][:, :], m.x[:, k, :], ACT.Square).then_inc(s.squared, 1)
            act.wait_ge(s.inv, 1)
            act.activation(rstd[:, :, :], rstd[:, :, :], ACT.Sqrt).then_inc(s.rstd, 1)
            if split:
                for k in range(KT):
                    act.wait_ge(s.shifted, k + 1)
                    act.activation(m.h_hi[:, k, :], hf[k % 2][:, :], ACT.Copy).then_inc(s.hi, 1)

        @block.tensor
        def _(pe):
            for k in range(KT):
                pe.wait_ge(s.squared, k + 1)
                for half in range(NHALF):
                    last = pe.matmul(m.ps[:, half, :], cst[:, K_ONE:K_ONE + P], sq[k % 2][:, half * HALF:(half + 1) * HALF],
                                     start=(k == 0), stop=(k == KT - 1))
                last.then_inc(s.summed, 1)

        @block.vector
        def _(dve):
            dve.wait_ge(s.summed, KT)
            dve.tensor_scalar(rstd[:, :, :], m.ps[:, 0:2, :], 1.0 / D, EPS, ALU.mult, ALU.add).then_inc(s.var, 1)
            dve.wait_ge(s.var, 1)
            dve.reciprocal(rstd[:, :, :], rstd[:, :, :]).then_inc(s.inv, 1)
            dve.wait_ge(s.rstd, 1)
            for k in range(KT):
                if k >= 2:
                    dve.wait_ge(s.shifted, k - 1)
                dve.tensor_tensor(tmp[k % 2][:, :], m.x[:, k, :], rstd[:, :, :].rearrange("p a b -> p (a b)"),
                                  ALU.mult).then_inc(s.scaled, 1)
                dve.wait_ge(s.scaled, k + 1)
                if split and k >= 2:
                    dve.wait_ge(s.lo, k - 1)
                dst = hf[k % 2][:, :] if split else m.h_f[:, k, :]
                dve.tensor_scalar(dst, tmp[k % 2][:, :], m.small[:, A + k:A + k + 1], m.small[:, B + k:B + k + 1],
                                  ALU.mult, ALU.add).then_inc(s.shifted, 1)

        if split:
            @block.gpsimd
            def _(pool):
                for k in range(KT):
                    pool.wait_ge(s.hi, k + 1)
                    pool.tensor_tensor(m.h_lo[:, k, :], hf[k % 2][:, :], m.h_hi[:, k, :].bitcast(F32), ALU.subtract).then_inc(s.lo, 1)


def project_phase(nc, m, a, l, col, nblocks, tail_col=None):
    w = a.w_in[l]
    n2 = nblocks // 2
    with phase(nc, "raw0", "raw1", "hi_ready", "lo_ready", "mm_done", "copied") as (block, s):
        @block.sync
        def _(sp):
            def step(i, last):
                for b in range(2):
                    c = tail_col if last and b and tail_col is not None else col + P * (2 * i + b)
                    w_load(sp, s, m, 2 * i + b, b, w_view(w, c))
            looped(sp, n2, step)

        @block.scalar
        def _(act):
            with act.Fori(0, n2) as i:
                for b in range(2):
                    w_round(act, s, m, 2 * i + b, i, b)

        @block.gpsimd
        def _(pool):
            credit_pool(pool, s)
            with pool.Fori(0, n2) as i:
                for b in range(2):
                    w_rest(pool, s, m, 2 * i + b, b)

        @block.tensor
        def _(pe):
            credit_pe(pe, s)
            with pe.Fori(0, n2) as i:
                for b in range(2):
                    pe.wait_ge(s.lo_ready, 2 * i + b + 3)
                    pe.wait_ge(s.copied, 2 * i + b + 1)
                    h_block(pe, m, b, 2 * b).then_inc(s.mm_done, 1)

        @block.vector
        def _(dve):
            dve.sem_inc(s.copied, 2)
            with dve.Fori(0, n2) as i:
                for b in range(2):
                    dve.wait_ge(s.mm_done, 2 * i + b + 3)
                    dve.tensor_scalar(m.z[:, ds(2 * i + b, 1), :, :],
                                      m.ps[:, 2 * b:2 * b + 2, :].rearrange("p (o a) n -> p o a n", o=1),
                                      1.0, None, ALU.mult).then_inc(s.copied, 1)


def zt(m, i, n=1):
    return m.z[:, i:i + n].rearrange("p t a n -> p (t a n)")


def conv_phase(nc, m, l):
    with phase(nc, "u", "acc") as (block, s):
        @block.gpsimd
        def _(pool):
            for t in range(2):
                pool.tensor_tensor(zt(m, 2 + t), zt(m, 2 + t), zt(m, 4 + t), ALU.mult).then_inc(s.u, 1)

        @block.vector
        def _(dve):
            n = 0
            for t in range(2):
                u, y = zt(m, 2 + t), zt(m, 4 + t)
                w = [m.small[:, S_VEC + V_N * l + V_CW + 2 * j + t:S_VEC + V_N * l + V_CW + 2 * j + t + 1] for j in range(3)]
                dve.wait_ge(s.u, t + 1)
                dve.tensor_scalar(y, u, w[2], None, ALU.mult).then_inc(s.acc, 1)
                for j in (1, 0):
                    n += 1
                    dve.wait_ge(s.acc, n)
                    d = 2 - j
                    dve.scalar_tensor_tensor(out=y[:, d:S], in0=u[:, 0:S - d], scalar=w[j], in1=y[:, d:S],
                                             op0=ALU.mult, op1=ALU.add).then_inc(s.acc, 1)
                n += 1
                dve.wait_ge(s.acc, n)
                dve.tensor_tensor(m.ys[:, t, :], y, zt(m, t), ALU.mult).then_inc(s.acc, 1)
                n += 1


def lora_norm_phase(nc, m, l):
    cst = m.const
    sq = m.place(f"l_sq{l}", [P, 3, S], F32, m.W0)
    rstd = m.place(f"l_rstd{l}", [P, 2, S], F32, m.W0 + 12288)
    with phase(nc, "squared", "summed", "var", "inv", "rstd", "done") as (block, s):
        @block.scalar
        def _(act):
            act.activation(sq[:, :, :].rearrange("p t n -> p (t n)"), zt(m, 6, 3), ACT.Square).then_inc(s.squared, 1)
            act.wait_ge(s.inv, 1)
            act.activation(rstd[:, :, :], rstd[:, :, :], ACT.Sqrt).then_inc(s.rstd, 1)

        @block.tensor
        def _(pe):
            pe.wait_ge(s.squared, 1)
            for bank, tiles in ((0, (0, 1)), (2, (2,))):
                for half in range(NHALF):
                    for k in tiles:
                        last = pe.matmul(m.ps[:, bank + half, :], cst[:, K_ONE:K_ONE + P], sq[:, k, half * HALF:(half + 1) * HALF],
                                         start=(k == tiles[0]), stop=(k == tiles[-1]))
            last.then_inc(s.summed, 1)

        @block.vector
        def _(dve):
            dve.wait_ge(s.summed, 1)
            for q, n in ((0, QL), (1, P)):
                dve.tensor_scalar(rstd[:, q, :], m.ps[:, 2 * q:2 * q + 2, :].rearrange("p a n -> p (a n)"), 1.0 / n, EPS,
                                  ALU.mult, ALU.add).then_inc(s.var, 1)
            dve.wait_ge(s.var, 2)
            dve.reciprocal(rstd[:, :, :], rstd[:, :, :]).then_inc(s.inv, 1)
            dve.wait_ge(s.rstd, 1)
            for k in range(3):
                dve.scalar_tensor_tensor(out=zt(m, 6 + k), in0=zt(m, 6 + k), scalar=m.small[:, S_VEC + V_N * l + V_CQ + k:S_VEC + V_N * l + V_CQ + k + 1],
                                         in1=rstd[:, k // 2, :], op0=ALU.mult, op1=ALU.mult).then_inc(s.done, 1)


def qk_phases(nc, m, l):
    cst = m.const
    qk = [m.place(f"qk{l}{n}", [P, 2, S], F32, m.Z0 + 8192 * n if n < 3 else m.W0) for n in range(NG)]
    sq = m.place(f"qk_sq{l}", [P, 2, S], F32, m.W0 + 8192)
    rstd = m.place(f"qk_rstd{l}", [P, 2, S], F32, m.W0 + 16384)
    R = slice(QKN, QK)
    for n in range(NG):
        with phase(nc, "up", "q_in", "k_in", "squared", "summed", "var", "inv", "rstd", "normed", "turned",
                   "cosed", "sined", "done") as (block, s):
            t = qk[n]

            @block.tensor
            def _(pe):
                for half in range(NHALF):
                    for k in range(2):
                        pe.matmul(m.ps[0:QK, half, :], m.w_uq[:, k, QK * n:QK * (n + 1)], m.z[:, 6 + k, half, :],
                                  start=(k == 0), stop=(k == 1))
                for half in range(NHALF):
                    last = pe.matmul(m.ps[0:QKN, 2 + half, :], m.w_ukv[:, P * n:P * n + QKN], m.z[:, 8, half, :],
                                     start=True, stop=True)
                last.then_inc(s.up, 1)
                pe.wait_ge(s.squared, 1)
                for q in range(2):
                    for half in range(NHALF):
                        last = pe.matmul(m.ps[0:QK, 4 + 2 * q + half, :], cst[0:QK, K_ONE:K_ONE + QK],
                                         sq[0:QK, q, half * HALF:(half + 1) * HALF], start=True, stop=True)
                last.then_inc(s.summed, 1)
                pe.wait_ge(s.normed, 2)
                for q in range(2):
                    for half in range(NHALF):
                        last = pe.matmul(m.ps[R, 2 * q + half, :], cst[R, K_PMLA + QKN:K_PMLA + QK],
                                         t[R, q, half * HALF:(half + 1) * HALF], start=True, stop=True)
                last.then_inc(s.turned, 1)

            @block.scalar
            def _(act):
                act.wait_ge(s.up, 1)
                act.activation(t[0:QK, 0, :], m.ps[0:QK, 0:2, :].rearrange("p a n -> p (a n)"), ACT.Copy).then_inc(s.q_in, 1)
                act.wait_ge(s.q_in, 1)
                act.wait_ge(s.k_in, 2)
                act.activation(sq[0:QK], t[0:QK], ACT.Square).then_inc(s.squared, 1)
                act.wait_ge(s.inv, 1)
                act.activation(rstd[0:QK], rstd[0:QK], ACT.Sqrt).then_inc(s.rstd, 1)

            @block.vector
            def _(dve):
                dve.tensor_copy(t[R, 1, :], zt(m, 9)[P - QKR:P, :]).then_inc(s.k_in, 1)
                dve.wait_ge(s.up, 1)
                dve.tensor_copy(t[0:QKN, 1, :], m.ps[0:QKN, 2:4, :].rearrange("p a n -> p (a n)")).then_inc(s.k_in, 1)
                dve.wait_ge(s.summed, 1)
                dve.tensor_scalar(rstd[0:QK].rearrange("p q n -> p (q n)"), m.ps[0:QK, 4:8, :].rearrange("p a n -> p (a n)"),
                                  1.0 / QK, EPS, ALU.mult, ALU.add).then_inc(s.var, 1)
                dve.wait_ge(s.var, 1)
                dve.reciprocal(rstd[0:QK], rstd[0:QK]).then_inc(s.inv, 1)
                dve.wait_ge(s.rstd, 1)
                for q in range(2):
                    dve.scalar_tensor_tensor(out=t[0:QK, q, :], in0=t[0:QK, q, :], scalar=m.small[0:QK, S_VEC + V_N * l + V_QN + q:S_VEC + V_N * l + V_QN + q + 1],
                                             in1=rstd[0:QK, q, :], op0=ALU.mult, op1=ALU.mult).then_inc(s.normed, 1)
                dve.wait_ge(s.turned, 1)
                for q in range(2):
                    dve.tensor_tensor(rstd[R, q, :], m.ps[R, 2 * q:2 * q + 2, :].rearrange("p a n -> p (a n)"),
                                      m.table[R, 3, :], ALU.mult).then_inc(s.sined, 1)
                dve.wait_ge(s.sined, 2)
                dve.wait_ge(s.cosed, 2)
                dve.tensor_tensor(t[R], sq[R], rstd[R], ALU.add).then_inc(s.done, 1)

            @block.gpsimd
            def _(pool):
                pool.wait_ge(s.normed, 2)
                for q in range(2):
                    pool.tensor_tensor(sq[R, q, :], t[R, q, :], m.table[R, 2, :], ALU.mult).then_inc(s.cosed, 1)
    return qk


def attention_phase(nc, m, l, qk):
    cst = m.const
    v = m.place(f"v{l}", [P, ST, MIX], F32, m.Z0 + 4096 * 10)
    prob = [m.place(f"prob{l}{b}", [P, S], F32, m.W0 + 8192 + 4096 * b) for b in range(2)]
    prob_t = [m.place(f"prob_t{l}{b}", [P, ST, P], F32, m.W0 + 16384 + 4096 * b) for b in range(2)]
    stat = m.place(f"attn_stat{l}", [P, 4, NG * ST], F32, m.top)
    steps = [(n, i) for n in range(NG) for i in range(ST)]
    N = len(steps)
    wv = m.w_ukv[:, :].rearrange("p (h c) -> p h c", h=NG)[:, :, QKN:QKN + HD]
    scale = float(QK) ** -0.5
    with phase(nc, "v_up", "v_in", "scored", "maxed", "neg", "exped", "inved", "probs", "turned", "t_in",
               "valued", "o_in") as (block, s):
        @block.tensor
        def _(pe):
            for t in range(ST):
                last = pe.matmul(m.ps[:, 4 + t // 2, MIX * (t % 2):MIX * (t % 2 + 1)], zt(m, 8)[:, P * t:P * t + P], wv,
                                 start=True, stop=True)
                last.then_inc(s.v_up, 1)

            def score(q):
                n, i = steps[q]
                if q >= 2:
                    pe.wait_ge(s.exped, q - 1)
                W = P * (i + 1)
                lhs = qk[n][0:QK, 0, P * i:P * i + P]
                for c in range(0, W, HALF):
                    e = min(W, c + HALF)
                    diag = e == W
                    last = pe.matmul(m.ps[:, 2 * (q % 2) + c // HALF, 0:e - c], lhs, qk[n][0:QK, 1, c:e], start=True, stop=not diag,
                                     skip_group_check=True)
                o = (W - P) % HALF
                last = pe.matmul(m.ps[:, 2 * (q % 2) + (W - P) // HALF, o:o + P], cst[:, K_ID:K_ID + P], cst[:, K_NEG:K_NEG + P],
                                 start=False, stop=True, skip_group_check=True)
                last.then_inc(s.scored, 1)

            def value(q):
                n, i = steps[q]
                pe.wait_ge(s.probs, q + 1)
                if q == 0:
                    pe.wait_ge(s.v_in, 4)
                else:
                    pe.wait_ge(s.t_in, q)
                for c in range(i + 1):
                    last = pe.transpose(m.ps[:, 4 + c // 4, P * (c % 4):P * (c % 4 + 1)], prob[q % 2][:, P * c:P * c + P],
                                        cst[:, K_ID:K_ID + P])
                last.then_inc(s.turned, 1)

            def output(q):
                n, i = steps[q]
                pe.wait_ge(s.t_in, q + 1)
                if q >= 2:
                    pe.wait_ge(s.o_in, q - 1)
                rows = slice(HD * (n % 2), HD * (n % 2) + HD)
                for c in range(i + 1):
                    last = pe.matmul(m.ps[rows, 6 + q % 2, 0:P], v[:, c, HD * n:HD * n + HD], prob_t[q % 2][:, c, :],
                                     start=(c == 0), stop=(c == i))
                last.then_inc(s.valued, 1)

            score(0)
            for q in range(N):
                if q + 1 < N:
                    score(q + 1)
                value(q)
                if q:
                    output(q - 1)
            output(N - 1)

        @block.scalar
        def _(act):
            def copy_turned(act, q):
                W = P * (steps[q][1] + 1)
                act.wait_ge(s.turned, q + 1)
                if q >= 2:
                    act.wait_ge(s.valued, q - 1)
                act.activation(prob_t[q % 2][:, :, :].rearrange("p c n -> p (c n)")[:, 0:W],
                               m.ps[:, 4:6, :].rearrange("p a n -> p (a n)")[:, 0:W], ACT.Copy).then_inc(s.t_in, 1)

            for q in range(N):
                n, i = steps[q]
                W = P * (i + 1)
                if q >= 2:
                    act.wait_ge(s.turned, q - 1)
                act.wait_ge(s.neg, q + 1)
                act.activation(prob[q % 2][:, 0:W], m.ps[:, 2 * (q % 2):2 * (q % 2) + 2, :].rearrange("p a n -> p (a n)")[:, 0:W],
                               ACT.Exp, bias=stat[:, 0, q:q + 1], scale=scale, accum_out=stat[:, 1, q:q + 1]).then_inc(s.exped, 1)
                if q:
                    copy_turned(act, q - 1)
            copy_turned(act, N - 1)

        @block.vector
        def _(dve):
            for t in range(4):
                dve.wait_ge(s.v_up, 2 * t + 2)
                dve.tensor_copy(v[:, 2 * t:2 * t + 2, :].rearrange("p t n -> p (t n)"), m.ps[:, 4 + t, :]).then_inc(s.v_in, 1)

            def row_max(q):
                W = P * (steps[q][1] + 1)
                dve.wait_ge(s.scored, q + 1)
                dve.reduce_max(stat[:, 2, q:q + 1], m.ps[:, 2 * (q % 2):2 * (q % 2) + 2, :].rearrange("p a n -> p (a n)")[:, 0:W],
                               AX.X).then_inc(s.maxed, 1)
                dve.wait_ge(s.maxed, q + 1)
                dve.tensor_scalar(stat[:, 0, q:q + 1], stat[:, 2, q:q + 1], -scale, None, ALU.mult).then_inc(s.neg, 1)

            def normalise(q):
                W = P * (steps[q][1] + 1)
                dve.wait_ge(s.exped, q + 1)
                dve.reciprocal(stat[:, 3, q:q + 1], stat[:, 1, q:q + 1]).then_inc(s.inved, 1)
                dve.wait_ge(s.inved, q + 1)
                dve.tensor_scalar(prob[q % 2][:, 0:W], prob[q % 2][:, 0:W], stat[:, 3, q:q + 1], None, ALU.mult).then_inc(s.probs, 1)

            def out_copy(q):
                n, i = steps[q]
                rows = slice(HD * (n % 2), HD * (n % 2) + HD)
                dve.wait_ge(s.valued, q + 1)
                dve.tensor_copy(m.ys[rows, 2 + n // 2, P * i:P * i + P], m.ps[rows, 6 + q % 2, 0:P]).then_inc(s.o_in, 1)

            row_max(0)
            for q in range(N):
                if q + 1 < N:
                    row_max(q + 1)
                normalise(q)
                if q >= 2:
                    out_copy(q - 2)
            out_copy(N - 2)
            out_copy(N - 1)


def sgu_phases(nc, m, l):
    cst = m.const
    vt = m.place(f"sg_vt{l}", [P, ST, MIX], F32, m.W0)
    sq = m.place(f"sg_sq{l}", [P, 2 * S], F32, m.W0 + 8192)
    rstd = m.place(f"sg_rstd{l}", [P, 2 * S], F32, m.W0 + 16384)
    with phase(nc, "gelu", "squared", "summed", "var", "inv", "rstd", "normed", "turned", "v_in", "mixed", "biased",
               "done") as (block, s):
        @block.scalar
        def _(act):
            act.activation(zt(m, 2, 2), zt(m, 2, 2), ACT.Gelu_apprx_tanh).then_inc(s.gelu, 1)
            act.activation(zt(m, 0, 2), zt(m, 0, 2), ACT.Gelu_apprx_tanh).then_inc(s.gelu, 1)
            act.wait_ge(s.gelu, 2)
            act.activation(sq[:, :], zt(m, 2, 2), ACT.Square).then_inc(s.squared, 1)
            act.wait_ge(s.inv, 1)
            act.activation(rstd[:, :], rstd[:, :], ACT.Sqrt).then_inc(s.rstd, 1)

        @block.tensor
        def _(pe):
            pe.wait_ge(s.squared, 1)
            for i in range(4):
                last = pe.matmul(m.ps[:, i, :], cst[:, K_BLK:K_BLK + P], sq[:, HALF * i:HALF * (i + 1)], start=True, stop=True)
            last.then_inc(s.summed, 1)
            pe.wait_ge(s.normed, 2)
            for c in range(ST):
                for t in range(2):
                    last = pe.transpose(m.ps[:, 4 + c // 2, MIX * (c % 2) + P * t:MIX * (c % 2) + P * t + P],
                                        zt(m, 2 + t)[:, P * c:P * c + P], cst[:, K_ID:K_ID + P])
                last.then_inc(s.turned, 1)
            pe.wait_ge(s.v_in, 4)
            for t in range(2):
                for c in range(ST):
                    for g in (2 * t, 2 * t + 1):
                        rows = slice(HD * (g % 2), HD * (g % 2) + HD)
                        last = pe.matmul(m.ps[rows, 2 * t + c // 4, P * (c % 4):P * (c % 4 + 1)], vt[:, c, HD * g:HD * g + HD],
                                         m.ws_t[:, g, :], start=True, stop=True)
                last.then_inc(s.mixed, 1)

        @block.vector
        def _(dve):
            dve.wait_ge(s.summed, 1)
            dve.tensor_scalar(rstd[:, :], m.ps[:, 0:4, :].rearrange("p a n -> p (a n)"), 1.0 / HD, EPS, ALU.mult, ALU.add).then_inc(s.var, 1)
            dve.wait_ge(s.var, 1)
            dve.reciprocal(rstd[:, :], rstd[:, :]).then_inc(s.inv, 1)
            dve.wait_ge(s.rstd, 1)
            for t in range(2):
                dve.scalar_tensor_tensor(out=zt(m, 2 + t), in0=zt(m, 2 + t), scalar=m.small[:, S_VEC + V_N * l + V_GV + t:S_VEC + V_N * l + V_GV + t + 1],
                                         in1=rstd[:, S * t:S * t + S], op0=ALU.mult, op1=ALU.mult).then_inc(s.normed, 1)
            for i in range(4):
                dve.wait_ge(s.turned, 2 * i + 2)
                dve.tensor_copy(vt[:, 2 * i:2 * i + 2, :].rearrange("p c n -> p (c n)"), m.ps[:, 4 + i, :]).then_inc(s.v_in, 1)
            for t in range(2):
                dve.wait_ge(s.mixed, t + 1)
                dve.tensor_tensor(sq[:, S * t:S * t + S].rearrange("p (c n) -> p c n", n=P),
                                  m.ps[:, 2 * t:2 * t + 2, :].rearrange("p a (c n) -> p (a c) n", n=P),
                                  m.bs[:, t:t + 1, :].broadcast_to([P, ST, P]), ALU.add).then_inc(s.biased, 1)
                dve.wait_ge(s.biased, t + 1)
                dve.wait_ge(s.gelu, 2)
                dve.tensor_tensor(m.ys[:, 4 + t, :], sq[:, S * t:S * t + S], zt(m, t), ALU.mult).then_inc(s.done, 1)


def retention_phases(nc, m, l):
    cst = m.const
    KB = 1024
    vt = m.place(f"rt_vt{l}", [P, ST, MIX], F32, m.Z0)
    kd = m.place(f"rt_kd{l}", [P, ST, MIX], F32, m.Z0 + 8 * KB)
    tmp = m.place(f"rt_tmp{l}", [P, 4, S], F32, m.W0)
    qd = m.place(f"rt_qd{l}", [P, 2, S], F32, m.W0)
    out = m.place(f"rt_out{l}", [P, 2 * S], F32, m.W0 + 8 * KB)
    state = m.place(f"rt_state{l}", [P, ST, 2, HD], F32, m.W0 + 16 * KB)
    pr = [m.place(f"rt_p{l}{b}", [P, 2, 2 * P], F32, m.W0 + (20 + 2 * b) * KB) for b in range(2)]
    sq = m.place(f"rt_sq{l}", [P, 2 * S], F32, m.Z0 + 16 * KB)
    rstd = m.place(f"rt_rstd{l}", [P, 2 * S], F32, m.Z0 + 24 * KB)
    with phase(nc, "turned", "cosed", "sined", "done", "silu") as (block, s):
        @block.scalar
        def _(act):
            act.activation(zt(m, 10, 2), zt(m, 10, 2), ACT.Silu).then_inc(s.silu, 1)

        @block.tensor
        def _(pe):
            for t in range(4):
                for half in range(NHALF):
                    last = pe.matmul(m.ps[:, 2 * t + half, :], cst[:, K_PRET:K_PRET + P], m.z[:, 4 + t, half, :], start=True, stop=True)
                last.then_inc(s.turned, 1)

        @block.gpsimd
        def _(pool):
            for t in range(4):
                pool.wait_ge(s.turned, t + 1)
                pool.tensor_tensor(zt(m, 4 + t), zt(m, 4 + t), m.table[:, 0, :], ALU.mult).then_inc(s.cosed, 1)

        @block.vector
        def _(dve):
            for t in range(4):
                dve.wait_ge(s.turned, t + 1)
                dve.tensor_tensor(tmp[:, t, :], m.ps[:, 2 * t:2 * t + 2, :].rearrange("p a n -> p (a n)"),
                                  m.table[:, 1, :], ALU.mult).then_inc(s.sined, 1)
                dve.wait_ge(s.sined, t + 1)
                dve.wait_ge(s.cosed, t + 1)
                dve.tensor_tensor(zt(m, 4 + t), zt(m, 4 + t), tmp[:, t, :], ALU.add).then_inc(s.done, 1)
    with phase(nc, "qd", "k_turned", "v_turned", "kd_in", "v_in", "kv", "state", "scored", "decayed", "o", "o_in") as (block, s):
        @block.tensor
        def _(pe):
            for c in range(ST):
                b = c % 2
                if c >= 2:
                    pe.wait_ge(s.v_in, c - 1)
                    pe.wait_ge(s.kd_in, c - 1)
                for first, bank, sem in ((6, 2 * b, s.k_turned), (8, 2 * b + 1, s.v_turned)):
                    for t in range(2):
                        last = pe.transpose(m.ps[:, bank, P * t:P * t + P], zt(m, first + t)[:, P * c:P * c + P], cst[:, K_ID:K_ID + P])
                    last.then_inc(sem, 1)
            for c in range(ST - 1):
                pe.wait_ge(s.v_in, c + 1)
                pe.wait_ge(s.kd_in, c + 1)
                if c >= 2:
                    pe.wait_ge(s.state, 2 * (c - 1) + 1)
                for h in range(NG):
                    rows = slice(HD * (h % 2), HD * (h % 2) + HD)
                    cols = slice(HD * h, HD * h + HD)
                    last = pe.matmul(m.ps[rows, 4 + c % 2, HD * (h // 2):HD * (h // 2) + HD], kd[:, c, cols], vt[:, c, cols],
                                     start=True, stop=True)
                last.then_inc(s.kv, 1)

            def scores(c):
                if c == 1:
                    pe.wait_ge(s.state, 2 * ST - 1)
                if c >= 2:
                    pe.wait_ge(s.decayed, c - 1)
                for h in range(NG):
                    rows = slice(HD * (h % 2), HD * (h % 2) + HD)
                    last = pe.matmul(m.ps[:, 6 - 2 * (c % 2) + h % 2, P * (h // 2):P * (h // 2) + P], zt(m, 6 + h // 2)[rows, P * c:P * c + P],
                                     zt(m, 4 + h // 2)[rows, P * c:P * c + P], start=True, stop=True)
                last.then_inc(s.scored, 1)

            scores(0)
            for c in range(ST):
                if c + 1 < ST:
                    scores(c + 1)
                pe.wait_ge(s.decayed, c + 1)
                if c == 0:
                    pe.wait_ge(s.v_in, ST)
                    pe.wait_ge(s.kd_in, ST)
                    pe.wait_ge(s.qd, 2)
                pe.wait_ge(s.state, 2 * c + 1)
                if c >= 2:
                    pe.wait_ge(s.o_in, c - 1)
                for h in range(NG):
                    rows = slice(HD * (h % 2), HD * (h % 2) + HD)
                    dst = m.ps[rows, c % 2, P * (h // 2):P * (h // 2) + P]
                    pe.matmul(dst, vt[:, c, HD * h:HD * h + HD], pr[c % 2][:, h % 2, P * (h // 2):P * (h // 2) + P],
                              start=True, stop=(c == 0),
                              skip_group_check=True)
                    if c:
                        pe.matmul(dst, state[rows, c, h // 2, :], qd[rows, h // 2, P * c:P * c + P], start=False, stop=True,
                                  skip_group_check=True)
                pe.drain().then_inc(s.o, 1)

        @block.scalar
        def _(act):
            for c in range(ST):
                act.wait_ge(s.v_turned, c + 1)
                act.activation(vt[:, c, :], m.ps[:, 2 * (c % 2) + 1, 0:MIX], ACT.Copy).then_inc(s.v_in, 1)
            for c in range(ST):
                act.wait_ge(s.o, c + 1)
                act.activation(out[:, :].rearrange("p (t c n) -> p t c n", t=2, n=P)[:, :, c, :],
                               m.ps[:, c % 2, 0:MIX].rearrange("p (t n) -> p t n", t=2), ACT.Copy).then_inc(s.o_in, 1)

        @block.vector
        def _(dve):
            for t in range(2):
                dve.tensor_tensor(qd[:, t, :].rearrange("p (c n) -> p c n", n=P), zt(m, 4 + t).rearrange("p (c n) -> p c n", n=P),
                                  cst[:, K_QDEC + P * t:K_QDEC + P * t + P].rearrange("p (o n) -> p o n", o=1).broadcast_to([P, ST, P]),
                                  ALU.mult).then_inc(s.qd, 1)
            for c in range(ST):
                dve.wait_ge(s.k_turned, c + 1)
                dve.tensor_tensor(kd[:, c, :], m.ps[:, 2 * (c % 2), 0:MIX], cst[:, K_KDEC:K_KDEC + MIX], ALU.mult).then_inc(s.kd_in, 1)
            dve.memset(state[:, 0], 0.0).then_inc(s.state, 1)
            for c in range(ST - 1):
                dve.wait_ge(s.state, 2 * c + 1)
                dve.wait_ge(s.kv, c + 1)
                for t in range(2):
                    dve.scalar_tensor_tensor(out=state[:, c + 1, t, :], in0=state[:, c, t, :], scalar=cst[:, K_CD + t:K_CD + t + 1],
                                             in1=m.ps[:, 4 + c % 2, HD * t:HD * t + HD], op0=ALU.mult, op1=ALU.add).then_inc(s.state, 1)
            for c in range(ST):
                dve.wait_ge(s.scored, c + 1)
                if c >= 2:
                    dve.wait_ge(s.o, c - 1)
                dve.tensor_tensor(pr[c % 2][:, :, :], m.ps[:, 6 - 2 * (c % 2):8 - 2 * (c % 2), 0:2 * P],
                                  cst[:, K_DEC:K_DEC + NG * P].rearrange("p (a n) -> p a n", a=2), ALU.mult).then_inc(s.decayed, 1)
    with phase(nc, "mean", "centred", "squared", "summed", "var", "inv", "rstd", "scaled", "done") as (block, s):
        @block.tensor
        def _(pe):
            for i in range(4):
                last = pe.matmul(m.ps[:, i, :], cst[:, K_BLK:K_BLK + P], out[:, HALF * i:HALF * (i + 1)], start=True, stop=True)
            last.then_inc(s.mean, 1)
            pe.wait_ge(s.squared, 1)
            for i in range(4):
                last = pe.matmul(m.ps[:, 4 + i, :], cst[:, K_BLK:K_BLK + P], sq[:, HALF * i:HALF * (i + 1)], start=True, stop=True)
            last.then_inc(s.summed, 1)

        @block.scalar
        def _(act):
            act.wait_ge(s.centred, 1)
            act.activation(sq[:, :], out[:, :], ACT.Square).then_inc(s.squared, 1)
            act.wait_ge(s.inv, 1)
            act.activation(rstd[:, :], rstd[:, :], ACT.Sqrt).then_inc(s.rstd, 1)

        @block.vector
        def _(dve):
            dve.wait_ge(s.mean, 1)
            dve.scalar_tensor_tensor(out=out[:, :], in0=m.ps[:, 0:4, :].rearrange("p a n -> p (a n)"), scalar=-1.0 / HD,
                                     in1=out[:, :], op0=ALU.mult, op1=ALU.add).then_inc(s.centred, 1)
            dve.wait_ge(s.summed, 1)
            dve.tensor_scalar(rstd[:, :], m.ps[:, 4:8, :].rearrange("p a n -> p (a n)"), 1.0 / HD, EPS, ALU.mult, ALU.add).then_inc(s.var, 1)
            dve.wait_ge(s.var, 1)
            dve.reciprocal(rstd[:, :], rstd[:, :]).then_inc(s.inv, 1)
            dve.wait_ge(s.rstd, 1)
            for t in range(2):
                dve.scalar_tensor_tensor(out=sq[:, S * t:S * t + S], in0=out[:, S * t:S * t + S],
                                         scalar=m.small[:, S_VEC + V_N * l + V_RET + t:S_VEC + V_N * l + V_RET + t + 1],
                                         in1=rstd[:, S * t:S * t + S], op0=ALU.mult, op1=ALU.mult).then_inc(s.scaled, 1)
                dve.wait_ge(s.scaled, t + 1)
                dve.tensor_tensor(m.ys[:, 6 + t, :], sq[:, S * t:S * t + S], zt(m, 10 + t), ALU.mult).then_inc(s.done, 1)


def gate_phase(nc, m, a, l):
    KB = 1024
    merged = m.place(f"merged{l}", [P, KT, S], F32, m.Z0)
    wb = [m.place(f"w_br{l}{b}", [P, 2, P], F32, m.Z0 + (32 + b) * KB) for b in range(2)]
    sig = [m.place(f"sig{l}{b}", [P, S], F32, m.Z0 + (34 + 4 * b) * KB) for b in range(2)]
    w = a.w_in[l]
    with phase(nc, "raw0", "raw1", "br0", "br1", "hi_ready", "lo_ready", "mm_done", "sig_ready", "gated", "summed") as (block, s):
        @block.sync
        def _(sp):
            with sp.Fori(0, KT) as mt:
                for n in range(NBR):
                    sp.wait_ge(s.mm_done, NBR * mt + n + 1)
                    w_load(sp, s, m, NBR * mt + n, n % 2, w_view(w, P * mt + (C_GATE + D * n)))
                    sp.dma_start(wb[n % 2][:, :, :], w_view(a.w_branch[l, n], P * mt)).then_inc((s.br0, s.br1)[n % 2], 16)

        @block.scalar
        def _(act):
            w_round(act, s, m, 0, 0, 0)

            def step(mt, last):
                for n in range(NBR):
                    if not (last and n == NBR - 1):
                        w_round(act, s, m, NBR * mt + n + 1, 2 * mt + (n + 1) // 2, (n + 1) % 2)
                    act.wait_ge(s.mm_done, NBR * mt + n + 3)
                    act.wait_ge(s.summed, NBR * mt + n + 1)
                    act.activation(sig[n % 2][:, :], m.ps[:, 4 * (n % 2):4 * (n % 2) + 2, :].rearrange("p a n -> p (a n)"),
                                   ACT.Sigmoid).then_inc(s.sig_ready, 1)
            looped(act, KT, step)

        @block.gpsimd
        def _(pool):
            credit_pool(pool, s)
            with pool.Fori(0, KT) as mt:
                for n in range(NBR):
                    w_rest(pool, s, m, NBR * mt + n, n % 2)

        @block.tensor
        def _(pe):
            credit_pe(pe, s)
            with pe.Fori(0, KT) as mt:
                for n in range(NBR):
                    b = n % 2
                    pe.wait_ge(s.lo_ready, NBR * mt + n + 3)
                    pe.wait_ge(s.summed, NBR * mt + n + 1)
                    h_block(pe, m, b, 4 * b)
                    pe.wait_ge((s.br0, s.br1)[b], 32 * mt + 16 * (n // 2) + 16)
                    for half in range(NHALF):
                        for k in range(2):
                            last = pe.matmul(m.ps[:, 4 * b + 2 + half, :], wb[b][:, k, :],
                                             m.ys[:, 2 * n + k, half * HALF:(half + 1) * HALF], start=(k == 0), stop=(k == 1))
                    last.then_inc(s.mm_done, 1)

        @block.vector
        def _(dve):
            dve.sem_inc(s.summed, 2)
            with dve.Fori(0, KT) as mt:
                dst = merged[:, ds(mt, 1), :].rearrange("p o n -> p (o n)")
                for n in range(NBR):
                    b = n % 2
                    dve.wait_ge(s.sig_ready, NBR * mt + n + 1)
                    prod = m.ps[:, 4 * b + 2:4 * b + 4, :].rearrange("p a n -> p (a n)")
                    if n == 0:
                        dve.tensor_tensor(dst, sig[b][:, :], prod, ALU.mult).then_inc(s.summed, 1)
                    else:
                        dve.tensor_tensor(sig[b][:, :], sig[b][:, :], prod, ALU.mult).then_inc(s.gated, 1)
                        dve.wait_ge(s.gated, (NBR - 1) * mt + n)
                        dve.wait_ge(s.summed, NBR * mt + n + 2)
                        dve.tensor_tensor(dst, dst, sig[b][:, :], ALU.add).then_inc(s.summed, 1)
    return merged


def out_proj_phase(nc, m, a, l, merged):
    w = a.w_o[l]
    G1 = S_ADA + 48 * l + 16
    with phase(nc, "raw0", "raw1", "hi_ready", "lo_ready", "mm_done", "m_hi", "m_lo", "x_in", "added", "stored") as (block, s):
        @block.sync
        def _(sp):
            for b in range(2):
                w_load(sp, s, m, b, b, w_view(w, P * b))
            sp.dma_start(m.x[:, :, :], a.xs.rearrange("(k p) n -> p k n", p=P)).then_inc(s.x_in, 16)
            for j in range(2, KT):
                w_load(sp, s, m, j, j % 2, w_view(w, P * j))
            for k in range(KT):
                sp.wait_ge(s.added, k + 3)
                sp.dma_start(a.xs[P * k:P * k + P, :], m.x[:, k, :]).then_inc(s.stored, 16)
            sp.wait_ge(s.stored, 16 * KT)

        @block.scalar
        def _(act):
            for b in range(2):
                w_round(act, s, m, b, 0, b)
            for k in range(KT):
                act.activation(m.h_hi[:, k, :], merged[:, k, :], ACT.Copy).then_inc(s.m_hi, 1)
            for j in range(2, KT):
                w_round(act, s, m, j, j // 2, j % 2)

        @block.gpsimd
        def _(pool):
            credit_pool(pool, s)
            for b in range(2):
                w_rest(pool, s, m, b, b)
            for j in range(2, KT):
                w_rest(pool, s, m, j, j % 2)

        @block.tensor
        def _(pe):
            credit_pe(pe, s)
            pe.wait_ge(s.m_lo, KT)
            for j in range(KT):
                pe.wait_ge(s.lo_ready, j + 3)
                pe.wait_ge(s.added, j + 1)
                h_block(pe, m, j % 2, 2 * (j % 2)).then_inc(s.mm_done, 1)

        @block.vector
        def _(dve):
            dve.sem_inc(s.added, 2)
            for k in range(KT):
                dve.wait_ge(s.m_hi, k + 1)
                dve.tensor_tensor(m.h_lo[:, k, :], merged[:, k, :], m.h_hi[:, k, :].bitcast(F32), ALU.subtract).then_inc(s.m_lo, 1)
            dve.wait_ge(s.x_in, 16)
            for j in range(KT):
                dve.wait_ge(s.mm_done, j + 3)
                dve.scalar_tensor_tensor(out=m.x[:, j, :], in0=m.ps[:, 2 * (j % 2):2 * (j % 2) + 2, :].rearrange("p a n -> p (a n)"),
                                         scalar=m.small[:, G1 + j:G1 + j + 1], in1=m.x[:, j, :], op0=ALU.mult,
                                         op1=ALU.add).then_inc(s.added, 1)


def ffn_phases(nc, m, a, l):
    KB = 1024
    hid_hi = m.place(f"hid_hi{l}", [P, FT, HALF], F32R, m.R + 88 * KB)
    hid_lo = m.place(f"hid_lo{l}", [P, FT, HALF], F32R, m.R + 132 * KB)
    act_t = [m.place(f"f_act{l}{b}", [P, HALF], F32, m.R + (176 + 2 * b) * KB) for b in range(2)]
    hid_f = [m.place(f"f_hid{l}{b}", [P, HALF], F32, m.R + (180 + 2 * b) * KB) for b in range(2)]
    x_t = [m.place(f"f_x{l}{b}", [P, HALF], F32, m.R + (184 + 2 * b) * KB) for b in range(2)]
    G2 = S_ADA + 48 * l + 40
    e = l // 2
    parts = [(0, 8), (8, 16), (16, FT)]
    for half in range(NHALF):
        tok = slice(half * HALF, (half + 1) * HALF)
        with phase(nc, "raw0", "raw1", "hi_ready", "lo_ready", "mm_done", "silu", "hid", "hid_hi", "hid_lo") as (block, s):
            @block.sync
            def _(sp):
                with sp.Fori(0, FT) as f:
                    for b, w in enumerate((a.ffn_w1[e], a.ffn_w3[e])):
                        w_load(sp, s, m, 2 * f + b, b, w_view(w, P * f))

            @block.scalar
            def _(act):
                for b in range(2):
                    w_round(act, s, m, b, 0, b)

                def step(i, last):
                    for c in range(2):
                        f = 2 * i + c
                        if not (last and c):
                            for b in range(2):
                                w_round(act, s, m, 2 * f + 2 + b, f + 1, b)
                        act.wait_ge(s.mm_done, 2 * f + 4)
                        act.wait_ge(s.hid, f + 1)
                        act.activation(act_t[c][:, :], m.ps[:, 2 * c, :], ACT.Silu).then_inc(s.silu, 1)
                looped(act, FT // 2, step)

            @block.gpsimd
            def _(pool):
                credit_pool(pool, s)
                with pool.Fori(0, FT) as f:
                    for b in range(2):
                        w_rest(pool, s, m, 2 * f + b, b)

            @block.tensor
            def _(pe):
                credit_pe(pe, s)
                with pe.Fori(0, FT // 2) as i:
                    for c in range(2):
                        pe.wait_ge(s.hid, 2 * i + c + 1)
                        for b in range(2):
                            pe.wait_ge(s.lo_ready, 4 * i + 2 * c + b + 3)
                            for k in range(KT):
                                last = mm3(pe, m.ps[:, 2 * c + b, :], m.w_hi[b][:, k, :], m.w_lo[b][:, k, :],
                                           m.h_hi[:, k, tok], m.h_lo[:, k, tok], k == 0, k == KT - 1)
                            last.then_inc(s.mm_done, 1)

            @block.vector
            def _(dve):
                dve.sem_inc(s.hid, 2)
                with dve.Fori(0, FT // 2) as i:
                    for c in range(2):
                        f = 2 * i + c
                        dve.wait_ge(s.silu, f + 1)
                        dve.wait_ge(s.mm_done, 2 * f + 4)
                        dve.tensor_tensor(hid_f[c][:, :], act_t[c][:, :], m.ps[:, 2 * c + 1, :], ALU.mult).then_inc(s.hid, 1)
                        dve.wait_ge(s.hid, f + 3)
                        dve.tensor_scalar(hid_hi[:, ds(f, 1), :], hid_f[c][:, :].rearrange("p (o n) -> p o n", o=1), 1.0, None,
                                          ALU.mult).then_inc(s.hid_hi, 1)
                        dve.wait_ge(s.hid_hi, f + 1)
                        dve.tensor_tensor(hid_lo[:, ds(f, 1), :], hid_f[c][:, :].rearrange("p (o n) -> p o n", o=1),
                                          hid_hi[:, ds(f, 1), :].bitcast(F32), ALU.subtract).then_inc(s.hid_lo, 1)
        with phase(nc, "raw0", "raw1", "hi_ready", "lo_ready", "mm_done", "x0", "x1", "tile", "added", "st0", "st1") as (block, s):
            @block.sync
            def _(sp):
                for j in range(KT):
                    c = j % 2
                    if j >= 2:
                        sp.wait_ge((s.st0, s.st1)[c], 16 * (j // 2))
                    sp.dma_start(x_t[c][:, :], a.xs[P * j:P * j + P, tok]).then_inc((s.x0, s.x1)[c], 16)
                    for q, (k0, k1) in enumerate(parts):
                        w_load(sp, s, m, 3 * j + q, (c + q) % 2, w_view(a.ffn_w2[e][P * k0:P * k1, :], P * j), k1 - k0)
                        if j and q == 1:
                            sp.wait_ge(s.added, j + 2)
                            sp.dma_start(a.xs[P * (j - 1):P * j, tok], x_t[1 - c][:, :]).then_inc((s.st0, s.st1)[1 - c], 16)
                sp.wait_ge(s.added, KT + 2)
                sp.dma_start(a.xs[P * (KT - 1):D, tok], x_t[(KT - 1) % 2][:, :]).then_inc((s.st0, s.st1)[(KT - 1) % 2], 16)
                sp.wait_ge(s.st0, 16 * KT // 2)
                sp.wait_ge(s.st1, 16 * KT // 2)

            @block.scalar
            def _(act):
                for j in range(KT):
                    c = j % 2
                    for q, (k0, k1) in enumerate(parts):
                        w_round(act, s, m, 3 * j + q, (3 * j + q) // 2, (c + q) % 2, k1 - k0)

            @block.gpsimd
            def _(pool):
                credit_pool(pool, s)
                with pool.Fori(0, KT // 2) as i:
                    for c in range(2):
                        for q, (k0, k1) in enumerate(parts):
                            w_rest(pool, s, m, 6 * i + 3 * c + q, (c + q) % 2, k1 - k0)

            @block.tensor
            def _(pe):
                credit_pe(pe, s)
                with pe.Fori(0, KT // 2) as i:
                    for c in range(2):
                        pe.wait_ge(s.added, 2 * i + c + 1)
                        for q, (k0, k1) in enumerate(parts):
                            b = (c + q) % 2
                            pe.wait_ge(s.lo_ready, 6 * i + 3 * c + q + 3)
                            for k in range(k0, k1):
                                last = mm3(pe, m.ps[:, c, :], m.w_hi[b][:, k - k0, :], m.w_lo[b][:, k - k0, :],
                                           hid_hi[:, k, :], hid_lo[:, k, :], k == 0, k == FT - 1)
                            last.then_inc(s.mm_done, 1)

            @block.vector
            def _(dve):
                dve.sem_inc(s.added, 2)
                for j in range(KT):
                    c = j % 2
                    dve.wait_ge((s.x0, s.x1)[c], 16 * (j // 2) + 16)
                    dve.wait_ge(s.mm_done, 3 * j + 5)
                    dve.scalar_tensor_tensor(out=x_t[c][:, :], in0=m.ps[:, c, :], scalar=m.small[:, G2 + j:G2 + j + 1],
                                             in1=x_t[c][:, :], op0=ALU.mult, op1=ALU.add).then_inc(s.added, 1)


ITEM = 256
SLOTS = 2 * S
MAX_ITEMS = (SLOTS + NE * (ITEM - 1)) // ITEM
FGRP = 4
NFG = FE // (P * FGRP)
NF2 = FE // (2 * P)


def moe_memory(m):
    KB = 1024
    R = m.R
    m.hrow = m.place("h_rows", [P, ST, D], F32, R + 32 * KB)
    E = R + 196 * KB
    m.slot = m.place("slot", [P, ST, 2], I32, E)
    m.top_w = m.place("top_w", [P, ST, 2], F32, E + 64)
    m.items = m.place("items", [1, (MAX_ITEMS + 1) * 4], I32, E + 128)
    m.route = R + 70 * KB


def route_phase(nc, m, a, l):
    cst = m.const
    rw = m.place("router_w_sb", [P, KT, NE], F32, m.route)
    rb = m.place("router_b_sb", [P, NE], F32, m.route + 256)
    big = m.R + 64 * 1024

    def grid(name, i, dt=F32, shape=(ST, NE)):
        return m.place(name, [P, *shape], dt, big + 256 * i)

    lg, pr, one0, one1, both, rank, t0 = (grid(n, i) for i, n in enumerate(
        ("r_logit", "r_prob", "r_hot0", "r_hot1", "r_both", "r_rank", "r_tmp")))
    top = grid("r_top", 7)
    idx = grid("r_idx", 8, U32)
    idx_f = grid("r_idxf", 9)
    mx, sm, inv, tw = (m.place(n, [P, ST], F32, big + 2560 + 32 * i) for i, n in enumerate(("r_mx", "r_sm", "r_inv", "r_tw")))
    cnt, off, nch, end, beg, c0, c1, hot, val = (m.place(n, [P, NE], F32, big + 2688 + 32 * i) for i, n in enumerate(
        ("r_cnt", "r_off", "r_nch", "r_end", "r_beg", "r_c0", "r_c1", "r_hot", "r_val")))
    tab_f = m.place("r_tabf", [P, 4], F32, big + 3072)
    tab = m.place("r_tab", [P, 4], I32, big + 3104)
    slot_f = m.place("r_slotf", [P, ST, 2], F32, big + 3136)
    e = l // 2
    with phase(nc, "w_in", "turned", "h_in", "logits", "shifted", "exped", "hot", "ranked", "step", "tab", "saved", "back") as (block, s):
        @block.sync
        def _(sp):
            sp.dma_start(rw[:, :, :], a.router_w[e].rearrange("(k p) n -> p k n", p=P)).then_inc(s.w_in, 16)
            sp.dma_start(rb[:, :], a.router_b[e].partition_broadcast(P)).then_inc(s.w_in, 16)
            sp.wait_ge(s.tab, 1)
            sp.dma_start(a.items, tab[0:MAX_ITEMS + 1, :]).then_inc(s.saved, 16)
            sp.wait_ge(s.saved, 16)
            sp.dma_start(m.items[:, :], a.items.rearrange("(o i) c -> o (i c)", o=1)).then_inc(s.back, 16)
            sp.wait_ge(s.back, 16)

        @block.tensor
        def _(pe):
            pe.wait_ge(s.w_in, 32)
            for t in range(ST):
                for k in range(KT):
                    last = pe.matmul(m.ps[:, 7, NE * t:NE * t + NE], m.h_f[:, k, P * t:P * t + P], rw[:, k, :],
                                     start=(k == 0), stop=(k == KT - 1))
            last.then_inc(s.logits, 1)
            for t in range(ST):
                if t >= 2:
                    pe.wait_ge(s.h_in, t - 1)
                for k in range(KT):
                    last = pe.transpose(m.ps[:, 2 * (t % 2) + k // 4, P * (k % 4):P * (k % 4 + 1)],
                                        m.h_f[:, k, P * t:P * t + P], cst[:, K_ID:K_ID + P])
                last.then_inc(s.turned, 1)
            pe.wait_ge(s.hot, 1)
            for t in range(ST):
                for u in range(t + 1):
                    w = K_LOW if u == t else K_ONE
                    last = pe.matmul(m.ps[:, 6, NE * t:NE * t + NE], cst[:, w:w + P], both[:, u, :], start=(u == 0), stop=(u == t))
            for u in range(ST):
                last = pe.matmul(m.ps[:, 5, 0:NE], cst[:, K_ONE:K_ONE + P], both[:, u, :], start=(u == 0), stop=(u == ST - 1))
            last.then_inc(s.ranked, 1)

        @block.scalar
        def _(act):
            for t in range(ST):
                act.wait_ge(s.turned, t + 1)
                act.activation(m.hrow[:, t, :], m.ps[:, 2 * (t % 2):2 * (t % 2) + 2, :].rearrange("p a n -> p (a n)"), ACT.Copy).then_inc(s.h_in, 1)
            act.wait_ge(s.shifted, 1)
            act.activation(pr[:, :, :], lg[:, :, :], ACT.Exp).then_inc(s.exped, 1)

        @block.vector
        def _(dve):
            n = 0

            def chain(ins):
                nonlocal n
                n += 1
                ins.then_inc(s.step, 1)
                dve.wait_ge(s.step, n)

            def wide(v):
                return v[:, :].rearrange("p (t o) -> p t o", o=1).broadcast_to([P, ST, NE])

            def row(v):
                return v[:, :].rearrange("p (o e) -> p o e", o=1).broadcast_to([P, ST, NE])

            dve.wait_ge(s.logits, 1)
            dve.wait_ge(s.w_in, 32)
            chain(dve.tensor_tensor(lg[:, :, :], m.ps[:, 7, 0:ST * NE].rearrange("p (t e) -> p t e", e=NE), row(rb), ALU.add))
            chain(dve.tensor_reduce(mx[:, :], lg[:, :, :], AX.X, ALU.max))
            dve.tensor_tensor(lg[:, :, :], lg[:, :, :], wide(mx), ALU.subtract).then_inc(s.shifted, 1)
            dve.wait_ge(s.exped, 1)
            chain(dve.tensor_reduce(sm[:, :], pr[:, :, :], AX.X, ALU.add))
            chain(dve.reciprocal(inv[:, :], sm[:, :]))
            chain(dve.tensor_tensor(pr[:, :, :], pr[:, :, :], wide(inv), ALU.mult))
            for t in range(ST):
                chain(dve.max(top[:, t, :], pr[:, t, :]))
                chain(dve.max_index(idx[:, t, :], top[:, t, :], pr[:, t, :]))
            chain(dve.tensor_copy(idx_f[:, :, :], idx[:, :, :]))
            chain(dve.tensor_tensor(tw[:, :], top[:, :, 0], top[:, :, 1], ALU.add))
            chain(dve.reciprocal(tw[:, :], tw[:, :]))
            experts = cst[:, K_EXP:K_EXP + NE].rearrange("p (o e) -> p o e", o=1).broadcast_to([P, ST, NE])
            for q, one in enumerate((one0, one1)):
                chain(dve.tensor_tensor(m.top_w[:, :, q], top[:, :, q], tw[:, :], ALU.mult))
                chain(dve.tensor_tensor(one[:, :, :], idx_f[:, :, q:q + 1].broadcast_to([P, ST, NE]), experts, ALU.is_equal))
            dve.tensor_tensor(both[:, :, :], one0[:, :, :], one1[:, :, :], ALU.add).then_inc(s.hot, 1)
            dve.wait_ge(s.ranked, 1)
            chain(dve.tensor_copy(cnt[:, :], m.ps[:, 5, 0:NE]))

            def prefix(out, v):
                chain(dve.memset(out[:, 0:1], 0.0))
                for j in range(1, NE):
                    chain(dve.tensor_tensor(out[:, j:j + 1], out[:, j - 1:j], v[:, j - 1:j], ALU.add))

            prefix(off, cnt)
            chain(dve.tensor_tensor(rank[:, :, :], m.ps[:, 6, 0:ST * NE].rearrange("p (t e) -> p t e", e=NE), row(off), ALU.add))
            for q, one in enumerate((one0, one1)):
                chain(dve.tensor_tensor(t0[:, :, :], rank[:, :, :], one[:, :, :], ALU.mult))
                chain(dve.tensor_reduce(slot_f[:, :, q], t0[:, :, :], AX.X, ALU.add))
            chain(dve.tensor_copy(m.slot[:, :, :], slot_f[:, :, :]))
            chain(dve.tensor_scalar(nch[:, :], cnt[:, :], 0.0, None, ALU.is_gt))
            for j in range(1, S // ITEM):
                chain(dve.scalar_tensor_tensor(out=nch[:, :], in0=cnt[:, :], scalar=float(ITEM * j), in1=nch[:, :], op0=ALU.is_gt, op1=ALU.add))
            prefix(beg, nch)
            chain(dve.tensor_tensor(end[:, :], beg[:, :], nch[:, :], ALU.add))
            item = cst[:, K_ITEM:K_ITEM + 1]
            chain(dve.tensor_scalar(c0[:, :], beg[:, :], item, None, ALU.is_le))
            chain(dve.tensor_scalar(c1[:, :], end[:, :], item, None, ALU.is_gt))
            chain(dve.tensor_tensor(hot[:, :], c0[:, :], c1[:, :], ALU.mult))
            chain(dve.tensor_scalar(val[:, :], beg[:, :], item, -float(ITEM), ALU.subtract, ALU.mult))
            for col, src, op in ((1, off, ALU.add), (2, cnt, ALU.subtract)):
                chain(dve.tensor_tensor(c0[:, :], src[:, :], val[:, :], op))
                chain(dve.tensor_tensor(c0[:, :], c0[:, :], hot[:, :], ALU.mult))
                chain(dve.tensor_reduce(tab_f[:, col:col + 1], c0[:, :], AX.X, ALU.add))
            chain(dve.tensor_tensor(c0[:, :], cst[:, K_EXP:K_EXP + NE], hot[:, :], ALU.mult))
            chain(dve.tensor_reduce(tab_f[:, 0:1], c0[:, :], AX.X, ALU.add))
            chain(dve.tensor_copy(tab_f[:, 3:4], end[:, NE - 1:NE]))
            dve.tensor_copy(tab[:, :], tab_f[:, :]).then_inc(s.tab, 1)


def scatter_phase(nc, m, a):
    zero = m.place("zeros", [P, 2, D], F32, m.R + 72 * 1024)
    with phase(nc, "zeroed", "filled", "scattered") as (block, s):
        @block.vector
        def _(dve):
            dve.memset(zero[:, :, :], 0.0).then_inc(s.zeroed, 1)

        @block.sync
        def _(sp):
            sp.wait_ge(s.zeroed, 1)
            sp.dma_start(a.rows[SLOTS:SLOTS + ITEM, :].rearrange("(t p) n -> p t n", p=P), zero[:, :, :]).then_inc(s.filled, 16)
            sp.wait_ge(s.filled, 16)

        @block.gpsimd
        def _(pool):
            for t in range(ST):
                for q in range(2):
                    pool.indirect_dma_start(a.rows, bass.IndirectOffsetOnAxis(ap=m.slot[:, t, q:q + 1].bitcast(U32), axis=0),
                                            m.hrow[:, t, :], None).then_inc(s.scattered, 16)
            pool.wait_ge(s.scattered, 16 * 2 * ST)


def expert_phase(nc, m, a, l):
    KB = 1024
    R = m.R
    e2 = l // 2
    hid_hi = m.place("e_hid_hi", [P, 2 * NF2, ITEM], F32R, R)
    hid_lo = m.place("e_hid_lo", [P, 2 * NF2, ITEM], F32R, R + 28 * KB)
    xg_hi = m.place("e_x_hi", [P, KT, ITEM], F32R, R + 56 * KB)
    xg_lo = m.place("e_x_lo", [P, KT, ITEM], F32R, R + 64 * KB)
    io = m.place("e_io", [P, 2, D], F32, R + 72 * KB)
    raw13 = [m.place(f"e_raw{q}", [P, KT, P * FGRP], F32, R + (80 + 16 * q) * KB) for q in range(2)]
    raw2 = [m.place(f"e_raw2{b}", [P, 2, D], F32, R + (112 + 8 * b) * KB) for b in range(2)]
    w_hi = [m.place(f"e_w_hi{b}", [P, 2, D], F32R, R + (128 + 8 * b) * KB) for b in range(4)]
    w_lo = [m.place(f"e_w_lo{b}", [P, 2, D], F32R, R + (160 + 8 * b) * KB) for b in range(4)]
    act_t = [m.place(f"e_act{b}", [P, HALF], F32, R + (192 + 2 * b) * KB) for b in range(2)]
    UNITS = 4 * NFG + NF2

    def flat(t):
        return t[:, :, :].rearrange("p k n -> p (k n)")

    def by_k(t):
        return flat(t).rearrange("p (k n) -> p k n", k=KT)

    def half_block(q, h):
        return raw13[q][:, :, 2 * P * h:2 * P * h + 2 * P]

    def field(eng, item, col, hi):
        return eng.value_load(m.items[0:1, ds(4 * item + col, 1)], min_val=0, max_val=hi)

    with phase(nc, "x_in", "raw1", "raw3", "raw2a", "raw2b", "hi_ready", "lo1", "lo3", "lo2", "mm_done", "turned", "x_hi", "x_lo",
               "silu", "hid", "hid_hi", "hid_lo", "y_done", "y_in", "y_stored", "closed") as (block, s):
        raw_sem = (s.raw1, s.raw3)
        raw2_sem = (s.raw2a, s.raw2b)
        lo_sem = (s.lo1, s.lo3)

        @block.sync
        def _(sp):
            def rows_in(item):
                base = field(sp, item, 1, SLOTS)
                sp.dma_start(io[:, :, :], a.rows[ds(base, ITEM), :].rearrange("(t p) n -> p t n", p=P)).then_inc(s.x_in, 16)

            def load13(ex, item, i):
                for q, w in enumerate((a.moe_w1, a.moe_w3)):
                    sp.wait_ge(lo_sem[q], 2 * (NFG * item + i) + 2)
                    sp.dma_start(raw13[q][:, :, :],
                                 w[e2, ds(ex, 1)].rearrange("o (k p) n -> p (o k) n", p=P)[:, :, ds(P * FGRP * i, P * FGRP)]
                                 ).then_inc(raw_sem[q], 16)

            rows_in(0)
            load13(field(sp, 0, 0, NE - 1), 0, 0)
            n_items = field(sp, 0, 3, MAX_ITEMS)
            with sp.Fori(0, MAX_ITEMS) as item:
                with sp.If(item < n_items):
                    ex = field(sp, item, 0, NE - 1)
                    with sp.Fori(1, NFG) as i:
                        load13(ex, item, i)
                    sp.wait_ge(s.turned, item + 1)
                    sp.wait_ge(s.y_stored, 16 * item + 16)
                    rows_in(item + 1)
                    with sp.Fori(0, NF2 // 2) as i:
                        for b in range(2):
                            sp.wait_ge(s.lo2, NF2 * item + 2 * i + b + 1)
                            sp.dma_start(raw2[b][:, :, :],
                                         a.moe_w2[e2, ds(ex, 1)].rearrange("o (g t p) n -> p (o g) t n", p=P, t=2)[:, ds(2 * i + b, 1)]
                                         .rearrange("p g t n -> p (g t) n")).then_inc(raw2_sem[b], 16)
                    load13(field(sp, item + 1, 0, NE - 1), item + 1, 0)
            sp.wait_ge(s.x_in, 16 * n_items + 16)
            sp.wait_ge(s.raw1, 16 * NFG * n_items + 16)
            sp.wait_ge(s.raw3, 16 * NFG * n_items + 16)
            sp.sem_inc(s.closed, 1)

        @block.scalar
        def _(act):
            def unit13(item, i, u, back=4):
                q, h = u % 2, u // 2
                act.wait_ge(raw_sem[q], 16 * (NFG * item + i) + 16)
                act.wait_ge(s.mm_done, UNITS * item + 4 * i + u + 5 - back)
                act.activation(by_k(w_hi[u]), half_block(q, h), ACT.Copy).then_inc(s.hi_ready, 1)

            def unit2(item, i, b):
                act.wait_ge(raw2_sem[b % 2], 16 * (NF2 // 2 * item + 2 * i + b // 2) + 16)
                act.wait_ge(s.mm_done, UNITS * item + 4 * NFG + 4 * i + b + 1)
                act.activation(flat(w_hi[b]), flat(raw2[b % 2]), ACT.Copy).then_inc(s.hi_ready, 1)

            def silu(item, i, h):
                act.wait_ge(s.mm_done, UNITS * item + 4 * i + 2 * h + 5)
                act.wait_ge(s.hid_lo, 2 * (NFG * item + i) + h + 1)
                act.activation(act_t[h][:, :], m.ps[:, h, :], ACT.Silu).then_inc(s.silu, 1)

            def x_round(count):
                act.wait_ge(s.turned, count)
                act.activation(flat(xg_hi), m.ps[:, 0:4, :].rearrange("p a n -> p (a n)"), ACT.Copy).then_inc(s.x_hi, 1)

            act.sem_inc(s.y_stored, 16)
            x_round(1)
            for u in range(4):
                unit13(0, 0, u, back=2 if u < 2 else 4)
            n_items = field(act, 0, 3, MAX_ITEMS)
            with act.Fori(0, MAX_ITEMS) as item:
                with act.If(item < n_items):
                    with act.Fori(0, NFG - 1) as i:
                        for h in range(2):
                            silu(item, i, h)
                            unit13(item, i + 1, 2 * h)
                            unit13(item, i + 1, 2 * h + 1)
                    for h in range(2):
                        silu(item, NFG - 1, h)
                        unit2(item, 0, 2 * h)
                        unit2(item, 0, 2 * h + 1)
                    x_round(item + 2)
                    with act.Fori(1, NF2 // 4) as i:
                        for b in range(4):
                            unit2(item, i, b)
                    for b in range(NF2 % 4):
                        unit2(item, NF2 // 4, b)
                    unit13(item + 1, 0, 0, back=2)
                    unit13(item + 1, 0, 1, back=2)
                    act.wait_ge(s.y_done, item + 1)
                    act.activation(flat(io), m.ps[:, 4:8, :].rearrange("p a n -> p (a n)"), ACT.Copy).then_inc(s.y_in, 1)
                    base = field(act, item, 1, SLOTS)
                    act.wait_ge(s.y_in, item + 2)
                    act.wait_ge(s.y_stored, 16 * item + 16)
                    act.dma_start(a.y_rows[ds(base, ITEM), :].rearrange("(t p) n -> p t n", p=P), io[:, :, :]).then_inc(s.y_stored, 16)
                    unit13(item + 1, 0, 2)
                    unit13(item + 1, 0, 3)
            act.wait_ge(s.y_stored, 16 * n_items + 16)
            act.sem_inc(s.closed, 1)

        def rest13(eng, item, i, u):
            q, h = u % 2, u // 2
            eng.wait_ge(s.hi_ready, UNITS * item + 4 * i + u + 1)
            eng.tensor_tensor(by_k(w_lo[u]), half_block(q, h), by_k(w_hi[u]).bitcast(F32), ALU.subtract).then_inc(lo_sem[q], 1)

        @block.gpsimd
        def _(pool):
            pool.sem_inc(s.lo3, 2)
            for h in range(2):
                rest13(pool, 0, 0, 2 * h + 1)
            n_items = field(pool, 0, 3, MAX_ITEMS)
            with pool.Fori(0, MAX_ITEMS) as item:
                with pool.If(item < n_items):
                    with pool.Fori(1, NFG) as i:
                        for h in range(2):
                            rest13(pool, item, i, 2 * h + 1)
                    for h in range(2):
                        rest13(pool, item + 1, 0, 2 * h + 1)

        @block.tensor
        def _(pe):
            pe.sem_inc(s.mm_done, 4)

            def turn(count, hid_count):
                pe.wait_ge(s.x_in, 16 * count)
                if hid_count is not None:
                    pe.wait_ge(s.hid, hid_count)
                for k in range(KT):
                    for t in range(2):
                        last = pe.transpose(m.ps[:, k // 2, ITEM * (k % 2) + P * t:ITEM * (k % 2) + P * t + P],
                                            io[:, t, P * k:P * k + P], m.const[:, K_ID:K_ID + P])
                last.then_inc(s.turned, 1)

            def up(item, width):
                with pe.Fori(0, NFG) as i:
                    for u in range(4):
                        q, h = u % 2, u // 2
                        if u == 0:
                            pe.wait_ge(s.x_lo, item + 1)
                        if q == 0:
                            pe.wait_ge(s.hid, 2 * (NFG * item + i) + h + 1)
                        pe.wait_ge(lo_sem[q], 2 * (NFG * item + i) + h + 3)
                        hi, lo = by_k(w_hi[u]), by_k(w_lo[u])
                        for f in range(2):
                            for k in range(KT):
                                last = mm3(pe, m.ps[:, 2 * q + h, ITEM * f:ITEM * f + width], hi[:, k, P * f:P * f + P],
                                           lo[:, k, P * f:P * f + P], xg_hi[:, k, 0:width], xg_lo[:, k, 0:width], k == 0, k == KT - 1)
                        last.then_inc(s.mm_done, 1)

            def down(item, width):
                for c in range(NF2):
                    pe.wait_ge(s.lo2, NF2 * item + c + 3)
                    hi, lo = flat(w_hi[c % 4]), flat(w_lo[c % 4])
                    for f in range(2):
                        for t in range(width // P):
                            hh = hid_hi[:, 2 * c + f, P * t:P * t + P]
                            hl = hid_lo[:, 2 * c + f, P * t:P * t + P]
                            for d in range(2):
                                cols = slice(D * f + HALF * d, D * f + HALF * (d + 1))
                                last = mm3(pe, m.ps[:, 4 + 2 * t + d, :], hh, hl, hi[:, cols], lo[:, cols],
                                           c == 0 and f == 0, c == NF2 - 1 and f == 1)
                    last.then_inc(s.mm_done, 1)

            def between(item):
                turn(item + 2, 2 * NFG * item + (2 * NFG + 2))
                pe.wait_ge(s.hid_lo, 2 * NFG * item + (2 * NFG + 2))
                pe.wait_ge(s.y_in, item + 1)

            turn(1, None)
            n_items = field(pe, 0, 3, MAX_ITEMS)
            with pe.Fori(0, MAX_ITEMS) as item:
                with pe.If(item < n_items):
                    left = field(pe, item, 2, S)
                    with pe.If(left < P + 1):
                        up(item, P)
                        between(item)
                        down(item, P)
                    with pe.Else():
                        up(item, ITEM)
                        between(item)
                        down(item, ITEM)
                    pe.drain().then_inc(s.y_done, 1)

        @block.vector
        def _(dve):
            dve.sem_inc(s.lo1, 2)
            dve.sem_inc(s.lo2, 2)
            dve.sem_inc(s.hid, 2)
            dve.sem_inc(s.hid_lo, 2)
            dve.sem_inc(s.y_in, 1)

            def x_rest(count):
                dve.wait_ge(s.x_hi, count)
                dve.tensor_tensor(flat(xg_lo), m.ps[:, 0:4, :].rearrange("p a n -> p (a n)"), flat(xg_hi).bitcast(F32),
                                  ALU.subtract).then_inc(s.x_lo, 1)

            def hidden(item, i, h):
                g = 2 * (NFG * item + i) + h
                dve.wait_ge(s.silu, g + 1)
                dve.wait_ge(s.mm_done, UNITS * item + 4 * i + 2 * h + 6)
                dve.tensor_tensor(act_t[h][:, :], act_t[h][:, :], m.ps[:, 2 + h, :], ALU.mult).then_inc(s.hid, 1)
                dve.wait_ge(s.hid, g + 3)
                src = act_t[h][:, :].rearrange("p (f n) -> p f n", f=2)
                dve.tensor_scalar(hid_hi[:, ds(4 * i + 2 * h, 2), :], src, 1.0, None, ALU.mult).then_inc(s.hid_hi, 1)
                dve.wait_ge(s.hid_hi, g + 1)
                dve.tensor_tensor(hid_lo[:, ds(4 * i + 2 * h, 2), :], src, hid_hi[:, ds(4 * i + 2 * h, 2), :].bitcast(F32),
                                  ALU.subtract).then_inc(s.hid_lo, 1)

            def rest2(item, i, b):
                dve.wait_ge(s.hi_ready, UNITS * item + 4 * NFG + 4 * i + b + 1)
                dve.tensor_tensor(flat(w_lo[b]), flat(raw2[b % 2]), flat(w_hi[b]).bitcast(F32), ALU.subtract).then_inc(s.lo2, 1)

            x_rest(1)
            for h in range(2):
                rest13(dve, 0, 0, 2 * h)
            n_items = field(dve, 0, 3, MAX_ITEMS)
            with dve.Fori(0, MAX_ITEMS) as item:
                with dve.If(item < n_items):
                    with dve.Fori(0, NFG - 1) as i:
                        for h in range(2):
                            hidden(item, i, h)
                            rest13(dve, item, i + 1, 2 * h)
                    for h in range(2):
                        hidden(item, NFG - 1, h)
                        rest2(item, 0, 2 * h)
                        rest2(item, 0, 2 * h + 1)
                    x_rest(item + 2)
                    with dve.Fori(1, NF2 // 4) as i:
                        for b in range(4):
                            rest2(item, i, b)
                    for b in range(NF2 % 4):
                        rest2(item, NF2 // 4, b)
                    for h in range(2):
                        rest13(dve, item + 1, 0, 2 * h)


def combine_phase(nc, m, a, l):
    KB = 1024
    cst = m.const
    R = m.R
    xt = m.place("c_xt", [P, KT, S], F32, R)
    g_row = m.place("c_g_row", [P, D], F32, R + 32 * KB)
    dg = m.place("c_diag", [P, KT, P], F32, R + 36 * KB)
    ya = [m.place(f"c_ya{b}", [P, D], F32, R + (40 + 4 * b) * KB) for b in range(2)]
    yb = [m.place(f"c_yb{b}", [P, D], F32, R + (48 + 4 * b) * KB) for b in range(2)]
    row = [m.place(f"c_row{b}", [P, D], F32, R + (56 + 4 * b) * KB) for b in range(2)]
    G2 = S_ADA + 48 * l + 40
    with phase(nc, "x_in", "diag", "spread", "g_in", "ga0", "ga1", "gb0", "gb1", "scaled", "mixed", "gated", "turned", "summed",
               "st0", "st1") as (block, s):
        @block.sync
        def _(sp):
            sp.dma_start(xt[:, :, :], a.xs.rearrange("(k p) n -> p k n", p=P)).then_inc(s.x_in, 16)
            for t in range(ST):
                sp.wait_ge(s.summed, t + 1)
                sp.dma_start(a.out[0, P * t:P * (t + 1), :], row[t % 2][:, :]).then_inc((s.st0, s.st1)[t % 2], 16)
            sp.wait_ge(s.st0, 16 * ST // 2)
            sp.wait_ge(s.st1, 16 * ST // 2)

        @block.gpsimd
        def _(pool):
            for t in range(ST):
                b = t % 2
                if t >= 2:
                    pool.wait_ge(s.mixed, t - 1)
                for q, (dst, sem) in enumerate(((ya[b], (s.ga0, s.ga1)[b]), (yb[b], (s.gb0, s.gb1)[b]))):
                    pool.indirect_dma_start(dst[:, :], None, a.y_rows[0:SLOTS, :],
                                            bass.IndirectOffsetOnAxis(ap=m.slot[:, t, q:q + 1].bitcast(U32), axis=0)).then_inc(sem, 16)

        @block.scalar
        def _(act):
            for t in range(ST):
                b = t % 2
                act.wait_ge((s.ga0, s.ga1)[b], 16 * (t // 2) + 16)
                act.activation(ya[b][:, :], ya[b][:, :], ACT.Copy, scale=m.top_w[:, t, 0:1]).then_inc(s.scaled, 1)

        @block.tensor
        def _(pe):
            pe.wait_ge(s.diag, KT)
            for k in range(KT):
                last = pe.matmul(m.ps[:, k // 4, P * (k % 4):P * (k % 4 + 1)], cst[:, K_ONE:K_ONE + P], dg[:, k, :], start=True, stop=True)
            last.then_inc(s.spread, 1)
            pe.wait_ge(s.g_in, 1)
            pe.wait_ge(s.x_in, 16)
            for t in range(ST):
                if t >= 2:
                    pe.wait_ge(s.summed, t - 1)
                for k in range(KT):
                    last = pe.transpose(m.ps[:, 2 * (t % 2) + k // 4, P * (k % 4):P * (k % 4 + 1)],
                                        xt[:, k, P * t:P * (t + 1)], cst[:, K_ID:K_ID + P])
                last.then_inc(s.turned, 1)

        @block.vector
        def _(dve):
            for k in range(KT):
                dve.tensor_scalar(dg[:, k, :], cst[:, K_ID:K_ID + P], m.small[:, G2 + k:G2 + k + 1], None, ALU.mult).then_inc(s.diag, 1)
            dve.wait_ge(s.spread, 1)
            dve.tensor_copy(g_row[:, :], m.ps[:, 0:2, :].rearrange("p a n -> p (a n)")).then_inc(s.g_in, 1)
            dve.wait_ge(s.g_in, 1)
            for t in range(ST):
                b = t % 2
                dve.wait_ge(s.scaled, t + 1)
                dve.wait_ge((s.gb0, s.gb1)[b], 16 * (t // 2) + 16)
                if t >= 2:
                    dve.wait_ge((s.st0, s.st1)[b], 16 * (t // 2))
                dve.scalar_tensor_tensor(out=row[b][:, :], in0=yb[b][:, :], scalar=m.top_w[:, t, 1:2], in1=ya[b][:, :],
                                         op0=ALU.mult, op1=ALU.add).then_inc(s.mixed, 1)
                dve.wait_ge(s.mixed, t + 1)
                dve.tensor_tensor(row[b][:, :], row[b][:, :], g_row[:, :], ALU.mult).then_inc(s.gated, 1)
                dve.wait_ge(s.gated, t + 1)
                dve.wait_ge(s.turned, t + 1)
                dve.tensor_tensor(row[b][:, :], row[b][:, :], m.ps[:, 2 * b:2 * b + 2, :].rearrange("p a n -> p (a n)"),
                                  ALU.add).then_inc(s.summed, 1)


def final_phase(nc, m, a):
    xt = m.place("o_xt", [P, KT, S], F32, m.R)
    row = m.place("o_row", [P, 2, 2, HALF], F32, m.R + 32 * 1024)
    with phase(nc, "x_in", "turned", "copied", "stored0", "stored1") as (block, s):
        @block.sync
        def _(sp):
            sp.dma_start(xt[:, :, :], a.xs.rearrange("(k p) n -> p k n", p=P)).then_inc(s.x_in, 16)
            for t in range(ST):
                sp.wait_ge(s.copied, t + 1)
                sp.dma_start(a.out[0, P * t:P * (t + 1), :], row[:, t % 2]).then_inc((s.stored0, s.stored1)[t % 2], 16)
            sp.wait_ge(s.stored0, 16 * ST // 2)
            sp.wait_ge(s.stored1, 16 * ST // 2)

        @block.tensor
        def _(pe):
            pe.wait_ge(s.x_in, 16)
            for t in range(ST):
                if t >= 2:
                    pe.wait_ge(s.copied, t - 1)
                for k in range(KT):
                    last = pe.transpose(m.ps[:, 2 * (t % 2) + k // 4, P * (k % 4):P * (k % 4 + 1)],
                                        xt[:, k, P * t:P * (t + 1)], m.const[:, K_ID:K_ID + P])
                last.then_inc(s.turned, 1)

        @block.vector
        def _(dve):
            for t in range(ST):
                dve.wait_ge(s.turned, t + 1)
                if t >= 2:
                    dve.wait_ge((s.stored0, s.stored1)[t % 2], 16 * (t // 2))
                dve.tensor_copy(row[:, t % 2], m.ps[:, 2 * (t % 2):2 * (t % 2) + 2, :]).then_inc(s.copied, 1)


def build(nc, a, stop=None):
    with ExitStack() as stack:
        m = Memory(nc, stack)
        setup_phases(nc, m, a)
        ada_phase(nc, m, a)
        for l in range(DEPTH):
            param_phase(nc, m, a, l)
            norm_phase(nc, m, a, l, 0, load=True, split=True)
            project_phase(nc, m, a, l, C_B, 10, tail_col=C_KR + QKR - P)
            conv_phase(nc, m, l)
            lora_norm_phase(nc, m, l)
            qk = qk_phases(nc, m, l)
            attention_phase(nc, m, l, qk)
            project_phase(nc, m, a, l, C_SU, 12)
            sgu_phases(nc, m, l)
            retention_phases(nc, m, l)
            merged = gate_phase(nc, m, a, l)
            out_proj_phase(nc, m, a, l, merged)
            if stop == f"mix{l}":
                break
            if l % 2 == 0:
                norm_phase(nc, m, a, l, 1, load=False, split=True)
                ffn_phases(nc, m, a, l)
            else:
                moe_memory(m)
                norm_phase(nc, m, a, l, 1, load=False, split=False)
                route_phase(nc, m, a, l)
                scatter_phase(nc, m, a)
                expert_phase(nc, m, a, l)
                combine_phase(nc, m, a, l)
                return
            if stop == f"ffn{l}":
                break
        final_phase(nc, m, a)


_INS = ["x", "positions", "ada_w", "w_in", "w_uq", "w_ukv", "w_s", "b_s", "w_branch", "w_o", "ffn_w1", "ffn_w3", "ffn_w2", "router_w",
        "router_b", "moe_w1", "moe_w3", "moe_w2"]
STOP = None


def kernel(**inputs):
    import concourse.bacc as _bacc
    from concourse.bass_utils import run_bass_kernel_spmd as _run

    nc = _bacc.Bacc("TRN2", target_bir_lowering=False, num_devices=1)
    arrays, args = {}, {}
    for name in _INS:
        v = np.ascontiguousarray(inputs[name])
        arrays[f"in_{name}_dram"] = v
        args[name] = nc.dram_tensor(f"in_{name}_dram", v.shape, mybir.dt.from_np(v.dtype), kind="ExternalInput").ap()
    arrays["in_vectors_dram"] = pack_vectors({k: np.asarray(v) for k, v in inputs.items()})
    args["vectors"] = nc.dram_tensor("in_vectors_dram", (P, KT + DEPTH * V_N), F32, kind="ExternalInput").ap()
    arrays["in_const_dram"] = constants()
    args["const"] = nc.dram_tensor("in_const_dram", (P, K_N), F32, kind="ExternalInput").ap()
    args["out"] = nc.dram_tensor("out_0_dram", (1, S, D), F32, kind="ExternalOutput").ap()
    args["xs"] = nc.dram_tensor("x_scratch", (D, S), F32, kind="Internal").ap()
    args["rows"] = nc.dram_tensor("row_scratch", (SLOTS + ITEM, D), F32, kind="Internal").ap()
    args["y_rows"] = nc.dram_tensor("y_scratch", (SLOTS + ITEM, D), F32, kind="Internal").ap()
    args["items"] = nc.dram_tensor("item_scratch", (MAX_ITEMS + 1, 4), I32, kind="Internal").ap()
    args["tables"] = nc.dram_tensor("table_scratch", (P, 4, S), F32, kind="Internal").ap()
    build(nc, namedtuple("Arrays", list(args))(**args), STOP)
    r = _run(nc, [arrays], core_ids=[0])
    return r.results[0]["out_0_dram"]
```

```python
from collections import namedtuple
from contextlib import ExitStack, contextmanager

import numpy as np
import concourse.bass as bass
from concourse import mybir

F32 = mybir.dt.float32
F32R = mybir.dt.float32r
I32 = mybir.dt.int32
U32 = mybir.dt.uint32
ACT = mybir.ActivationFunctionType
ALU = mybir.AluOpType
AX = mybir.AxisListType
ds = bass.ds

P = 128
D = 1024
S = 1024
DEPTH = 2
KT = D // P
HALF = 512
NHALF = S // HALF
ST = S // P
HD = 64
NG = 4
MIX = NG * HD
NBR = 4
QL = 256
QKN = 64
QKR = 32
QK = QKN + QKR
FF = 2816
FT = FF // P
NE = 8
FE = 3584
EPS = 1e-6
BIG = 1e30
TWO_PI = 2.0 * np.pi

C_B, C_C, C_X, C_CQ, C_CKV, C_KR = 0, 256, 512, 768, 1024, 1152
C_SU, C_SV, C_RQ, C_RK, C_RV, C_RG, C_GATE = 1184, 1440, 1696, 1952, 2208, 2464, 2720

(K_ID, K_ONE, K_BLK, K_PRET, K_PMLA, K_NEG, K_TRI, K_LOW) = [P * i for i in range(8)]
K_DEC = 8 * P
K_KDEC = K_DEC + NG * P
K_QDEC = K_KDEC + MIX
K_CD = K_QDEC + 2 * P
K_FRET = K_CD + 2
K_FMLA = K_FRET + 1
K_ITEM = K_FMLA + 1
K_EXP = K_ITEM + 1
K_EPS = K_EXP + NE
K_N = K_EPS + 1


def constants():
    f = np.float32
    c = np.zeros((P, K_N), f)
    i = np.arange(P)
    c[:, K_ID:K_ID + P] = np.eye(P)
    c[:, K_ONE:K_ONE + P] = 1.0
    c[:, K_BLK:K_BLK + P] = i[:, None] // HD == i[None, :] // HD

    def swap(first, half, col):
        for j in range(half):
            c[first + half + j, col + first + j] = -1.0
            c[first + j, col + first + half + j] = 1.0

    swap(0, HD // 2, K_PRET)
    swap(HD, HD // 2, K_PRET)
    swap(QKN, QKR // 2, K_PMLA)
    c[:, K_NEG:K_NEG + P] = np.where(i[None, :] > i[:, None], -BIG, 0.0)
    c[:, K_TRI:K_TRI + P] = i[:, None] <= i[None, :]
    c[:, K_LOW:K_LOW + P] = i[:, None] < i[None, :]
    lg = np.log1p(-(2.0 ** (-5.0 - np.arange(NG)))).astype(f).astype(np.float64)
    for h in range(NG):
        rel = i[None, :] - i[:, None]
        slot = 2 * (h % 2) + h // 2
        c[:, K_DEC + P * slot:K_DEC + P * slot + P] = np.where(rel >= 0, np.exp(lg[h] * np.maximum(rel, 0)), 0) * HD ** -0.5
        c[:, K_KDEC + HD * h:K_KDEC + HD * h + HD] = (np.exp(lg[h] * (P - 1 - i)) * HD ** -0.5)[:, None]
        rows = slice(HD * (h % 2), HD * (h % 2) + HD)
        c[rows, K_QDEC + P * (h // 2):K_QDEC + P * (h // 2) + P] = np.exp(lg[h] * (i + 1.0))[None, :]
        c[rows, K_CD + h // 2] = np.exp(lg[h] * P)

    def freq(half):
        return (f(10000.0) ** (-np.arange(half, dtype=f) / f(half))).astype(f)

    c[:, K_FRET] = np.tile(freq(HD // 2), P // (HD // 2))
    c[:, K_FMLA] = np.tile(freq(QKR // 2), P // (QKR // 2))
    c[:, K_ITEM] = i
    c[:, K_EXP:K_EXP + NE] = np.arange(NE)
    c[:, K_EPS] = EPS
    return c


SEM0 = 104
SW_DMA = ("scattered", "ga0", "ga1", "gb0", "gb1")
SEM_SW = 160


@contextmanager
def phase(nc, *names):
    with ExitStack() as stack:
        sems = {n: stack.enter_context(nc.semaphore(n, num=SEM_SW + SW_DMA.index(n) if n in SW_DMA else SEM0 + i))
                for i, n in enumerate(names)}
        with nc.Block() as block:
            yield block, namedtuple("Semaphores", names)(**sems)
        nc.all_engine_barrier(sems_to_clear=range(SEM0, SEM0 + len(names)))


def looped(eng, n, body):
    if n > 1:
        with eng.Fori(0, n - 1) as i:
            body(i, False)
    body(n - 1, True)


def two_pi_parts():
    rest, parts = TWO_PI, []
    for bits in (8, 8, 8):
        e = int(np.floor(np.log2(rest)))
        q = 2.0 ** (e - bits + 1)
        v = float(np.floor(rest / q) * q)
        parts.append(v)
        rest -= v
    return parts + [float(np.float32(rest))]


class Memory:

    def __init__(self, nc, stack):
        self.nc = nc
        self.base = (nc.sbuf_base + 63) // 64 * 64
        self.end = nc.sbuf_usable_end
        self.at = {}
        ps = stack.enter_context(nc.psum_tensor("banks", [P, 8, HALF], F32))
        self.ps = ps
        KB = 1024
        o = 0
        self.const = self.place("const", [P, K_N], F32, o)
        o += 9 * KB
        self.small = self.place("small", [P, S_END], F32, o)
        o += KB + KB // 2
        R = o
        self.R = R
        self.h_hi = self.place("h_hi", [P, KT, S], F32R, R)
        self.h_lo = self.place("h_lo", [P, KT, S], F32R, R + 32 * KB)
        self.h_f = self.place("h_f", [P, KT, S], F32, R)
        self.w_raw = [self.place(f"w_raw{b}", [P, KT, P], F32, R + (64 + 4 * b) * KB) for b in range(2)]
        self.w_hi = [self.place(f"w_hi{b}", [P, KT, P], F32R, R + (72 + 4 * b) * KB) for b in range(2)]
        self.w_lo = [self.place(f"w_lo{b}", [P, KT, P], F32R, R + (80 + 4 * b) * KB) for b in range(2)]
        self.W0 = R + 64 * KB
        self.table = self.place("rope_tables", [P, 4, S], F32, R + 88 * KB)
        self.ys = self.place("ys", [P, 2 * NBR, S], F32, R + 104 * KB)
        self.YS4 = R + 120 * KB
        self.x = self.place("x_res", [P, KT, S], F32, R + 104 * KB)
        LP = R + 136 * KB
        self.w_uq = self.place("w_uq_sb", [P, QL // P, NG * QK], F32, LP)
        self.w_ukv = self.place("w_ukv_sb", [P, NG * (QKN + HD)], F32, LP + 3 * KB)
        self.bs = self.place("bs_sb", [P, 2, P], F32, LP + 5 * KB)
        self.ws_t = self.place("ws_t", [P, NG, P], F32, LP + 6 * KB)
        self.Z0 = R + 146 * KB
        self.z = self.place("z", [P, 12, 2, HALF], F32, self.Z0)
        self.top = R + 194 * KB

    def place(self, name, shape, dt, offset):
        return self.nc.alloc_sbuf_tensor_at(name, shape, dt, offset=self.base + offset)


S_ADA = 0
S_A = S_ADA + DEPTH * 6 * KT
S_COND = S_A + DEPTH * 2 * KT
S_VEC = S_COND + KT
(V_BIAS, V_NORM, V_CW, V_CQ, V_CKV, V_QN, V_KN, V_GV, V_RET, V_N) = (0, 48, 64, 70, 72, 73, 74, 75, 77, 79)
S_END = S_VEC + DEPTH * V_N


def pack_vectors(inp):
    def cols(v):
        return v.reshape(-1, P).T

    def padded(v):
        return np.concatenate([v, np.zeros(P - len(v), v.dtype)])[:, None]

    parts = [cols(inp["c"])]
    for l in range(DEPTH):
        parts += [cols(inp["ada_b"][l]), cols(inp["norm1_g"][l]), cols(inp["norm2_g"][l]), cols(inp["conv_w"][l]),
                  cols(inp["cq_g"][l]), cols(inp["ckv_g"][l]), padded(inp["qn_g"][l]), padded(inp["kn_g"][l]),
                  cols(inp["gv_g"][l]), cols(inp["ret_g"][l])]
    return np.ascontiguousarray(np.concatenate(parts, axis=1))



def credit_pool(pool, s):
    pool.sem_inc(s.lo_ready, 2)


def credit_pe(pe, s):
    pe.sem_inc(s.mm_done, 2)


def w_load(sp, s, m, j, b, src, kt=KT):
    sp.wait_ge(s.lo_ready, j + 1)
    sp.dma_start(m.w_raw[b][:, 0:kt, :], src).then_inc((s.raw0, s.raw1)[b], 16)


def w_round(act, s, m, j, r, b, kt=KT):
    act.wait_ge((s.raw0, s.raw1)[b], 16 * r + 16)
    act.wait_ge(s.mm_done, j + 1)
    act.activation(m.w_hi[b][:, 0:kt, :], m.w_raw[b][:, 0:kt, :], ACT.Copy).then_inc(s.hi_ready, 1)


def w_rest(pool, s, m, j, b, kt=KT):
    pool.wait_ge(s.hi_ready, j + 1)
    pool.tensor_tensor(m.w_lo[b][:, 0:kt, :], m.w_raw[b][:, 0:kt, :], m.w_hi[b][:, 0:kt, :].bitcast(F32),
                       ALU.subtract).then_inc(s.lo_ready, 1)


def mm3(pe, out, wh, wl, rh, rl, first, last):
    pe.matmul(out, wh, rh, start=first, stop=False)
    pe.matmul(out, wh, rl, start=False, stop=False)
    return pe.matmul(out, wl, rh, start=False, stop=last)


def h_block(pe, m, b, bank, split=None):
    for half in range(NHALF):
        tok = slice(half * HALF, (half + 1) * HALF)
        for k in range(KT):
            if split is not None and half == 0:
                pe.wait_ge(split, k + 1)
            last = mm3(pe, m.ps[:, bank + half, :], m.w_hi[b][:, k, :], m.w_lo[b][:, k, :],
                       m.h_hi[:, k, tok], m.h_lo[:, k, tok], k == 0, k == KT - 1)
    return last


def w_view(w2d, col, n=P):
    return w2d.rearrange("(k p) n -> p k n", p=P)[:, :, ds(col, n)]


def opening_phase(nc, m, a):
    KB = 1024
    cst = m.const
    GRP = 6
    W = P * GRP
    NB = 6 * D // W
    xrow = m.place("x_rows", [P, ST, D], F32, m.R)
    xt = m.place("x_turned", [P, 2, 2, HALF], F32, m.R + 32 * KB)
    pos_i = m.place("pos_i", [P, S], I32, m.R + 48 * KB)
    pos_f, ang, cnt, red, wrap = (m.place(n, [P, S], F32, m.R + (52 + 4 * i) * KB)
                                  for i, n in enumerate(("pos_f", "ang", "cnt", "red", "wrap")))
    part_sum = [m.place(f"ada_part{b}", [P, W], F32, m.R + (72 + 3 * b) * KB) for b in range(2)]
    wb = [m.place(f"ada_w{b}", [P, KT, W], F32, m.R + (104 + 24 * b) * KB) for b in range(3)]
    two_pi = two_pi_parts()
    edge = 3.1415925
    with phase(nc, "c_in", "p_in", "x_in", "w0", "w1", "w2", "turned", "copied", "stored0", "stored1", "saved", "step", "reduced",
               "used", "silu", "scaled", "added", "summed", "folded") as (block, s):
        w_in = (s.w0, s.w1, s.w2)

        @block.sync
        def _(sp):
            sp.dma_start(m.small[:, S_COND:S_END], a.vectors).then_inc(s.c_in, 16)
            sp.dma_start(pos_i[:, :], a.positions.rearrange("o s -> (o s)").partition_broadcast(P)).then_inc(s.p_in, 16)
            sp.dma_start(cst[:, :], a.const).then_inc(s.c_in, 16)
            sp.dma_start(xrow[:, :, :], a.x.rearrange("o (t p) d -> p (o t) d", p=P)).then_inc(s.x_in, 16)
            for j in range(DEPTH * NB):
                if j >= 3:
                    sp.wait_ge(s.added, j - 2)
                sp.dma_start(wb[j % 3][:, :, :], w_view(a.ada_w[j // NB], (j % NB) * W, W)).then_inc(w_in[j % 3], 16)

        @block.tensor
        def _(pe):
            pe.wait_ge(s.c_in, 32)
            pe.wait_ge(s.x_in, 16)
            for k in range(KT):
                if k >= 2:
                    pe.wait_ge(s.copied, k - 1)
                for t in range(ST):
                    last = pe.transpose(m.ps[:, 2 * (k % 2) + t // 4, P * (t % 4):P * (t % 4 + 1)],
                                        xrow[:, t, P * k:P * (k + 1)], cst[:, K_ID:K_ID + P])
                last.then_inc(s.turned, 1)
            for j in range(DEPTH * NB):
                pe.wait_ge(s.added, j + 1)
                for i in range(GRP):
                    last = pe.matmul(m.ps[:, 7, j * GRP + i:j * GRP + i + 1], part_sum[j % 2][:, P * i:P * i + P],
                                     cst[:, K_ONE:K_ONE + 1], start=True, stop=True)
                last.then_inc(s.summed, 1)

        @block.vector
        def _(dve):
            n = 0

            def chain(ins):
                nonlocal n
                n += 1
                ins.then_inc(s.step, 1)
                dve.wait_ge(s.step, n)

            dve.wait_ge(s.p_in, 16)
            dve.wait_ge(s.c_in, 32)
            chain(dve.tensor_copy(pos_f[:, :], pos_i[:, :]))
            for t, col in enumerate((K_FRET, K_FMLA)):
                if t:
                    dve.wait_ge(s.used, 2)
                chain(dve.tensor_scalar(ang[:, :], pos_f[:, :], cst[:, col:col + 1], None, ALU.mult))
                chain(dve.tensor_scalar(cnt[:, :], ang[:, :], float(np.float32(1.0 / TWO_PI)), None, ALU.mult))
                chain(dve.tensor_scalar(cnt[:, :], cnt[:, :], 12582912.0, None, ALU.add))
                chain(dve.tensor_scalar(cnt[:, :], cnt[:, :], -12582912.0, None, ALU.add))
                for part in two_pi:
                    chain(dve.scalar_tensor_tensor(out=ang[:, :], in0=cnt[:, :], scalar=-part, in1=ang[:, :],
                                                   op0=ALU.mult, op1=ALU.add))
                dve.tensor_scalar(red[:, :], ang[:, :], edge, -edge, ALU.min, ALU.max).then_inc(s.reduced, 1)
                chain(dve.tensor_scalar(ang[:, :], ang[:, :], float(np.pi / 2), None, ALU.add))
                chain(dve.tensor_scalar(wrap[:, :], ang[:, :], edge, -float(TWO_PI), ALU.is_gt, ALU.mult))
                chain(dve.tensor_tensor(ang[:, :], ang[:, :], wrap[:, :], ALU.add))
                dve.tensor_scalar(wrap[:, :], ang[:, :], edge, -edge, ALU.min, ALU.max).then_inc(s.reduced, 1)

            dve.wait_ge(s.silu, 1)
            for j in range(DEPTH * NB):
                w, acc = wb[j % 3], part_sum[j % 2][:, :]
                dve.wait_ge(w_in[j % 3], 16 * (j // 3) + 16)
                if j >= 2:
                    dve.wait_ge(s.summed, j - 1)
                dve.tensor_scalar(acc, w[:, 0, :], m.small[:, S_COND:S_COND + 1], None, ALU.mult).then_inc(s.scaled, 1)
                for k in range(1, KT):
                    dve.wait_ge(s.scaled, (KT - 1) * j + k)
                    dve.scalar_tensor_tensor(out=acc, in0=w[:, k, :], scalar=m.small[:, S_COND + k:S_COND + k + 1], in1=acc,
                                             op0=ALU.mult, op1=ALU.add).then_inc(s.scaled if k < KT - 1 else s.added, 1)
            dve.wait_ge(s.summed, DEPTH * NB)
            for l in range(DEPTH):
                v = S_VEC + V_N * l + V_BIAS
                dve.tensor_tensor(m.small[:, S_ADA + 48 * l:S_ADA + 48 * l + 48], m.ps[:, 7, 48 * l:48 * l + 48],
                                  m.small[:, v:v + 48], ALU.add).then_inc(s.folded, 1)
            dve.wait_ge(s.folded, DEPTH)
            for l in range(DEPTH):
                for q in range(2):
                    sc = S_ADA + 48 * l + 8 * (3 * q + 1)
                    i = 8 * (2 * l + q)
                    g = S_VEC + V_N * l + V_NORM + 8 * q
                    dve.scalar_tensor_tensor(out=m.small[:, S_A + i:S_A + i + 8], in0=m.small[:, sc:sc + 8], scalar=1.0,
                                             in1=m.small[:, g:g + 8], op0=ALU.add, op1=ALU.mult).then_inc(s.folded, 1)

        @block.scalar
        def _(act):
            act.wait_ge(s.c_in, 32)
            act.activation(m.small[:, S_COND:S_COND + KT], m.small[:, S_COND:S_COND + KT], ACT.Silu).then_inc(s.silu, 1)
            for t in range(2):
                act.wait_ge(s.reduced, 2 * t + 1)
                act.activation(m.table[:, 2 * t + 1, :], red[:, :], ACT.Sin).then_inc(s.used, 1)
                act.wait_ge(s.reduced, 2 * t + 2)
                act.activation(m.table[:, 2 * t, :], wrap[:, :], ACT.Sin).then_inc(s.used, 1)
            act.wait_ge(s.used, 4)
            act.dma_start(a.tables, m.table[:, :, :]).then_inc(s.saved, 16)
            for k in range(KT):
                act.wait_ge(s.turned, k + 1)
                if k >= 2:
                    act.wait_ge((s.stored0, s.stored1)[k % 2], 16 * (k // 2))
                act.activation(xt[:, k % 2], m.ps[:, 2 * (k % 2):2 * (k % 2) + 2, :], ACT.Copy).then_inc(s.copied, 1)
                act.wait_ge(s.copied, k + 1)
                act.dma_start(a.xs[P * k:P * (k + 1), :], xt[:, k % 2]).then_inc((s.stored0, s.stored1)[k % 2], 16)
            act.wait_ge(s.saved, 16)
            act.wait_ge(s.stored0, 16 * KT // 2)
            act.wait_ge(s.stored1, 16 * KT // 2)


def param_phase(nc, m, a, l):
    ws = m.place(f"ws_nat{l}", [P, NG, P], F32, m.W0)
    cst = m.const
    with phase(nc, "p_in", "ws_in", "turned", "masked") as (block, s):
        @block.sync
        def _(sp):
            sp.dma_start(ws[:, :, :], a.w_s[l].rearrange("g t s -> t g s")).then_inc(s.ws_in, 16)
            sp.dma_start(m.w_uq[:, :, :], a.w_uq[l].rearrange("(k p) n -> p k n", p=P)).then_inc(s.p_in, 16)
            sp.dma_start(m.w_ukv[:, :], a.w_ukv[l]).then_inc(s.p_in, 16)
            if l:
                sp.dma_start(m.table[:, :, :], a.tables).then_inc(s.p_in, 16)
            for h in range(NG):
                sp.dma_start(m.bs[HD * (h % 2):HD * (h % 2) + HD, h // 2, :], a.b_s[l, h].partition_broadcast(HD)).then_inc(s.p_in, 16)
            sp.wait_ge(s.p_in, 16 * (6 + (l > 0)))

        @block.tensor
        def _(pe):
            pe.wait_ge(s.ws_in, 16)
            for g in range(NG):
                last = pe.transpose(m.ps[:, 0, P * g:P * g + P], ws[:, g, :], cst[:, K_ID:K_ID + P])
            last.then_inc(s.turned, 1)

        @block.vector
        def _(dve):
            dve.wait_ge(s.turned, 1)
            for g in range(NG):
                dve.tensor_tensor(m.ws_t[:, g, :], m.ps[:, 0, P * g:P * g + P], cst[:, K_TRI:K_TRI + P], ALU.mult).then_inc(s.masked, 1)


def norm_phase(nc, m, l, split):
    cst = m.const
    sq = [m.place(f"n_sq{l}{b}", [P, S], F32, m.Z0 + 4096 * b) for b in range(2)]
    rstd = m.place(f"n_rstd{l}", [P, 2, HALF], F32, m.Z0 + 8192)
    tmp = [m.place(f"n_tmp{l}{b}", [P, S], F32, m.Z0 + 12288 + 4096 * b) for b in range(3)]
    A = S_A + 8 * (2 * l + 1)
    B = S_ADA + 48 * l + 24
    with phase(nc, "squared", "summed", "root", "inv", "scaled", "hi", "lo") as (block, s):
        @block.scalar
        def _(act):
            for k in range(KT):
                if k >= 2:
                    act.wait_ge(s.summed, k - 1)
                act.activation(sq[k % 2][:, :], m.x[:, k, :], ACT.Square).then_inc(s.squared, 1)
            act.wait_ge(s.summed, KT)
            act.activation(rstd[:, :, :], m.ps[:, 0:2, :], ACT.Sqrt, bias=cst[:, K_EPS:K_EPS + 1], scale=1.0 / D).then_inc(s.root, 1)
            for k in range(KT):
                act.wait_ge(s.scaled, k + 1)
                dst = m.h_hi[:, k, :] if split else m.h_f[:, k, :]
                act.activation(dst, tmp[k % 3][:, :], ACT.Identity, bias=m.small[:, B + k:B + k + 1]).then_inc(s.hi, 1)

        @block.tensor
        def _(pe):
            for k in range(KT):
                pe.wait_ge(s.squared, k + 1)
                for half in range(NHALF):
                    last = pe.matmul(m.ps[:, half, :], cst[:, K_ONE:K_ONE + P], sq[k % 2][:, half * HALF:(half + 1) * HALF],
                                     start=(k == 0), stop=(k == KT - 1))
                last.then_inc(s.summed, 1)

        @block.vector
        def _(dve):
            def rest(k):
                dve.wait_ge(s.hi, k + 1)
                dve.scalar_tensor_tensor(out=m.h_lo[:, k, :], in0=tmp[k % 3][:, :], scalar=m.small[:, B + k:B + k + 1],
                                         in1=m.h_hi[:, k, :].bitcast(F32), op0=ALU.add, op1=ALU.subtract).then_inc(s.lo, 1)

            dve.wait_ge(s.root, 1)
            dve.reciprocal(rstd[:, :, :], rstd[:, :, :]).then_inc(s.inv, 1)
            dve.wait_ge(s.inv, 1)
            for k in range(KT):
                if k >= 3:
                    dve.wait_ge(s.hi, k - 2)
                    if split:
                        dve.wait_ge(s.lo, k - 2)
                dve.scalar_tensor_tensor(out=tmp[k % 3][:, :], in0=m.x[:, k, :], scalar=m.small[:, A + k:A + k + 1],
                                         in1=rstd[:, :, :].rearrange("p a b -> p (a b)"), op0=ALU.mult, op1=ALU.mult
                                         ).then_inc(s.scaled, 1)
                if split and k:
                    rest(k - 1)
            if split:
                rest(KT - 1)


def norm_project_phase(nc, m, a, l, col, nblocks, tail_col):
    cst = m.const
    T = m.Z0 + 24 * 1024
    sq = [m.place(f"np_sq{l}{b}", [P, S], F32, T + 4096 * b) for b in range(2)]
    rstd = m.place(f"np_rstd{l}", [P, 2, HALF], F32, T + 8192)
    tmp = [m.place(f"np_tmp{l}{b}", [P, S], F32, T + 12288 + 4096 * b) for b in range(3)]
    A = S_A + 16 * l
    B = S_ADA + 48 * l
    w = a.w_in[l]
    n2 = nblocks // 2
    with phase(nc, "x0", "x1", "x2", "x3", "squared", "summed", "root", "inv", "scaled", "hi", "lo",
               "raw0", "raw1", "hi_ready", "lo_ready", "mm_done", "copied") as (block, s):
        x_in = (s.x0, s.x1, s.x2, s.x3)

        @block.sync
        def _(sp):
            for k in range(KT):
                if k >= 4:
                    sp.wait_ge(x_in[k % 4], 16)
                sp.dma_start(m.x[:, k, :], a.xs[P * k:P * k + P, :]).then_inc(x_in[k % 4], 16)

            def step(i, last):
                for b in range(2):
                    c = tail_col if last and b else col + P * (2 * i + b)
                    w_load(sp, s, m, 2 * i + b, b, w_view(w, c))
            looped(sp, n2, step)

        @block.scalar
        def _(act):
            for k in range(KT):
                act.wait_ge(x_in[k % 4], 16 * (k // 4) + 16)
                if k >= 2:
                    act.wait_ge(s.summed, k - 1)
                act.activation(sq[k % 2][:, :], m.x[:, k, :], ACT.Square).then_inc(s.squared, 1)
            for b in range(2):
                w_round(act, s, m, b, 0, b)
            act.wait_ge(s.summed, KT)
            act.activation(rstd[:, :, :], m.ps[:, 0:2, :], ACT.Sqrt, bias=cst[:, K_EPS:K_EPS + 1], scale=1.0 / D).then_inc(s.root, 1)
            for k in range(KT):
                act.wait_ge(s.scaled, k + 1)
                act.activation(m.h_hi[:, k, :], tmp[k % 3][:, :], ACT.Identity, bias=m.small[:, B + k:B + k + 1]).then_inc(s.hi, 1)
            with act.Fori(1, n2) as i:
                for b in range(2):
                    w_round(act, s, m, 2 * i + b, i, b)

        @block.gpsimd
        def _(pool):
            credit_pool(pool, s)
            with pool.Fori(0, n2) as i:
                for b in range(2):
                    w_rest(pool, s, m, 2 * i + b, b)

        @block.tensor
        def _(pe):
            credit_pe(pe, s)
            for k in range(KT):
                pe.wait_ge(s.squared, k + 1)
                for half in range(NHALF):
                    last = pe.matmul(m.ps[:, half, :], cst[:, K_ONE:K_ONE + P], sq[k % 2][:, half * HALF:(half + 1) * HALF],
                                     start=(k == 0), stop=(k == KT - 1))
                last.then_inc(s.summed, 1)
            for b in range(2):
                pe.wait_ge(s.lo_ready, b + 3)
                h_block(pe, m, b, 2 * b, s.lo if b == 0 else None).then_inc(s.mm_done, 1)
            with pe.Fori(1, n2) as i:
                for b in range(2):
                    pe.wait_ge(s.lo_ready, 2 * i + b + 3)
                    pe.wait_ge(s.copied, 2 * i + b - 1)
                    h_block(pe, m, b, 2 * b).then_inc(s.mm_done, 1)

        @block.vector
        def _(dve):
            def rest(k):
                dve.wait_ge(s.hi, k + 1)
                dve.scalar_tensor_tensor(out=m.h_lo[:, k, :], in0=tmp[k % 3][:, :], scalar=m.small[:, B + k:B + k + 1],
                                         in1=m.h_hi[:, k, :].bitcast(F32), op0=ALU.add, op1=ALU.subtract).then_inc(s.lo, 1)

            dve.wait_ge(s.root, 1)
            dve.reciprocal(rstd[:, :, :], rstd[:, :, :]).then_inc(s.inv, 1)
            dve.wait_ge(s.inv, 1)
            for k in range(KT):
                if k >= 3:
                    dve.wait_ge(s.hi, k - 2)
                    dve.wait_ge(s.lo, k - 2)
                dve.scalar_tensor_tensor(out=tmp[k % 3][:, :], in0=m.x[:, k, :], scalar=m.small[:, A + k:A + k + 1],
                                         in1=rstd[:, :, :].rearrange("p a b -> p (a b)"), op0=ALU.mult, op1=ALU.mult
                                         ).then_inc(s.scaled, 1)
                if k:
                    rest(k - 1)
            rest(KT - 1)
            with dve.Fori(0, n2) as i:
                for b in range(2):
                    dve.wait_ge(s.mm_done, 2 * i + b + 3)
                    dve.tensor_scalar(m.z[:, ds(2 * i + b, 1), :, :],
                                      m.ps[:, 2 * b:2 * b + 2, :].rearrange("p (o a) n -> p o a n", o=1),
                                      1.0, None, ALU.mult).then_inc(s.copied, 1)


def project_phase(nc, m, a, l, col, nblocks):
    w = a.w_in[l]
    n2 = nblocks // 2
    with phase(nc, "raw0", "raw1", "hi_ready", "lo_ready", "mm_done", "copied") as (block, s):
        @block.sync
        def _(sp):
            with sp.Fori(0, n2) as i:
                for b in range(2):
                    w_load(sp, s, m, 2 * i + b, b, w_view(w, col + P * (2 * i + b)))

        @block.scalar
        def _(act):
            with act.Fori(0, n2) as i:
                for b in range(2):
                    w_round(act, s, m, 2 * i + b, i, b)

        @block.gpsimd
        def _(pool):
            credit_pool(pool, s)
            with pool.Fori(0, n2) as i:
                for b in range(2):
                    w_rest(pool, s, m, 2 * i + b, b)

        @block.tensor
        def _(pe):
            credit_pe(pe, s)
            with pe.Fori(0, n2) as i:
                for b in range(2):
                    pe.wait_ge(s.lo_ready, 2 * i + b + 3)
                    pe.wait_ge(s.copied, 2 * i + b + 1)
                    h_block(pe, m, b, 2 * b).then_inc(s.mm_done, 1)

        @block.vector
        def _(dve):
            dve.sem_inc(s.copied, 2)
            with dve.Fori(0, n2) as i:
                for b in range(2):
                    dve.wait_ge(s.mm_done, 2 * i + b + 3)
                    dve.tensor_scalar(m.z[:, ds(2 * i + b, 1), :, :],
                                      m.ps[:, 2 * b:2 * b + 2, :].rearrange("p (o a) n -> p o a n", o=1),
                                      1.0, None, ALU.mult).then_inc(s.copied, 1)


def zt(m, i, n=1):
    return m.z[:, i:i + n].rearrange("p t a n -> p (t a n)")


GR = 32


def group_sums(pe, m, cst, j, bank, rows, src, first, last):
    return pe.matmul(m.ps[GR * j:GR * (j + 1), bank, :], cst[rows, K_ONE:K_ONE + GR], src, start=first, stop=last)


def group_spread(pe, m, cst, j, bank, packed):
    r = slice(GR * j, GR * j + 1)
    return pe.matmul(m.ps[:, bank, :], cst[r, K_ONE:K_ONE + P], packed[r, :], start=True, stop=True)


def conv_lora_phase(nc, m, l):
    cst = m.const
    sq = m.place(f"l_sq{l}", [P, 3, S], F32, m.W0)
    rstd = m.place(f"l_rstd{l}", [P, HALF], F32, m.W0 + 12288)
    with phase(nc, "u", "acc", "y0", "squared", "summed", "root", "inv", "spread", "done") as (block, s):
        @block.scalar
        def _(act):
            act.activation(sq[:, :, :].rearrange("p t n -> p (t n)"), zt(m, 6, 3), ACT.Square).then_inc(s.squared, 1)
            act.wait_ge(s.summed, 1)
            for q, n in ((0, QL), (1, P)):
                r = slice(2 * GR * q, 2 * GR * (q + 1))
                act.activation(rstd[r, :], m.ps[r, 0, :], ACT.Sqrt, bias=cst[r, K_EPS:K_EPS + 1], scale=1.0 / n).then_inc(s.root, 1)

        @block.tensor
        def _(pe):
            pe.wait_ge(s.squared, 1)
            for q, tiles in ((0, (0, 1)), (1, (2,))):
                for half in range(NHALF):
                    for k in tiles:
                        last = group_sums(pe, m, cst, 2 * q + half, 0, slice(0, P), sq[:, k, half * HALF:(half + 1) * HALF],
                                          k == tiles[0], k == tiles[-1])
            last.then_inc(s.summed, 1)
            pe.wait_ge(s.inv, 1)
            for j in range(4):
                last = group_spread(pe, m, cst, j, 2 + j, rstd)
            last.then_inc(s.spread, 1)

        @block.gpsimd
        def _(pool):
            for t in range(2):
                pool.tensor_tensor(zt(m, 2 + t), zt(m, 2 + t), zt(m, 4 + t), ALU.mult).then_inc(s.u, 1)
            for t in range(2):
                pool.wait_ge(s.acc, 3 * t + 3)
                pool.tensor_tensor(m.ys[:, t, :], zt(m, 4 + t), zt(m, t), ALU.mult).then_inc(s.y0, 1)

        @block.vector
        def _(dve):
            for t in range(2):
                u, y = zt(m, 2 + t), zt(m, 4 + t)
                w = [m.small[:, S_VEC + V_N * l + V_CW + 2 * j + t:S_VEC + V_N * l + V_CW + 2 * j + t + 1] for j in range(3)]
                dve.wait_ge(s.u, t + 1)
                dve.tensor_scalar(y, u, w[2], None, ALU.mult).then_inc(s.acc, 1)
                for j in (1, 0):
                    dve.wait_ge(s.acc, 3 * t + 2 - j)
                    d = 2 - j
                    dve.scalar_tensor_tensor(out=y[:, d:S], in0=u[:, 0:S - d], scalar=w[j], in1=y[:, d:S],
                                             op0=ALU.mult, op1=ALU.add).then_inc(s.acc, 1)
            dve.wait_ge(s.root, 2)
            dve.reciprocal(rstd[:, :], rstd[:, :]).then_inc(s.inv, 1)
            dve.wait_ge(s.spread, 1)
            for k in range(3):
                dve.scalar_tensor_tensor(out=zt(m, 6 + k), in0=zt(m, 6 + k), scalar=m.small[:, S_VEC + V_N * l + V_CQ + k:S_VEC + V_N * l + V_CQ + k + 1],
                                         in1=m.ps[:, 2 + 2 * (k // 2):4 + 2 * (k // 2), :].rearrange("p a n -> p (a n)"),
                                         op0=ALU.mult, op1=ALU.mult).then_inc(s.done, 1)


def qk_phase(nc, m, l):
    cst = m.const
    qk = [m.place(f"qk{l}{n}", [P, 2, S], F32, m.Z0 + 8192 * n if n < 3 else m.W0) for n in range(NG)]
    sq = [m.place(f"qk_sq{l}", [P, 2, S], F32, m.W0 + 8192), m.place(f"qk_sq_b{l}", [P, 2, S], F32, m.Z0 + 8192 * 5)]
    rstd = m.place(f"qk_rstd{l}", [P, HALF], F32, m.W0 + 16384)
    sined = m.ys[:, 4:6, :]
    R = slice(QKN, QK)

    def flat(t):
        return t.rearrange("p a n -> p (a n)")

    with phase(nc, "up", "rope_in", "q_in", "squared", "summed", "root", "inv", "spread", "normed", "turned",
               "cosed", "sined", "done") as (block, s):
        @block.tensor
        def _(pe):
            def up(n):
                for half in range(NHALF):
                    for k in range(2):
                        pe.matmul(m.ps[0:QK, half, :], m.w_uq[:, k, QK * n:QK * (n + 1)], m.z[:, 6 + k, half, :],
                                  start=(k == 0), stop=(k == 1))
                for half in range(NHALF):
                    last = pe.matmul(m.ps[0:QKN, 2 + half, :], m.w_ukv[:, P * n:P * n + QKN], m.z[:, 8, half, :],
                                     start=True, stop=True)
                last.then_inc(s.up, 1)

            up(0)
            for n in range(NG):
                pe.wait_ge(s.squared, 2 * n + 2)
                if n:
                    pe.wait_ge(s.sined, 2 * n)
                for q in range(2):
                    for half in range(NHALF):
                        last = group_sums(pe, m, cst, 2 * q + half, 4, slice(0, QK),
                                          sq[n % 2][0:QK, q, half * HALF:(half + 1) * HALF], True, True)
                last.then_inc(s.summed, 1)
                if n + 1 < NG:
                    up(n + 1)
                pe.wait_ge(s.inv, n + 1)
                for j in range(4):
                    last = group_spread(pe, m, cst, j, 4 + j, rstd)
                last.then_inc(s.spread, 1)
                for q in range(2):
                    pe.wait_ge(s.normed, 2 * n + q + 1)
                    for half in range(NHALF):
                        last = pe.matmul(m.ps[R, 4 + 2 * q + half, :], cst[R, K_PMLA + QKN:K_PMLA + QK],
                                         qk[n][R, q, half * HALF:(half + 1) * HALF], start=True, stop=True)
                    last.then_inc(s.turned, 1)

        @block.scalar
        def _(act):
            def squares(n):
                t = qk[n]
                act.wait_ge(s.up, n + 1)
                act.activation(t[0:QK, 0, :], flat(m.ps[0:QK, 0:2, :]), ACT.Copy).then_inc(s.q_in, 1)
                act.activation(t[0:QKN, 1, :], flat(m.ps[0:QKN, 2:4, :]), ACT.Copy).then_inc(s.q_in, 1)
                if n >= 2:
                    act.wait_ge(s.done, n - 1)
                act.wait_ge(s.q_in, 2 * n + 1)
                act.activation(sq[n % 2][0:QK, 0, :], t[0:QK, 0, :], ACT.Square).then_inc(s.squared, 1)
                act.wait_ge(s.q_in, 2 * n + 2)
                act.wait_ge(s.rope_in, n + 1)
                act.activation(sq[n % 2][0:QK, 1, :], t[0:QK, 1, :], ACT.Square).then_inc(s.squared, 1)

            squares(0)
            for n in range(NG):
                act.wait_ge(s.summed, n + 1)
                if n:
                    act.wait_ge(s.spread, n)
                act.activation(rstd[:, :], m.ps[:, 4, :], ACT.Sqrt, bias=cst[:, K_EPS:K_EPS + 1],
                               scale=1.0 / QK).then_inc(s.root, 1)
                if n + 1 < NG:
                    squares(n + 1)

        @block.vector
        def _(dve):
            for n in range(NG):
                dve.tensor_copy(qk[n][R, 1, :], zt(m, 9)[P - QKR:P, :]).then_inc(s.rope_in, 1)
            for n in range(NG):
                t = qk[n]
                dve.wait_ge(s.root, n + 1)
                dve.reciprocal(rstd[:, :], rstd[:, :]).then_inc(s.inv, 1)
                dve.wait_ge(s.spread, n + 1)
                for q in range(2):
                    g = S_VEC + V_N * l + V_QN + q
                    dve.scalar_tensor_tensor(out=t[0:QK, q, :], in0=t[0:QK, q, :], scalar=m.small[0:QK, g:g + 1],
                                             in1=flat(m.ps[0:QK, 4 + 2 * q:6 + 2 * q, :]), op0=ALU.mult, op1=ALU.mult
                                             ).then_inc(s.normed, 1)
                for q in range(2):
                    dve.wait_ge(s.turned, 2 * n + q + 1)
                    if n and q == 0:
                        dve.wait_ge(s.done, n)
                    dve.tensor_tensor(sined[R, q, :], flat(m.ps[R, 4 + 2 * q:6 + 2 * q, :]), m.table[R, 3, :], ALU.mult).then_inc(s.sined, 1)

        @block.gpsimd
        def _(pool):
            for n in range(NG):
                t = qk[n]
                for q in range(2):
                    pool.wait_ge(s.normed, 2 * n + q + 1)
                    pool.tensor_tensor(sq[n % 2][R, q, :], t[R, q, :], m.table[R, 2, :], ALU.mult).then_inc(s.cosed, 1)
                pool.wait_ge(s.cosed, 2 * n + 2)
                pool.wait_ge(s.turned, 2 * n + 2)
                pool.wait_ge(s.sined, 2 * n + 2)
                pool.tensor_tensor(t[R], sq[n % 2][R], sined[R], ALU.add).then_inc(s.done, 1)
    return qk


def attention_phase(nc, m, l, qk):
    cst = m.const
    v1 = m.place(f"v_ones{l}", [P, ST, NG, P], F32, m.YS4)
    inv = [m.place(f"attn_inv{l}{b}", [P, P], F32, m.Z0 + 4096 * 10 + 512 * b) for b in range(2)]
    prob = [m.place(f"prob{l}{b}", [P, S], F32, m.W0 + 8192 + 4096 * b) for b in range(2)]
    prob_t = [m.place(f"prob_t{l}{b}", [P, ST, P], F32, m.W0 + 16384 + 4096 * b) for b in range(2)]
    stat = m.place(f"attn_stat{l}", [P, 3, NG * ST], F32, m.top)
    steps = [(n, i) for n in range(NG) for i in range(ST)]
    N = len(steps)
    wv = m.w_ukv[:, :].rearrange("p (h c) -> p h c", h=NG)[:, :, QKN:QKN + HD]
    scale = float(QK) ** -0.5
    with phase(nc, "v_up", "v_in", "scored", "maxed", "neg", "exped", "turned", "t_in", "valued", "inved", "o_in") as (block, s):
        @block.tensor
        def _(pe):
            for t in range(ST):
                last = pe.matmul(m.ps[:, 4 + t // 2, MIX * (t % 2):MIX * (t % 2 + 1)], zt(m, 8)[:, P * t:P * t + P], wv,
                                 start=True, stop=True)
                last.then_inc(s.v_up, 1)

            def score(q):
                n, i = steps[q]
                if q >= 2:
                    pe.wait_ge(s.exped, q - 1)
                W = P * (i + 1)
                lhs = qk[n][0:QK, 0, P * i:P * i + P]
                for c in range(0, W, HALF):
                    e = min(W, c + HALF)
                    diag = e == W
                    last = pe.matmul(m.ps[:, 2 * (q % 2) + c // HALF, 0:e - c], lhs, qk[n][0:QK, 1, c:e], start=True, stop=not diag,
                                     skip_group_check=True)
                o = (W - P) % HALF
                last = pe.matmul(m.ps[:, 2 * (q % 2) + (W - P) // HALF, o:o + P], cst[:, K_ID:K_ID + P], cst[:, K_NEG:K_NEG + P],
                                 start=False, stop=True, skip_group_check=True)
                last.then_inc(s.scored, 1)

            def value(q):
                n, i = steps[q]
                pe.wait_ge(s.exped, q + 1)
                if q == 0:
                    pe.wait_ge(s.v_in, 9)
                else:
                    pe.wait_ge(s.t_in, q)
                for c in range(i + 1):
                    last = pe.transpose(m.ps[:, 4 + c // 4, P * (c % 4):P * (c % 4 + 1)], prob[q % 2][:, P * c:P * c + P],
                                        cst[:, K_ID:K_ID + P])
                last.then_inc(s.turned, 1)

            def output(q):
                n, i = steps[q]
                pe.wait_ge(s.t_in, q + 1)
                if q >= 2:
                    pe.wait_ge(s.o_in, q - 1)
                for c in range(i + 1):
                    last = pe.matmul(m.ps[:, 6 + q % 2, 0:P], v1[:, c, n, :], prob_t[q % 2][:, c, :],
                                     start=(c == 0), stop=(c == i))
                last.then_inc(s.valued, 1)

            score(0)
            for q in range(N):
                if q + 1 < N:
                    score(q + 1)
                value(q)
                if q:
                    output(q - 1)
            output(N - 1)

        @block.scalar
        def _(act):
            def copy_turned(act, q):
                W = P * (steps[q][1] + 1)
                act.wait_ge(s.turned, q + 1)
                if q >= 2:
                    act.wait_ge(s.valued, q - 1)
                act.activation(prob_t[q % 2][:, :, :].rearrange("p c n -> p (c n)")[:, 0:W],
                               m.ps[:, 4:6, :].rearrange("p a n -> p (a n)")[:, 0:W], ACT.Copy).then_inc(s.t_in, 1)

            for q in range(N):
                n, i = steps[q]
                W = P * (i + 1)
                if q >= 2:
                    act.wait_ge(s.turned, q - 1)
                act.wait_ge(s.neg, q + 1)
                act.activation(prob[q % 2][:, 0:W], m.ps[:, 2 * (q % 2):2 * (q % 2) + 2, :].rearrange("p a n -> p (a n)")[:, 0:W],
                               ACT.Exp, bias=stat[:, 0, q:q + 1], scale=scale).then_inc(s.exped, 1)
                if q:
                    copy_turned(act, q - 1)
            copy_turned(act, N - 1)

        @block.vector
        def _(dve):
            dve.memset(v1[:, :, :, :], 1.0).then_inc(s.v_in, 1)
            dve.wait_ge(s.v_in, 1)
            for t in range(4):
                dve.wait_ge(s.v_up, 2 * t + 2)
                for b in range(2):
                    dve.tensor_copy(v1[:, 2 * t:2 * t + 2, b::2, HD * b:HD * b + HD],
                                    m.ps[:, 4 + t, :].rearrange("p (t n c) -> p t n c", t=2, c=HD)[:, :, b::2, :]).then_inc(s.v_in, 1)

            def row_max(q):
                W = P * (steps[q][1] + 1)
                dve.wait_ge(s.scored, q + 1)
                dve.reduce_max(stat[:, 2, q:q + 1], m.ps[:, 2 * (q % 2):2 * (q % 2) + 2, :].rearrange("p a n -> p (a n)")[:, 0:W],
                               AX.X).then_inc(s.maxed, 1)
                dve.wait_ge(s.maxed, q + 1)
                dve.tensor_scalar(stat[:, 0, q:q + 1], stat[:, 2, q:q + 1], -scale, None, ALU.mult).then_inc(s.neg, 1)

            def out_copy(q):
                n, i = steps[q]
                rows = slice(HD * (n % 2), HD * (n % 2) + HD)
                sums = slice(HD - HD * (n % 2), 2 * HD - HD * (n % 2))
                dve.wait_ge(s.valued, q + 1)
                dve.reciprocal(inv[q % 2][rows, :], m.ps[sums, 6 + q % 2, 0:P]).then_inc(s.inved, 1)
                dve.wait_ge(s.inved, q + 1)
                dve.tensor_tensor(m.ys[rows, 2 + n // 2, P * i:P * i + P], m.ps[rows, 6 + q % 2, 0:P], inv[q % 2][rows, :],
                                  ALU.mult).then_inc(s.o_in, 1)

            row_max(0)
            for q in range(N):
                if q + 1 < N:
                    row_max(q + 1)
                if q >= 2:
                    out_copy(q - 2)
            out_copy(N - 2)
            out_copy(N - 1)


def sgu_phase(nc, m, l):
    cst = m.const
    vt = m.place(f"sg_vt{l}", [P, ST, MIX], F32, m.W0)
    sq = m.place(f"sg_sq{l}", [P, 2 * S], F32, m.W0 + 8192)
    rstd = m.place(f"sg_rstd{l}", [P, 2 * S], F32, m.W0 + 16384)
    sine = m.ys[:, 6:8, :]
    with phase(nc, "rot_turned", "cosed", "sined", "rotated", "silu", "gelu", "squared", "summed", "root", "inv", "normed",
               "turned", "v_in", "mixed", "biased", "done") as (block, s):
        @block.scalar
        def _(act):
            act.activation(zt(m, 2, 2), zt(m, 2, 2), ACT.Gelu_apprx_tanh).then_inc(s.gelu, 1)
            act.activation(zt(m, 0, 2), zt(m, 0, 2), ACT.Gelu_apprx_tanh).then_inc(s.gelu, 1)
            act.wait_ge(s.gelu, 2)
            act.activation(sq[:, :], zt(m, 2, 2), ACT.Square).then_inc(s.squared, 1)
            act.wait_ge(s.summed, 1)
            act.activation(rstd[:, :], m.ps[:, 0:4, :].rearrange("p a n -> p (a n)"), ACT.Sqrt, bias=cst[:, K_EPS:K_EPS + 1],
                           scale=1.0 / HD).then_inc(s.root, 1)
            act.activation(zt(m, 10, 2), zt(m, 10, 2), ACT.Silu).then_inc(s.silu, 1)

        @block.tensor
        def _(pe):
            for t in range(4):
                if t >= 2:
                    pe.wait_ge(s.sined, t - 1)
                for half in range(NHALF):
                    last = pe.matmul(m.ps[:, 4 + 2 * (t % 2) + half, :], cst[:, K_PRET:K_PRET + P], m.z[:, 4 + t, half, :],
                                     start=True, stop=True)
                last.then_inc(s.rot_turned, 1)
            pe.wait_ge(s.squared, 1)
            for i in range(4):
                last = pe.matmul(m.ps[:, i, :], cst[:, K_BLK:K_BLK + P], sq[:, HALF * i:HALF * (i + 1)], start=True, stop=True)
            last.then_inc(s.summed, 1)
            pe.wait_ge(s.sined, 4)
            pe.wait_ge(s.normed, 2)
            for c in range(ST):
                for t in range(2):
                    last = pe.transpose(m.ps[:, 4 + c // 2, MIX * (c % 2) + P * t:MIX * (c % 2) + P * t + P],
                                        zt(m, 2 + t)[:, P * c:P * c + P], cst[:, K_ID:K_ID + P])
                last.then_inc(s.turned, 1)
            pe.wait_ge(s.v_in, 4)
            for t in range(2):
                for c in range(ST):
                    for g in (2 * t, 2 * t + 1):
                        rows = slice(HD * (g % 2), HD * (g % 2) + HD)
                        last = pe.matmul(m.ps[rows, 2 * t + c // 4, P * (c % 4):P * (c % 4 + 1)], vt[:, c, HD * g:HD * g + HD],
                                         m.ws_t[:, g, :], start=True, stop=True)
                last.then_inc(s.mixed, 1)

        @block.gpsimd
        def _(pool):
            for t in range(4):
                pool.wait_ge(s.rot_turned, t + 1)
                pool.tensor_tensor(zt(m, 4 + t), zt(m, 4 + t), m.table[:, 0, :], ALU.mult).then_inc(s.cosed, 1)

        @block.vector
        def _(dve):
            for t in range(4):
                dve.wait_ge(s.rot_turned, t + 1)
                dve.tensor_tensor(sine[:, t % 2, :], m.ps[:, 4 + 2 * (t % 2):6 + 2 * (t % 2), :].rearrange("p a n -> p (a n)"),
                                  m.table[:, 1, :], ALU.mult).then_inc(s.sined, 1)
                dve.wait_ge(s.sined, t + 1)
                dve.wait_ge(s.cosed, t + 1)
                dve.tensor_tensor(zt(m, 4 + t), zt(m, 4 + t), sine[:, t % 2, :], ALU.add).then_inc(s.rotated, 1)
            dve.wait_ge(s.root, 1)
            dve.reciprocal(rstd[:, :], rstd[:, :]).then_inc(s.inv, 1)
            dve.wait_ge(s.inv, 1)
            for t in range(2):
                dve.scalar_tensor_tensor(out=zt(m, 2 + t), in0=zt(m, 2 + t), scalar=m.small[:, S_VEC + V_N * l + V_GV + t:S_VEC + V_N * l + V_GV + t + 1],
                                         in1=rstd[:, S * t:S * t + S], op0=ALU.mult, op1=ALU.mult).then_inc(s.normed, 1)
            for i in range(4):
                dve.wait_ge(s.turned, 2 * i + 2)
                dve.tensor_copy(vt[:, 2 * i:2 * i + 2, :].rearrange("p c n -> p (c n)"), m.ps[:, 4 + i, :]).then_inc(s.v_in, 1)
            for t in range(2):
                dve.wait_ge(s.mixed, t + 1)
                dve.tensor_tensor(sq[:, S * t:S * t + S].rearrange("p (c n) -> p c n", n=P),
                                  m.ps[:, 2 * t:2 * t + 2, :].rearrange("p a (c n) -> p (a c) n", n=P),
                                  m.bs[:, t:t + 1, :].broadcast_to([P, ST, P]), ALU.add).then_inc(s.biased, 1)
                dve.wait_ge(s.biased, t + 1)
                dve.wait_ge(s.gelu, 2)
                dve.tensor_tensor(m.ys[:, 4 + t, :], sq[:, S * t:S * t + S], zt(m, t), ALU.mult).then_inc(s.done, 1)


def retention_phases(nc, m, l):
    cst = m.const
    KB = 1024
    vt = m.place(f"rt_vt{l}", [P, ST, MIX], F32, m.Z0)
    kd = m.place(f"rt_kd{l}", [P, ST, MIX], F32, m.Z0 + 8 * KB)
    qd = m.place(f"rt_qd{l}", [P, 2, S], F32, m.W0)
    out = m.place(f"rt_out{l}", [P, 2 * S], F32, m.W0 + 8 * KB)
    state = m.place(f"rt_state{l}", [P, ST, 2, HD], F32, m.W0 + 16 * KB)
    pr = [m.place(f"rt_p{l}{b}", [P, 2, 2 * P], F32, m.W0 + (20 + 2 * b) * KB) for b in range(2)]
    sq = m.place(f"rt_sq{l}", [P, 2 * S], F32, m.Z0 + 16 * KB)
    rstd = m.place(f"rt_rstd{l}", [P, 2 * S], F32, m.Z0 + 24 * KB)
    with phase(nc, "qd", "k_turned", "v_turned", "kd_in", "v_in", "kv", "state", "scored", "decayed", "o", "o_in") as (block, s):
        @block.tensor
        def _(pe):
            for c in range(ST):
                b = c % 2
                if c >= 2:
                    pe.wait_ge(s.v_in, c - 1)
                    pe.wait_ge(s.kd_in, c - 1)
                for first, bank, sem in ((6, 2 * b, s.k_turned), (8, 2 * b + 1, s.v_turned)):
                    for t in range(2):
                        last = pe.transpose(m.ps[:, bank, P * t:P * t + P], zt(m, first + t)[:, P * c:P * c + P], cst[:, K_ID:K_ID + P])
                    last.then_inc(sem, 1)
            for c in range(ST - 1):
                pe.wait_ge(s.v_in, c + 1)
                pe.wait_ge(s.kd_in, c + 1)
                if c >= 2:
                    pe.wait_ge(s.state, 2 * (c - 1) + 1)
                for h in range(NG):
                    rows = slice(HD * (h % 2), HD * (h % 2) + HD)
                    cols = slice(HD * h, HD * h + HD)
                    last = pe.matmul(m.ps[rows, 4 + c % 2, HD * (h // 2):HD * (h // 2) + HD], kd[:, c, cols], vt[:, c, cols],
                                     start=True, stop=True)
                last.then_inc(s.kv, 1)

            def scores(c):
                if c == 1:
                    pe.wait_ge(s.state, 2 * ST - 1)
                if c >= 2:
                    pe.wait_ge(s.decayed, c - 1)
                for h in range(NG):
                    rows = slice(HD * (h % 2), HD * (h % 2) + HD)
                    last = pe.matmul(m.ps[:, 6 - 2 * (c % 2) + h % 2, P * (h // 2):P * (h // 2) + P], zt(m, 6 + h // 2)[rows, P * c:P * c + P],
                                     zt(m, 4 + h // 2)[rows, P * c:P * c + P], start=True, stop=True)
                last.then_inc(s.scored, 1)

            scores(0)
            for c in range(ST):
                if c + 1 < ST:
                    scores(c + 1)
                pe.wait_ge(s.decayed, c + 1)
                if c == 0:
                    pe.wait_ge(s.v_in, ST)
                    pe.wait_ge(s.kd_in, ST)
                    pe.wait_ge(s.qd, 2)
                pe.wait_ge(s.state, 2 * c + 1)
                if c >= 2:
                    pe.wait_ge(s.o_in, c - 1)
                for h in range(NG):
                    rows = slice(HD * (h % 2), HD * (h % 2) + HD)
                    dst = m.ps[rows, c % 2, P * (h // 2):P * (h // 2) + P]
                    pe.matmul(dst, vt[:, c, HD * h:HD * h + HD], pr[c % 2][:, h % 2, P * (h // 2):P * (h // 2) + P],
                              start=True, stop=(c == 0),
                              skip_group_check=True)
                    if c:
                        pe.matmul(dst, state[rows, c, h // 2, :], qd[rows, h // 2, P * c:P * c + P], start=False, stop=True,
                                  skip_group_check=True)
                pe.drain().then_inc(s.o, 1)

        @block.scalar
        def _(act):
            for c in range(ST):
                act.wait_ge(s.v_turned, c + 1)
                act.activation(vt[:, c, :], m.ps[:, 2 * (c % 2) + 1, 0:MIX], ACT.Copy).then_inc(s.v_in, 1)
            for c in range(ST):
                act.wait_ge(s.o, c + 1)
                act.activation(out[:, :].rearrange("p (t c n) -> p t c n", t=2, n=P)[:, :, c, :],
                               m.ps[:, c % 2, 0:MIX].rearrange("p (t n) -> p t n", t=2), ACT.Copy).then_inc(s.o_in, 1)

        @block.vector
        def _(dve):
            for t in range(2):
                dve.tensor_tensor(qd[:, t, :].rearrange("p (c n) -> p c n", n=P), zt(m, 4 + t).rearrange("p (c n) -> p c n", n=P),
                                  cst[:, K_QDEC + P * t:K_QDEC + P * t + P].rearrange("p (o n) -> p o n", o=1).broadcast_to([P, ST, P]),
                                  ALU.mult).then_inc(s.qd, 1)
            for c in range(ST):
                dve.wait_ge(s.k_turned, c + 1)
                dve.tensor_tensor(kd[:, c, :], m.ps[:, 2 * (c % 2), 0:MIX], cst[:, K_KDEC:K_KDEC + MIX], ALU.mult).then_inc(s.kd_in, 1)
            dve.memset(state[:, 0], 0.0).then_inc(s.state, 1)
            for c in range(ST - 1):
                dve.wait_ge(s.state, 2 * c + 1)
                dve.wait_ge(s.kv, c + 1)
                for t in range(2):
                    dve.scalar_tensor_tensor(out=state[:, c + 1, t, :], in0=state[:, c, t, :], scalar=cst[:, K_CD + t:K_CD + t + 1],
                                             in1=m.ps[:, 4 + c % 2, HD * t:HD * t + HD], op0=ALU.mult, op1=ALU.add).then_inc(s.state, 1)
            for c in range(ST):
                dve.wait_ge(s.scored, c + 1)
                if c >= 2:
                    dve.wait_ge(s.o, c - 1)
                dve.tensor_tensor(pr[c % 2][:, :, :], m.ps[:, 6 - 2 * (c % 2):8 - 2 * (c % 2), 0:2 * P],
                                  cst[:, K_DEC:K_DEC + NG * P].rearrange("p (a n) -> p a n", a=2), ALU.mult).then_inc(s.decayed, 1)
    with phase(nc, "mean", "centred", "squared", "summed", "root", "inv", "scaled", "done") as (block, s):
        @block.tensor
        def _(pe):
            for i in range(4):
                last = pe.matmul(m.ps[:, i, :], cst[:, K_BLK:K_BLK + P], out[:, HALF * i:HALF * (i + 1)], start=True, stop=True)
            last.then_inc(s.mean, 1)
            pe.wait_ge(s.squared, 1)
            for i in range(4):
                last = pe.matmul(m.ps[:, 4 + i, :], cst[:, K_BLK:K_BLK + P], sq[:, HALF * i:HALF * (i + 1)], start=True, stop=True)
            last.then_inc(s.summed, 1)

        @block.scalar
        def _(act):
            act.wait_ge(s.centred, 1)
            act.activation(sq[:, :], out[:, :], ACT.Square).then_inc(s.squared, 1)
            act.wait_ge(s.summed, 1)
            act.activation(rstd[:, :], m.ps[:, 4:8, :].rearrange("p a n -> p (a n)"), ACT.Sqrt, bias=cst[:, K_EPS:K_EPS + 1],
                           scale=1.0 / HD).then_inc(s.root, 1)

        @block.vector
        def _(dve):
            dve.wait_ge(s.mean, 1)
            dve.scalar_tensor_tensor(out=out[:, :], in0=m.ps[:, 0:4, :].rearrange("p a n -> p (a n)"), scalar=-1.0 / HD,
                                     in1=out[:, :], op0=ALU.mult, op1=ALU.add).then_inc(s.centred, 1)
            dve.wait_ge(s.root, 1)
            dve.reciprocal(rstd[:, :], rstd[:, :]).then_inc(s.inv, 1)
            dve.wait_ge(s.inv, 1)
            for t in range(2):
                dve.scalar_tensor_tensor(out=sq[:, S * t:S * t + S], in0=out[:, S * t:S * t + S],
                                         scalar=m.small[:, S_VEC + V_N * l + V_RET + t:S_VEC + V_N * l + V_RET + t + 1],
                                         in1=rstd[:, S * t:S * t + S], op0=ALU.mult, op1=ALU.mult).then_inc(s.scaled, 1)
                dve.wait_ge(s.scaled, t + 1)
                dve.tensor_tensor(m.ys[:, 6 + t, :], sq[:, S * t:S * t + S], zt(m, 10 + t), ALU.mult).then_inc(s.done, 1)


def gate_phase(nc, m, a, l):
    KB = 1024
    merged = m.place(f"merged{l}", [P, KT, S], F32, m.Z0)
    wb = [m.place(f"w_br{l}{b}", [P, 2, P], F32, m.Z0 + (32 + b) * KB) for b in range(2)]
    sig = [m.place(f"sig{l}{b}", [P, S], F32, m.Z0 + (34 + 4 * b) * KB) for b in range(2)]
    w = a.w_in[l]
    with phase(nc, "raw0", "raw1", "br0", "br1", "hi_ready", "lo_ready", "mm_done", "sig_ready", "gated", "summed") as (block, s):
        @block.sync
        def _(sp):
            with sp.Fori(0, KT) as mt:
                for n in range(NBR):
                    sp.wait_ge(s.mm_done, NBR * mt + n + 1)
                    w_load(sp, s, m, NBR * mt + n, n % 2, w_view(w, P * mt + (C_GATE + D * n)))
                    sp.dma_start(wb[n % 2][:, :, :], w_view(a.w_branch[l, n], P * mt)).then_inc((s.br0, s.br1)[n % 2], 16)

        @block.scalar
        def _(act):
            w_round(act, s, m, 0, 0, 0)

            def step(mt, last):
                for n in range(NBR):
                    if not (last and n == NBR - 1):
                        w_round(act, s, m, NBR * mt + n + 1, 2 * mt + (n + 1) // 2, (n + 1) % 2)
                    act.wait_ge(s.mm_done, NBR * mt + n + 3)
                    act.wait_ge(s.summed, NBR * mt + n + 1)
                    act.activation(sig[n % 2][:, :], m.ps[:, 4 * (n % 2):4 * (n % 2) + 2, :].rearrange("p a n -> p (a n)"),
                                   ACT.Sigmoid).then_inc(s.sig_ready, 1)
            looped(act, KT, step)

        @block.gpsimd
        def _(pool):
            credit_pool(pool, s)
            with pool.Fori(0, KT) as mt:
                for n in range(NBR):
                    w_rest(pool, s, m, NBR * mt + n, n % 2)

        @block.tensor
        def _(pe):
            credit_pe(pe, s)
            with pe.Fori(0, KT) as mt:
                for n in range(NBR):
                    b = n % 2
                    pe.wait_ge(s.lo_ready, NBR * mt + n + 3)
                    pe.wait_ge(s.summed, NBR * mt + n + 1)
                    h_block(pe, m, b, 4 * b)
                    pe.wait_ge((s.br0, s.br1)[b], 32 * mt + 16 * (n // 2) + 16)
                    for half in range(NHALF):
                        for k in range(2):
                            last = pe.matmul(m.ps[:, 4 * b + 2 + half, :], wb[b][:, k, :],
                                             m.ys[:, 2 * n + k, half * HALF:(half + 1) * HALF], start=(k == 0), stop=(k == 1))
                    last.then_inc(s.mm_done, 1)

        @block.vector
        def _(dve):
            dve.sem_inc(s.summed, 2)
            with dve.Fori(0, KT) as mt:
                dst = merged[:, ds(mt, 1), :].rearrange("p o n -> p (o n)")
                for n in range(NBR):
                    b = n % 2
                    dve.wait_ge(s.sig_ready, NBR * mt + n + 1)
                    prod = m.ps[:, 4 * b + 2:4 * b + 4, :].rearrange("p a n -> p (a n)")
                    if n == 0:
                        dve.tensor_tensor(dst, sig[b][:, :], prod, ALU.mult).then_inc(s.summed, 1)
                    else:
                        dve.tensor_tensor(sig[b][:, :], sig[b][:, :], prod, ALU.mult).then_inc(s.gated, 1)
                        dve.wait_ge(s.gated, (NBR - 1) * mt + n)
                        dve.wait_ge(s.summed, NBR * mt + n + 2)
                        dve.tensor_tensor(dst, dst, sig[b][:, :], ALU.add).then_inc(s.summed, 1)
    return merged


def out_proj_phase(nc, m, a, l, merged):
    w = a.w_o[l]
    G1 = S_ADA + 48 * l + 16
    with phase(nc, "raw0", "raw1", "hi_ready", "lo_ready", "mm_done", "m_hi", "m_lo", "x_in", "added", "stored") as (block, s):
        @block.sync
        def _(sp):
            def store(k):
                sp.wait_ge(s.added, k + 3)
                sp.dma_start(a.xs[P * k:P * k + P, :], m.x[:, k, :]).then_inc(s.stored, 16)

            for b in range(2):
                w_load(sp, s, m, b, b, w_view(w, P * b))
            sp.dma_start(m.x[:, :, :], a.xs.rearrange("(k p) n -> p k n", p=P)).then_inc(s.x_in, 16)
            for j in range(2, KT):
                if j >= 3:
                    store(j - 3)
                w_load(sp, s, m, j, j % 2, w_view(w, P * j))
            for k in range(KT - 3, KT):
                store(k)
            sp.wait_ge(s.stored, 16 * KT)

        @block.scalar
        def _(act):
            for b in range(2):
                w_round(act, s, m, b, 0, b)
            for k in range(KT):
                act.activation(m.h_hi[:, k, :], merged[:, k, :], ACT.Copy).then_inc(s.m_hi, 1)
            for j in range(2, KT):
                w_round(act, s, m, j, j // 2, j % 2)

        @block.gpsimd
        def _(pool):
            credit_pool(pool, s)
            for b in range(2):
                w_rest(pool, s, m, b, b)
            for j in range(2, KT):
                w_rest(pool, s, m, j, j % 2)

        @block.tensor
        def _(pe):
            credit_pe(pe, s)
            for j in range(KT):
                pe.wait_ge(s.lo_ready, j + 3)
                pe.wait_ge(s.added, j + 1)
                h_block(pe, m, j % 2, 2 * (j % 2), s.m_lo if j == 0 else None).then_inc(s.mm_done, 1)

        @block.vector
        def _(dve):
            dve.sem_inc(s.added, 2)
            for k in range(KT):
                dve.wait_ge(s.m_hi, k + 1)
                dve.tensor_tensor(m.h_lo[:, k, :], merged[:, k, :], m.h_hi[:, k, :].bitcast(F32), ALU.subtract).then_inc(s.m_lo, 1)
            dve.wait_ge(s.x_in, 16)
            for j in range(KT):
                dve.wait_ge(s.mm_done, j + 3)
                dve.scalar_tensor_tensor(out=m.x[:, j, :], in0=m.ps[:, 2 * (j % 2):2 * (j % 2) + 2, :].rearrange("p a n -> p (a n)"),
                                         scalar=m.small[:, G1 + j:G1 + j + 1], in1=m.x[:, j, :], op0=ALU.mult,
                                         op1=ALU.add).then_inc(s.added, 1)


def ffn_phases(nc, m, a, l):
    KB = 1024
    hid_hi = m.place(f"hid_hi{l}", [P, FT, HALF], F32R, m.R + 88 * KB)
    hid_lo = m.place(f"hid_lo{l}", [P, FT, HALF], F32R, m.R + 132 * KB)
    act_t = [m.place(f"f_act{l}{b}", [P, HALF], F32, m.R + (176 + 2 * b) * KB) for b in range(2)]
    hid_f = [m.place(f"f_hid{l}{b}", [P, HALF], F32, m.R + (180 + 2 * b) * KB) for b in range(2)]
    x_t = [m.place(f"f_x{l}{b}", [P, HALF], F32, m.R + (184 + 2 * b) * KB) for b in range(2)]
    G2 = S_ADA + 48 * l + 40
    e = l // 2
    parts = [(0, 8), (8, 16), (16, FT)]
    for half in range(NHALF):
        tok = slice(half * HALF, (half + 1) * HALF)
        with phase(nc, "raw0", "raw1", "hi_ready", "lo_ready", "mm_done", "silu", "hid", "hid_hi", "hid_lo") as (block, s):
            @block.sync
            def _(sp):
                with sp.Fori(0, FT) as f:
                    for b, w in enumerate((a.ffn_w1[e], a.ffn_w3[e])):
                        w_load(sp, s, m, 2 * f + b, b, w_view(w, P * f))

            @block.scalar
            def _(act):
                for b in range(2):
                    w_round(act, s, m, b, 0, b)

                def step(i, last):
                    for c in range(2):
                        f = 2 * i + c
                        if not (last and c):
                            for b in range(2):
                                w_round(act, s, m, 2 * f + 2 + b, f + 1, b)
                        act.wait_ge(s.mm_done, 2 * f + 4)
                        act.wait_ge(s.hid, f + 1)
                        act.activation(act_t[c][:, :], m.ps[:, 2 * c, :], ACT.Silu).then_inc(s.silu, 1)
                looped(act, FT // 2, step)

            @block.gpsimd
            def _(pool):
                credit_pool(pool, s)
                with pool.Fori(0, FT) as f:
                    for b in range(2):
                        w_rest(pool, s, m, 2 * f + b, b)

            @block.tensor
            def _(pe):
                credit_pe(pe, s)
                with pe.Fori(0, FT // 2) as i:
                    for c in range(2):
                        pe.wait_ge(s.hid, 2 * i + c + 1)
                        for b in range(2):
                            pe.wait_ge(s.lo_ready, 4 * i + 2 * c + b + 3)
                            for k in range(KT):
                                last = mm3(pe, m.ps[:, 2 * c + b, :], m.w_hi[b][:, k, :], m.w_lo[b][:, k, :],
                                           m.h_hi[:, k, tok], m.h_lo[:, k, tok], k == 0, k == KT - 1)
                            last.then_inc(s.mm_done, 1)

            @block.vector
            def _(dve):
                dve.sem_inc(s.hid, 2)
                with dve.Fori(0, FT // 2) as i:
                    for c in range(2):
                        f = 2 * i + c
                        dve.wait_ge(s.silu, f + 1)
                        dve.wait_ge(s.mm_done, 2 * f + 4)
                        dve.tensor_tensor(hid_f[c][:, :], act_t[c][:, :], m.ps[:, 2 * c + 1, :], ALU.mult).then_inc(s.hid, 1)
                        dve.wait_ge(s.hid, f + 3)
                        dve.tensor_scalar(hid_hi[:, ds(f, 1), :], hid_f[c][:, :].rearrange("p (o n) -> p o n", o=1), 1.0, None,
                                          ALU.mult).then_inc(s.hid_hi, 1)
                        dve.wait_ge(s.hid_hi, f + 1)
                        dve.tensor_tensor(hid_lo[:, ds(f, 1), :], hid_f[c][:, :].rearrange("p (o n) -> p o n", o=1),
                                          hid_hi[:, ds(f, 1), :].bitcast(F32), ALU.subtract).then_inc(s.hid_lo, 1)
        with phase(nc, "raw0", "raw1", "hi_ready", "lo_ready", "mm_done", "x0", "x1", "tile", "added", "st0", "st1") as (block, s):
            @block.sync
            def _(sp):
                for j in range(KT):
                    c = j % 2
                    if j >= 2:
                        sp.wait_ge((s.st0, s.st1)[c], 16 * (j // 2))
                    sp.dma_start(x_t[c][:, :], a.xs[P * j:P * j + P, tok]).then_inc((s.x0, s.x1)[c], 16)
                    for q, (k0, k1) in enumerate(parts):
                        w_load(sp, s, m, 3 * j + q, (c + q) % 2, w_view(a.ffn_w2[e][P * k0:P * k1, :], P * j), k1 - k0)
                        if j and q == 1:
                            sp.wait_ge(s.added, j + 2)
                            sp.dma_start(a.xs[P * (j - 1):P * j, tok], x_t[1 - c][:, :]).then_inc((s.st0, s.st1)[1 - c], 16)
                sp.wait_ge(s.added, KT + 2)
                sp.dma_start(a.xs[P * (KT - 1):D, tok], x_t[(KT - 1) % 2][:, :]).then_inc((s.st0, s.st1)[(KT - 1) % 2], 16)
                sp.wait_ge(s.st0, 16 * KT // 2)
                sp.wait_ge(s.st1, 16 * KT // 2)

            @block.scalar
            def _(act):
                for j in range(KT):
                    c = j % 2
                    for q, (k0, k1) in enumerate(parts):
                        w_round(act, s, m, 3 * j + q, (3 * j + q) // 2, (c + q) % 2, k1 - k0)

            @block.gpsimd
            def _(pool):
                credit_pool(pool, s)
                with pool.Fori(0, KT // 2) as i:
                    for c in range(2):
                        for q, (k0, k1) in enumerate(parts):
                            w_rest(pool, s, m, 6 * i + 3 * c + q, (c + q) % 2, k1 - k0)

            @block.tensor
            def _(pe):
                credit_pe(pe, s)
                with pe.Fori(0, KT // 2) as i:
                    for c in range(2):
                        pe.wait_ge(s.added, 2 * i + c + 1)
                        for q, (k0, k1) in enumerate(parts):
                            b = (c + q) % 2
                            pe.wait_ge(s.lo_ready, 6 * i + 3 * c + q + 3)
                            for k in range(k0, k1):
                                last = mm3(pe, m.ps[:, c, :], m.w_hi[b][:, k - k0, :], m.w_lo[b][:, k - k0, :],
                                           hid_hi[:, k, :], hid_lo[:, k, :], k == 0, k == FT - 1)
                            last.then_inc(s.mm_done, 1)

            @block.vector
            def _(dve):
                dve.sem_inc(s.added, 2)
                for j in range(KT):
                    c = j % 2
                    dve.wait_ge((s.x0, s.x1)[c], 16 * (j // 2) + 16)
                    dve.wait_ge(s.mm_done, 3 * j + 5)
                    dve.scalar_tensor_tensor(out=x_t[c][:, :], in0=m.ps[:, c, :], scalar=m.small[:, G2 + j:G2 + j + 1],
                                             in1=x_t[c][:, :], op0=ALU.mult, op1=ALU.add).then_inc(s.added, 1)


ITEM = 256
SLOTS = 2 * S
MAX_ITEMS = (SLOTS + NE * (ITEM - 1)) // ITEM
FGRP = 4
NFG = FE // (P * FGRP)
NF2 = FE // (2 * P)


def moe_memory(m):
    KB = 1024
    R = m.R
    m.hrow = m.place("h_rows", [P, ST, D], F32, R + 32 * KB)
    E = R + 196 * KB
    m.slot = m.place("slot", [P, ST, 2], I32, E)
    m.top_w = m.place("top_w", [P, ST, 2], F32, E + 64)
    m.items = m.place("items", [1, (MAX_ITEMS + 1) * 4], I32, E + 128)
    m.route = R + 70 * KB


def route_phase(nc, m, a, l):
    cst = m.const
    rw = m.place("router_w_sb", [P, KT, NE], F32, m.route)
    rb = m.place("router_b_sb", [P, NE], F32, m.route + 256)
    big = m.R + 64 * 1024

    def grid(name, i, dt=F32, shape=(ST, NE)):
        return m.place(name, [P, *shape], dt, big + 256 * i)

    lg, pr, one0, one1, both, rank, t0 = (grid(n, i) for i, n in enumerate(
        ("r_logit", "r_prob", "r_hot0", "r_hot1", "r_both", "r_rank", "r_tmp")))
    top = grid("r_top", 7)
    idx = grid("r_idx", 8, U32)
    idx_f = grid("r_idxf", 9)
    mx, sm, inv, tw = (m.place(n, [P, ST], F32, big + 2560 + 32 * i) for i, n in enumerate(("r_mx", "r_sm", "r_inv", "r_tw")))
    cnt, off, nch, end, beg, c0, c1, hot, val = (m.place(n, [P, NE], F32, big + 2688 + 32 * i) for i, n in enumerate(
        ("r_cnt", "r_off", "r_nch", "r_end", "r_beg", "r_c0", "r_c1", "r_hot", "r_val")))
    tab_f = m.place("r_tabf", [P, 4], F32, big + 3072)
    tab = m.place("r_tab", [P, 4], I32, big + 3104)
    slot_f = m.place("r_slotf", [P, ST, 2], F32, big + 3136)
    e = l // 2
    with phase(nc, "w_in", "turned", "h_in", "logits", "shifted", "exped", "hot", "ranked", "step", "tab", "saved", "back") as (block, s):
        @block.sync
        def _(sp):
            sp.dma_start(rw[:, :, :], a.router_w[e].rearrange("(k p) n -> p k n", p=P)).then_inc(s.w_in, 16)
            sp.dma_start(rb[:, :], a.router_b[e].partition_broadcast(P)).then_inc(s.w_in, 16)
            sp.wait_ge(s.tab, 1)
            sp.dma_start(a.items, tab[0:MAX_ITEMS + 1, :]).then_inc(s.saved, 16)
            sp.wait_ge(s.saved, 16)
            sp.dma_start(m.items[:, :], a.items.rearrange("(o i) c -> o (i c)", o=1)).then_inc(s.back, 16)
            sp.wait_ge(s.back, 16)

        @block.tensor
        def _(pe):
            pe.wait_ge(s.w_in, 32)
            for t in range(ST):
                for k in range(KT):
                    last = pe.matmul(m.ps[:, 7, NE * t:NE * t + NE], m.h_f[:, k, P * t:P * t + P], rw[:, k, :],
                                     start=(k == 0), stop=(k == KT - 1))
            last.then_inc(s.logits, 1)
            for t in range(ST):
                if t >= 2:
                    pe.wait_ge(s.h_in, t - 1)
                for k in range(KT):
                    last = pe.transpose(m.ps[:, 2 * (t % 2) + k // 4, P * (k % 4):P * (k % 4 + 1)],
                                        m.h_f[:, k, P * t:P * t + P], cst[:, K_ID:K_ID + P])
                last.then_inc(s.turned, 1)
            pe.wait_ge(s.hot, 1)
            for t in range(ST):
                for u in range(t + 1):
                    w = K_LOW if u == t else K_ONE
                    last = pe.matmul(m.ps[:, 6, NE * t:NE * t + NE], cst[:, w:w + P], both[:, u, :], start=(u == 0), stop=(u == t))
            for u in range(ST):
                last = pe.matmul(m.ps[:, 5, 0:NE], cst[:, K_ONE:K_ONE + P], both[:, u, :], start=(u == 0), stop=(u == ST - 1))
            last.then_inc(s.ranked, 1)

        @block.scalar
        def _(act):
            for t in range(ST):
                act.wait_ge(s.turned, t + 1)
                act.activation(m.hrow[:, t, :], m.ps[:, 2 * (t % 2):2 * (t % 2) + 2, :].rearrange("p a n -> p (a n)"), ACT.Copy).then_inc(s.h_in, 1)
            act.wait_ge(s.shifted, 1)
            act.activation(pr[:, :, :], lg[:, :, :], ACT.Exp).then_inc(s.exped, 1)

        @block.vector
        def _(dve):
            n = 0

            def chain(ins):
                nonlocal n
                n += 1
                ins.then_inc(s.step, 1)
                dve.wait_ge(s.step, n)

            def wide(v):
                return v[:, :].rearrange("p (t o) -> p t o", o=1).broadcast_to([P, ST, NE])

            def row(v):
                return v[:, :].rearrange("p (o e) -> p o e", o=1).broadcast_to([P, ST, NE])

            dve.wait_ge(s.logits, 1)
            dve.wait_ge(s.w_in, 32)
            chain(dve.tensor_tensor(lg[:, :, :], m.ps[:, 7, 0:ST * NE].rearrange("p (t e) -> p t e", e=NE), row(rb), ALU.add))
            chain(dve.tensor_reduce(mx[:, :], lg[:, :, :], AX.X, ALU.max))
            dve.tensor_tensor(lg[:, :, :], lg[:, :, :], wide(mx), ALU.subtract).then_inc(s.shifted, 1)
            dve.wait_ge(s.exped, 1)
            chain(dve.tensor_reduce(sm[:, :], pr[:, :, :], AX.X, ALU.add))
            chain(dve.reciprocal(inv[:, :], sm[:, :]))
            chain(dve.tensor_tensor(pr[:, :, :], pr[:, :, :], wide(inv), ALU.mult))
            for t in range(ST):
                chain(dve.max(top[:, t, :], pr[:, t, :]))
                chain(dve.max_index(idx[:, t, :], top[:, t, :], pr[:, t, :]))
            chain(dve.tensor_copy(idx_f[:, :, :], idx[:, :, :]))
            chain(dve.tensor_tensor(tw[:, :], top[:, :, 0], top[:, :, 1], ALU.add))
            chain(dve.reciprocal(tw[:, :], tw[:, :]))
            experts = cst[:, K_EXP:K_EXP + NE].rearrange("p (o e) -> p o e", o=1).broadcast_to([P, ST, NE])
            for q, one in enumerate((one0, one1)):
                chain(dve.tensor_tensor(m.top_w[:, :, q], top[:, :, q], tw[:, :], ALU.mult))
                chain(dve.tensor_tensor(one[:, :, :], idx_f[:, :, q:q + 1].broadcast_to([P, ST, NE]), experts, ALU.is_equal))
            dve.tensor_tensor(both[:, :, :], one0[:, :, :], one1[:, :, :], ALU.add).then_inc(s.hot, 1)
            dve.wait_ge(s.ranked, 1)
            chain(dve.tensor_copy(cnt[:, :], m.ps[:, 5, 0:NE]))

            def prefix(out, v):
                chain(dve.memset(out[:, 0:1], 0.0))
                for j in range(1, NE):
                    chain(dve.tensor_tensor(out[:, j:j + 1], out[:, j - 1:j], v[:, j - 1:j], ALU.add))

            prefix(off, cnt)
            chain(dve.tensor_tensor(rank[:, :, :], m.ps[:, 6, 0:ST * NE].rearrange("p (t e) -> p t e", e=NE), row(off), ALU.add))
            for q, one in enumerate((one0, one1)):
                chain(dve.tensor_tensor(t0[:, :, :], rank[:, :, :], one[:, :, :], ALU.mult))
                chain(dve.tensor_reduce(slot_f[:, :, q], t0[:, :, :], AX.X, ALU.add))
            chain(dve.tensor_copy(m.slot[:, :, :], slot_f[:, :, :]))
            chain(dve.tensor_scalar(nch[:, :], cnt[:, :], 0.0, None, ALU.is_gt))
            for j in range(1, S // ITEM):
                chain(dve.scalar_tensor_tensor(out=nch[:, :], in0=cnt[:, :], scalar=float(ITEM * j), in1=nch[:, :], op0=ALU.is_gt, op1=ALU.add))
            prefix(beg, nch)
            chain(dve.tensor_tensor(end[:, :], beg[:, :], nch[:, :], ALU.add))
            item = cst[:, K_ITEM:K_ITEM + 1]
            chain(dve.tensor_scalar(c0[:, :], beg[:, :], item, None, ALU.is_le))
            chain(dve.tensor_scalar(c1[:, :], end[:, :], item, None, ALU.is_gt))
            chain(dve.tensor_tensor(hot[:, :], c0[:, :], c1[:, :], ALU.mult))
            chain(dve.tensor_scalar(val[:, :], beg[:, :], item, -float(ITEM), ALU.subtract, ALU.mult))
            for col, src, op in ((1, off, ALU.add), (2, cnt, ALU.subtract)):
                chain(dve.tensor_tensor(c0[:, :], src[:, :], val[:, :], op))
                chain(dve.tensor_tensor(c0[:, :], c0[:, :], hot[:, :], ALU.mult))
                chain(dve.tensor_reduce(tab_f[:, col:col + 1], c0[:, :], AX.X, ALU.add))
            chain(dve.tensor_tensor(c0[:, :], cst[:, K_EXP:K_EXP + NE], hot[:, :], ALU.mult))
            chain(dve.tensor_reduce(tab_f[:, 0:1], c0[:, :], AX.X, ALU.add))
            chain(dve.tensor_copy(tab_f[:, 3:4], end[:, NE - 1:NE]))
            dve.tensor_copy(tab[:, :], tab_f[:, :]).then_inc(s.tab, 1)


def scatter_phase(nc, m, a):
    zero = m.place("zeros", [P, 2, D], F32, m.R + 72 * 1024)
    with phase(nc, "zeroed", "filled", "scattered") as (block, s):
        @block.vector
        def _(dve):
            dve.memset(zero[:, :, :], 0.0).then_inc(s.zeroed, 1)

        @block.sync
        def _(sp):
            sp.wait_ge(s.zeroed, 1)
            sp.dma_start(a.rows[SLOTS:SLOTS + ITEM, :].rearrange("(t p) n -> p t n", p=P), zero[:, :, :]).then_inc(s.filled, 16)
            sp.wait_ge(s.filled, 16)

        @block.gpsimd
        def _(pool):
            for t in range(ST):
                for q in range(2):
                    pool.indirect_dma_start(a.rows, bass.IndirectOffsetOnAxis(ap=m.slot[:, t, q:q + 1].bitcast(U32), axis=0),
                                            m.hrow[:, t, :], None).then_inc(s.scattered, 16)
            pool.wait_ge(s.scattered, 16 * 2 * ST)


def expert_phase(nc, m, a, l):
    KB = 1024
    R = m.R
    e2 = l // 2
    hid_hi = m.place("e_hid_hi", [P, 2 * NF2, ITEM], F32R, R)
    hid_lo = m.place("e_hid_lo", [P, 2 * NF2, ITEM], F32R, R + 28 * KB)
    xg_hi = m.place("e_x_hi", [P, KT, ITEM], F32R, R + 56 * KB)
    xg_lo = m.place("e_x_lo", [P, KT, ITEM], F32R, R + 64 * KB)
    io = m.place("e_io", [P, 2, D], F32, R + 72 * KB)
    raw13 = [m.place(f"e_raw{q}", [P, KT, P * FGRP], F32, R + (80 + 16 * q) * KB) for q in range(2)]
    raw2 = [m.place(f"e_raw2{b}", [P, 2, D], F32, R + (112 + 8 * b) * KB) for b in range(2)]
    w_hi = [m.place(f"e_w_hi{b}", [P, 2, D], F32R, R + (128 + 8 * b) * KB) for b in range(4)]
    w_lo = [m.place(f"e_w_lo{b}", [P, 2, D], F32R, R + (160 + 8 * b) * KB) for b in range(4)]
    act_t = [m.place(f"e_act{b}", [P, HALF], F32, R + (192 + 2 * b) * KB) for b in range(2)]
    UNITS = 4 * NFG + NF2

    def flat(t):
        return t[:, :, :].rearrange("p k n -> p (k n)")

    def by_k(t):
        return flat(t).rearrange("p (k n) -> p k n", k=KT)

    def half_block(q, h):
        return raw13[q][:, :, 2 * P * h:2 * P * h + 2 * P]

    def field(eng, item, col, hi):
        return eng.value_load(m.items[0:1, ds(4 * item + col, 1)], min_val=0, max_val=hi)

    with phase(nc, "x_in", "raw1a", "raw3a", "raw1b", "raw3b", "raw2a", "raw2b", "hi_ready", "lo1", "lo3", "lo2", "mm_done", "turned", "x_hi", "x_lo",
               "silu", "hid", "hid_turned", "hid_hi", "hid_lo", "y_done", "y_in", "y_stored", "closed") as (block, s):
        raw_sem = (s.raw1a, s.raw3a, s.raw1b, s.raw3b)
        raw2_sem = (s.raw2a, s.raw2b)
        lo_sem = (s.lo1, s.lo3)

        @block.sync
        def _(sp):
            def rows_in(item):
                base = field(sp, item, 1, SLOTS)
                sp.dma_start(io[:, :, :], a.rows[ds(base, ITEM), :].rearrange("(t p) n -> p t n", p=P)).then_inc(s.x_in, 16)

            def load13(ex, item, i):
                for u in range(4):
                    q, h = u % 2, u // 2
                    w = (a.moe_w1, a.moe_w3)[q]
                    sp.wait_ge(lo_sem[q], 2 * (NFG * item + i) + h + 1)
                    sp.dma_start(half_block(q, h),
                                 w[e2, ds(ex, 1)].rearrange("o (k p) n -> p (o k) n", p=P)[:, :, ds(P * FGRP * i + 2 * P * h, 2 * P)]
                                 ).then_inc(raw_sem[u], 16)

            rows_in(0)
            load13(field(sp, 0, 0, NE - 1), 0, 0)
            n_items = field(sp, 0, 3, MAX_ITEMS)
            with sp.Fori(0, MAX_ITEMS) as item:
                with sp.If(item < n_items):
                    ex = field(sp, item, 0, NE - 1)
                    with sp.Fori(1, NFG) as i:
                        load13(ex, item, i)
                    sp.wait_ge(s.turned, item + 1)
                    sp.wait_ge(s.y_stored, 16 * item + 16)
                    rows_in(item + 1)
                    with sp.Fori(0, NF2 // 2) as i:
                        for b in range(2):
                            sp.wait_ge(s.lo2, NF2 * item + 2 * i + b + 1)
                            sp.dma_start(raw2[b][:, :, :],
                                         a.moe_w2[e2, ds(ex, 1)].rearrange("o (g t p) n -> p (o g) t n", p=P, t=2)[:, ds(2 * i + b, 1)]
                                         .rearrange("p g t n -> p (g t) n")).then_inc(raw2_sem[b], 16)
                    load13(field(sp, item + 1, 0, NE - 1), item + 1, 0)
            sp.wait_ge(s.x_in, 16 * n_items + 16)
            for u in range(4):
                sp.wait_ge(raw_sem[u], 16 * NFG * n_items + 16)
            sp.sem_inc(s.closed, 1)

        @block.scalar
        def _(act):
            def unit13(item, i, u, back=4):
                q, h = u % 2, u // 2
                act.wait_ge(raw_sem[u], 16 * (NFG * item + i) + 16)
                act.wait_ge(s.mm_done, UNITS * item + 4 * i + u + 5 - back)
                act.activation(by_k(w_hi[u]), half_block(q, h), ACT.Copy).then_inc(s.hi_ready, 1)

            def unit2(item, i, b):
                act.wait_ge(raw2_sem[b % 2], 16 * (NF2 // 2 * item + 2 * i + b // 2) + 16)
                act.wait_ge(s.mm_done, UNITS * item + 4 * NFG + 4 * i + b + 1)
                act.activation(flat(w_hi[b]), flat(raw2[b % 2]), ACT.Copy).then_inc(s.hi_ready, 1)

            def silu(item, i, h, width):
                act.wait_ge(s.mm_done, UNITS * item + 4 * i + 2 * h + 5)
                act.wait_ge(s.hid_lo, 2 * (NFG * item + i) + h + 1)
                act.activation(act_t[h][:, 0:width], m.ps[:, h, 0:width], ACT.Silu).then_inc(s.silu, 1)

            def gate_blocks(item, width):
                with act.Fori(0, NFG - 1) as i:
                    for h in range(2):
                        silu(item, i, h, width)
                        unit13(item, i + 1, 2 * h)
                        unit13(item, i + 1, 2 * h + 1)
                for h in range(2):
                    silu(item, NFG - 1, h, width)
                    unit2(item, 0, 2 * h)
                    unit2(item, 0, 2 * h + 1)

            def x_round(count):
                act.wait_ge(s.turned, count)
                act.activation(flat(xg_hi), m.ps[:, 0:4, :].rearrange("p a n -> p (a n)"), ACT.Copy).then_inc(s.x_hi, 1)

            act.sem_inc(s.y_stored, 16)
            x_round(1)
            for u in range(4):
                unit13(0, 0, u, back=2 if u < 2 else 4)
            n_items = field(act, 0, 3, MAX_ITEMS)
            with act.Fori(0, MAX_ITEMS) as item:
                with act.If(item < n_items):
                    left = field(act, item, 2, S)
                    with act.If(left < P + 1):
                        gate_blocks(item, 2 * P)
                    with act.Else():
                        gate_blocks(item, HALF)
                    x_round(item + 2)
                    with act.Fori(1, NF2 // 4) as i:
                        for b in range(4):
                            unit2(item, i, b)
                    for b in range(NF2 % 4):
                        unit2(item, NF2 // 4, b)
                    unit13(item + 1, 0, 0, back=2)
                    unit13(item + 1, 0, 1, back=2)
                    act.wait_ge(s.y_done, item + 1)
                    act.activation(flat(io), m.ps[:, 4:8, :].rearrange("p a n -> p (a n)"), ACT.Copy).then_inc(s.y_in, 1)
                    base = field(act, item, 1, SLOTS)
                    act.wait_ge(s.y_in, item + 2)
                    act.wait_ge(s.y_stored, 16 * item + 16)
                    act.dma_start(a.y_rows[ds(base, ITEM), :].rearrange("(t p) n -> p t n", p=P), io[:, :, :]).then_inc(s.y_stored, 16)
                    unit13(item + 1, 0, 2)
                    unit13(item + 1, 0, 3)
            act.wait_ge(s.y_stored, 16 * n_items + 16)
            act.sem_inc(s.closed, 1)

        def rest13(eng, item, i, u):
            q, h = u % 2, u // 2
            eng.wait_ge(s.hi_ready, UNITS * item + 4 * i + u + 1)
            eng.tensor_tensor(by_k(w_lo[u]), half_block(q, h), by_k(w_hi[u]).bitcast(F32), ALU.subtract).then_inc(lo_sem[q], 1)

        @block.gpsimd
        def _(pool):
            pool.sem_inc(s.lo3, 2)
            for h in range(2):
                rest13(pool, 0, 0, 2 * h + 1)
            n_items = field(pool, 0, 3, MAX_ITEMS)
            with pool.Fori(0, MAX_ITEMS) as item:
                with pool.If(item < n_items):
                    with pool.Fori(1, NFG) as i:
                        for h in range(2):
                            rest13(pool, item, i, 2 * h + 1)
                    for h in range(2):
                        rest13(pool, item + 1, 0, 2 * h + 1)

        @block.tensor
        def _(pe):
            pe.sem_inc(s.mm_done, 4)

            def turn(count, hid_count):
                pe.wait_ge(s.x_in, 16 * count)
                if hid_count is not None:
                    pe.wait_ge(s.hid, hid_count)
                for k in range(KT):
                    for t in range(2):
                        last = pe.transpose(m.ps[:, k // 2, ITEM * (k % 2) + P * t:ITEM * (k % 2) + P * t + P],
                                            io[:, t, P * k:P * k + P], m.const[:, K_ID:K_ID + P])
                last.then_inc(s.turned, 1)

            def up(item):
                with pe.Fori(0, NFG) as i:
                    for u in range(4):
                        q, h = u % 2, u // 2
                        if u == 0:
                            pe.wait_ge(s.x_lo, item + 1)
                        if q == 0:
                            pe.wait_ge(s.hid, 2 * (NFG * item + i) + h + 1)
                        pe.wait_ge(lo_sem[q], 2 * (NFG * item + i) + h + 3)
                        hi, lo = by_k(w_hi[u]), by_k(w_lo[u])
                        for f in range(2):
                            for k in range(KT):
                                last = mm3(pe, m.ps[:, 2 * q + h, ITEM * f:ITEM * (f + 1)], hi[:, k, P * f:P * f + P],
                                           lo[:, k, P * f:P * f + P], xg_hi[:, k, :], xg_lo[:, k, :], k == 0, k == KT - 1)
                        last.then_inc(s.mm_done, 1)

            def up_unit(item, i, u):
                q, h = u % 2, u // 2
                if u == 0:
                    pe.wait_ge(s.x_lo, item + 1)
                if q == 0:
                    pe.wait_ge(s.hid, 2 * (NFG * item + i) + h + 1)
                pe.wait_ge(lo_sem[q], 2 * (NFG * item + i) + h + 3)
                hi, lo = by_k(w_hi[u]), by_k(w_lo[u])
                for k in range(KT):
                    last = mm3(pe, m.ps[:, 2 * q + h, 0:2 * P], xg_hi[:, k, 0:P], xg_lo[:, k, 0:P], hi[:, k, :], lo[:, k, :],
                               k == 0, k == KT - 1)
                last.then_inc(s.mm_done, 1)

            def turn_hidden(item, i, h):
                g = 2 * (NFG * item + i) + h
                pe.wait_ge(s.hid, g + 3)
                pe.wait_ge(s.hid_lo, g + 1)
                for f in range(2):
                    last = pe.transpose(m.ps[:, 6 + h, P * f:P * (f + 1)], act_t[h][:, P * f:P * (f + 1)],
                                        m.const[:, K_ID:K_ID + P])
                last.then_inc(s.hid_turned, 1)

            def up_narrow(item):
                for u in range(4):
                    up_unit(item, 0, u)
                pe.wait_ge(s.y_in, item + 1)
                turn_hidden(item, 0, 0)
                with pe.Fori(1, NFG) as i:
                    up_unit(item, i, 0)
                    up_unit(item, i, 1)
                    turn_hidden(item, i - 1, 1)
                    up_unit(item, i, 2)
                    up_unit(item, i, 3)
                    turn_hidden(item, i, 0)
                turn_hidden(item, NFG - 1, 1)

            def down(item, width):
                for c in range(NF2):
                    pe.wait_ge(s.lo2, NF2 * item + c + 3)
                    hi, lo = flat(w_hi[c % 4]), flat(w_lo[c % 4])
                    for f in range(2):
                        for t in range(width // P):
                            hh = hid_hi[:, 2 * c + f, P * t:P * t + P]
                            hl = hid_lo[:, 2 * c + f, P * t:P * t + P]
                            for d in range(2):
                                cols = slice(D * f + HALF * d, D * f + HALF * (d + 1))
                                last = mm3(pe, m.ps[:, 4 + 2 * t + d, :], hh, hl, hi[:, cols], lo[:, cols],
                                           c == 0 and f == 0, c == NF2 - 1 and f == 1)
                    last.then_inc(s.mm_done, 1)

            def between(item):
                pe.wait_ge(s.hid_lo, 2 * NFG * item + (2 * NFG + 2))
                pe.wait_ge(s.y_in, item + 1)

            turn(1, None)
            n_items = field(pe, 0, 3, MAX_ITEMS)
            with pe.Fori(0, MAX_ITEMS) as item:
                with pe.If(item < n_items):
                    left = field(pe, item, 2, S)
                    with pe.If(left < P + 1):
                        up_narrow(item)
                        turn(item + 2, 2 * NFG * item + (2 * NFG + 2))
                        between(item)
                        down(item, P)
                    with pe.Else():
                        up(item)
                        pe.sem_inc(s.hid_turned, 2 * NFG)
                        turn(item + 2, 2 * NFG * item + (2 * NFG + 2))
                        between(item)
                        down(item, ITEM)
                    pe.drain().then_inc(s.y_done, 1)

        @block.vector
        def _(dve):
            dve.sem_inc(s.lo1, 2)
            dve.sem_inc(s.lo2, 2)
            dve.sem_inc(s.hid, 2)
            dve.sem_inc(s.hid_lo, 2)
            dve.sem_inc(s.y_in, 1)

            def x_rest(count):
                dve.wait_ge(s.x_hi, count)
                dve.tensor_tensor(flat(xg_lo), m.ps[:, 0:4, :].rearrange("p a n -> p (a n)"), flat(xg_hi).bitcast(F32),
                                  ALU.subtract).then_inc(s.x_lo, 1)

            def gated(item, i, h, width):
                g = 2 * (NFG * item + i) + h
                dve.wait_ge(s.silu, g + 1)
                dve.wait_ge(s.mm_done, UNITS * item + 4 * i + 2 * h + 6)
                dve.tensor_tensor(act_t[h][:, 0:width], act_t[h][:, 0:width], m.ps[:, 2 + h, 0:width], ALU.mult).then_inc(s.hid, 1)

            def split(item, i, h, src, width):
                g = 2 * (NFG * item + i) + h
                src = src.rearrange("p (f n) -> p f n", f=2)
                hi, lo = (t[:, ds(4 * i + 2 * h, 2), 0:width] for t in (hid_hi, hid_lo))
                dve.tensor_scalar(hi, src, 1.0, None, ALU.mult).then_inc(s.hid_hi, 1)
                dve.wait_ge(s.hid_hi, g + 1)
                dve.tensor_tensor(lo, src, hi.bitcast(F32), ALU.subtract).then_inc(s.hid_lo, 1)

            def hidden(item, i, h):
                gated(item, i, h, HALF)
                dve.wait_ge(s.hid, 2 * (NFG * item + i) + h + 3)
                split(item, i, h, act_t[h][:, :], ITEM)

            def turned(item, i, h):
                dve.wait_ge(s.hid_turned, 2 * (NFG * item + i) + h + 1)
                split(item, i, h, m.ps[:, 6 + h, 0:2 * P], P)

            def rest2(item, i, b):
                dve.wait_ge(s.hi_ready, UNITS * item + 4 * NFG + 4 * i + b + 1)
                dve.tensor_tensor(flat(w_lo[b]), flat(raw2[b % 2]), flat(w_hi[b]).bitcast(F32), ALU.subtract).then_inc(s.lo2, 1)

            x_rest(1)
            for h in range(2):
                rest13(dve, 0, 0, 2 * h)
            n_items = field(dve, 0, 3, MAX_ITEMS)
            with dve.Fori(0, MAX_ITEMS) as item:
                with dve.If(item < n_items):
                    left = field(dve, item, 2, S)
                    with dve.If(left < P + 1):
                        gated(item, 0, 0, 2 * P)
                        rest13(dve, item, 1, 0)
                        gated(item, 0, 1, 2 * P)
                        turned(item, 0, 0)
                        rest13(dve, item, 1, 2)
                        with dve.Fori(1, NFG - 1) as i:
                            gated(item, i, 0, 2 * P)
                            turned(item, i - 1, 1)
                            rest13(dve, item, i + 1, 0)
                            gated(item, i, 1, 2 * P)
                            turned(item, i, 0)
                            rest13(dve, item, i + 1, 2)
                        gated(item, NFG - 1, 0, 2 * P)
                        turned(item, NFG - 2, 1)
                        rest2(item, 0, 0)
                        rest2(item, 0, 1)
                        gated(item, NFG - 1, 1, 2 * P)
                        turned(item, NFG - 1, 0)
                        turned(item, NFG - 1, 1)
                        rest2(item, 0, 2)
                        rest2(item, 0, 3)
                    with dve.Else():
                        with dve.Fori(0, NFG - 1) as i:
                            for h in range(2):
                                hidden(item, i, h)
                                rest13(dve, item, i + 1, 2 * h)
                        for h in range(2):
                            hidden(item, NFG - 1, h)
                            rest2(item, 0, 2 * h)
                            rest2(item, 0, 2 * h + 1)
                    x_rest(item + 2)
                    with dve.Fori(1, NF2 // 4) as i:
                        for b in range(4):
                            rest2(item, i, b)
                    for b in range(NF2 % 4):
                        rest2(item, NF2 // 4, b)
                    for h in range(2):
                        rest13(dve, item + 1, 0, 2 * h)


def combine_phase(nc, m, a, l):
    KB = 1024
    cst = m.const
    R = m.R
    xt = m.place("c_xt", [P, KT, S], F32, R)
    g_row = m.place("c_g_row", [P, D], F32, R + 32 * KB)
    dg = m.place("c_diag", [P, KT, P], F32, R + 36 * KB)
    ya = [m.place(f"c_ya{b}", [P, D], F32, R + (40 + 4 * b) * KB) for b in range(2)]
    yb = [m.place(f"c_yb{b}", [P, D], F32, R + (48 + 4 * b) * KB) for b in range(2)]
    row = [m.place(f"c_row{b}", [P, D], F32, R + (56 + 4 * b) * KB) for b in range(2)]
    G2 = S_ADA + 48 * l + 40
    with phase(nc, "x_in", "diag", "spread", "g_in", "ga0", "ga1", "gb0", "gb1", "scaled", "mixed", "gated", "turned", "summed",
               "st0", "st1") as (block, s):
        @block.sync
        def _(sp):
            sp.dma_start(xt[:, :, :], a.xs.rearrange("(k p) n -> p k n", p=P)).then_inc(s.x_in, 16)
            for t in range(ST):
                sp.wait_ge(s.summed, t + 1)
                sp.dma_start(a.out[0, P * t:P * (t + 1), :], row[t % 2][:, :]).then_inc((s.st0, s.st1)[t % 2], 16)
            sp.wait_ge(s.st0, 16 * ST // 2)
            sp.wait_ge(s.st1, 16 * ST // 2)

        @block.gpsimd
        def _(pool):
            for t in range(ST):
                b = t % 2
                if t >= 2:
                    pool.wait_ge(s.mixed, t - 1)
                for q, (dst, sem) in enumerate(((ya[b], (s.ga0, s.ga1)[b]), (yb[b], (s.gb0, s.gb1)[b]))):
                    pool.indirect_dma_start(dst[:, :], None, a.y_rows[0:SLOTS, :],
                                            bass.IndirectOffsetOnAxis(ap=m.slot[:, t, q:q + 1].bitcast(U32), axis=0)).then_inc(sem, 16)

        @block.scalar
        def _(act):
            for t in range(ST):
                b = t % 2
                act.wait_ge((s.ga0, s.ga1)[b], 16 * (t // 2) + 16)
                act.activation(ya[b][:, :], ya[b][:, :], ACT.Copy, scale=m.top_w[:, t, 0:1]).then_inc(s.scaled, 1)

        @block.tensor
        def _(pe):
            pe.wait_ge(s.diag, KT)
            for k in range(KT):
                last = pe.matmul(m.ps[:, k // 4, P * (k % 4):P * (k % 4 + 1)], cst[:, K_ONE:K_ONE + P], dg[:, k, :], start=True, stop=True)
            last.then_inc(s.spread, 1)
            pe.wait_ge(s.g_in, 1)
            pe.wait_ge(s.x_in, 16)
            for t in range(ST):
                if t >= 2:
                    pe.wait_ge(s.summed, t - 1)
                for k in range(KT):
                    last = pe.transpose(m.ps[:, 2 * (t % 2) + k // 4, P * (k % 4):P * (k % 4 + 1)],
                                        xt[:, k, P * t:P * (t + 1)], cst[:, K_ID:K_ID + P])
                last.then_inc(s.turned, 1)

        @block.vector
        def _(dve):
            for k in range(KT):
                dve.tensor_scalar(dg[:, k, :], cst[:, K_ID:K_ID + P], m.small[:, G2 + k:G2 + k + 1], None, ALU.mult).then_inc(s.diag, 1)
            dve.wait_ge(s.spread, 1)
            dve.tensor_copy(g_row[:, :], m.ps[:, 0:2, :].rearrange("p a n -> p (a n)")).then_inc(s.g_in, 1)
            dve.wait_ge(s.g_in, 1)
            for t in range(ST):
                b = t % 2
                dve.wait_ge(s.scaled, t + 1)
                dve.wait_ge((s.gb0, s.gb1)[b], 16 * (t // 2) + 16)
                if t >= 2:
                    dve.wait_ge((s.st0, s.st1)[b], 16 * (t // 2))
                dve.scalar_tensor_tensor(out=row[b][:, :], in0=yb[b][:, :], scalar=m.top_w[:, t, 1:2], in1=ya[b][:, :],
                                         op0=ALU.mult, op1=ALU.add).then_inc(s.mixed, 1)
                dve.wait_ge(s.mixed, t + 1)
                dve.tensor_tensor(row[b][:, :], row[b][:, :], g_row[:, :], ALU.mult).then_inc(s.gated, 1)
                dve.wait_ge(s.gated, t + 1)
                dve.wait_ge(s.turned, t + 1)
                dve.tensor_tensor(row[b][:, :], row[b][:, :], m.ps[:, 2 * b:2 * b + 2, :].rearrange("p a n -> p (a n)"),
                                  ALU.add).then_inc(s.summed, 1)


def build(nc, a):
    with ExitStack() as stack:
        m = Memory(nc, stack)
        opening_phase(nc, m, a)
        for l in range(DEPTH):
            param_phase(nc, m, a, l)
            norm_project_phase(nc, m, a, l, C_B, 10, C_KR + QKR - P)
            conv_lora_phase(nc, m, l)
            qk = qk_phase(nc, m, l)
            attention_phase(nc, m, l, qk)
            project_phase(nc, m, a, l, C_SU, 12)
            sgu_phase(nc, m, l)
            retention_phases(nc, m, l)
            merged = gate_phase(nc, m, a, l)
            out_proj_phase(nc, m, a, l, merged)
            if l % 2 == 0:
                norm_phase(nc, m, l, split=True)
                ffn_phases(nc, m, a, l)
            else:
                moe_memory(m)
                norm_phase(nc, m, l, split=False)
                route_phase(nc, m, a, l)
                scatter_phase(nc, m, a)
                expert_phase(nc, m, a, l)
                combine_phase(nc, m, a, l)


_INS = ["x", "positions", "ada_w", "w_in", "w_uq", "w_ukv", "w_s", "b_s", "w_branch", "w_o", "ffn_w1", "ffn_w3", "ffn_w2", "router_w",
        "router_b", "moe_w1", "moe_w3", "moe_w2"]


def kernel(**inputs):
    import concourse.bacc as _bacc
    from concourse.bass_utils import run_bass_kernel_spmd as _run

    nc = _bacc.Bacc("TRN2", target_bir_lowering=False, num_devices=1)
    arrays, args = {}, {}
    for name in _INS:
        v = np.ascontiguousarray(inputs[name])
        arrays[f"in_{name}_dram"] = v
        args[name] = nc.dram_tensor(f"in_{name}_dram", v.shape, mybir.dt.from_np(v.dtype), kind="ExternalInput").ap()
    arrays["in_vectors_dram"] = pack_vectors({k: np.asarray(v) for k, v in inputs.items()})
    args["vectors"] = nc.dram_tensor("in_vectors_dram", (P, KT + DEPTH * V_N), F32, kind="ExternalInput").ap()
    arrays["in_const_dram"] = constants()
    args["const"] = nc.dram_tensor("in_const_dram", (P, K_N), F32, kind="ExternalInput").ap()
    args["out"] = nc.dram_tensor("out_0_dram", (1, S, D), F32, kind="ExternalOutput").ap()
    args["xs"] = nc.dram_tensor("x_scratch", (D, S), F32, kind="Internal").ap()
    args["rows"] = nc.dram_tensor("row_scratch", (SLOTS + ITEM, D), F32, kind="Internal").ap()
    args["y_rows"] = nc.dram_tensor("y_scratch", (SLOTS + ITEM, D), F32, kind="Internal").ap()
    args["items"] = nc.dram_tensor("item_scratch", (MAX_ITEMS + 1, 4), I32, kind="Internal").ap()
    args["tables"] = nc.dram_tensor("table_scratch", (P, 4, S), F32, kind="Internal").ap()
    build(nc, namedtuple("Arrays", list(args))(**args))
    r = _run(nc, [arrays], core_ids=[0])
    return r.results[0]["out_0_dram"]
```
